# Optimizing a Trainium2 kernel written in Bass

```python
import math
import jax, jax.numpy as jnp
from jax import lax
import numpy as np

D_MODEL = 1024
BATCH = 1
SEQ = 512
DEPTH = 2

M_HEADS = 4
M_HEAD_DIM = D_MODEL // 8
M_WIDTH = M_HEADS * M_HEAD_DIM
M_CHUNK = 64
DA_HEADS = 4
DA_HEAD_DIM = D_MODEL // 16
DA_V_DIM = 2 * DA_HEAD_DIM
DA_QK_WIDTH = DA_HEADS * 2 * DA_HEAD_DIM
DA_WIDTH = DA_HEADS * DA_V_DIM
Q_BLOCK = 128
REL_BUCKETS = 32
REL_MAX_DIST = 128
CONV_WIDTH = 3
CONV_DIM = D_MODEL
MOE_GROUPS = 4
EXPERTS_PER_GROUP = 4
N_EXPERTS = MOE_GROUPS * EXPERTS_PER_GROUP
EXPERT_TOP_K = 2
EXPERT_FF = D_MODEL // 2

NORM_EPS = 1e-6
N_EVEN_LAYERS = (DEPTH + 1) // 2
N_ODD_LAYERS = DEPTH // 2
EVEN_SPLITS = [M_WIDTH, M_WIDTH, M_WIDTH, M_WIDTH, M_HEADS, M_HEADS, DA_QK_WIDTH, DA_QK_WIDTH, DA_WIDTH]
EVEN_IN = sum(EVEN_SPLITS)

kernel_name = "hybrid_mlstm_diffattn_shortconv_hmoe"

def rmsnorm(x, g):
    xf = x.astype(jnp.float32)
    y = xf * lax.rsqrt(jnp.mean(xf * xf, axis=-1, keepdims=True) + NORM_EPS)
    return (y * g.astype(jnp.float32)).astype(x.dtype)

def rel_bucket(rel):
    n = jnp.maximum(-rel, 0)
    max_exact = REL_BUCKETS // 2
    nf = jnp.maximum(n, 1).astype(jnp.float32)
    large = max_exact + (jnp.log(nf / max_exact) / math.log(REL_MAX_DIST / max_exact)
                         * (REL_BUCKETS - max_exact)).astype(jnp.int32)
    large = jnp.minimum(large, REL_BUCKETS - 1)
    return jnp.where(n < max_exact, n, large)

def mlstm(q, k, v, ig, fg):
    Bn, S, H, dh = q.shape
    L = M_CHUNK
    nc = S // L
    to_chunks = lambda a: a.reshape(Bn, nc, L, H, dh).transpose(1, 0, 3, 2, 4)
    g_chunks = lambda a: a.reshape(Bn, nc, L, H).transpose(1, 0, 3, 2)
    qc, kc, vc = to_chunks(q), to_chunks(k * (dh ** -0.5)), to_chunks(v)
    ic, lf = g_chunks(ig), g_chunks(jax.nn.log_sigmoid(fg))
    causal = jnp.tril(jnp.ones((L, L), dtype=bool))

    def step(carry, xs):
        C, n, m = carry
        qt, kt, vt, it, lft = xs
        b = jnp.cumsum(lft, axis=-1)
        g = b[..., -1]
        dmat = jnp.where(causal, b[..., :, None] - b[..., None, :] + it[..., None, :], -jnp.inf)
        inter = b + m[..., None]
        mt = jnp.maximum(inter, jnp.max(dmat, axis=-1))
        w = jnp.exp(dmat - mt[..., None])
        sc = jnp.exp(inter - mt)
        qk = jnp.einsum('bhtd,bhsd->bhts', qt, kt) * w
        num = sc[..., None] * jnp.einsum('bhtd,bhde->bhte', qt, C) + jnp.einsum('bhts,bhse->bhte', qk, vt)
        den = sc * jnp.einsum('bhtd,bhd->bht', qt, n) + jnp.sum(qk, axis=-1)
        h = num / jnp.maximum(jnp.abs(den), jnp.exp(-mt))[..., None]
        ws = g[..., None] - b + it
        m_new = jnp.maximum(g + m, jnp.max(ws, axis=-1))
        a = jnp.exp(g + m - m_new)
        wk = jnp.exp(ws - m_new[..., None])[..., None] * kt
        C_new = a[..., None, None] * C + jnp.einsum('bhsd,bhse->bhde', wk, vt)
        n_new = a[..., None] * n + jnp.sum(wk, axis=-2)
        return (C_new, n_new, m_new), h

    init = (jnp.zeros((Bn, H, dh, dh), jnp.float32), jnp.zeros((Bn, H, dh), jnp.float32),
            jnp.zeros((Bn, H), jnp.float32))
    _, hs = lax.scan(step, init, (qc, kc, vc, ic, lf))
    return hs.transpose(1, 0, 3, 2, 4).reshape(Bn, S, H, dh)

def diff_attention(dq, dk, dv, rel_bias, lq1, lk1, lq2, lk2, subln, layer):
    Bn, S, _ = dq.shape
    H, d = DA_HEADS, DA_HEAD_DIM
    nb = S // Q_BLOCK
    q = dq.reshape(Bn, S, H, 2, d)
    k = dk.reshape(Bn, S, H, 2, d)
    q1, q2 = q[..., 0, :].transpose(0, 2, 1, 3), q[..., 1, :].transpose(0, 2, 1, 3)
    k1, k2 = k[..., 0, :].transpose(0, 2, 1, 3), k[..., 1, :].transpose(0, 2, 1, 3)
    v = dv.reshape(Bn, S, H, DA_V_DIM).transpose(0, 2, 1, 3)
    lam_init = 0.8 - 0.6 * math.exp(-0.3 * layer)
    lam = (jnp.exp(jnp.sum(lq1.astype(jnp.float32) * lk1.astype(jnp.float32)))
           - jnp.exp(jnp.sum(lq2.astype(jnp.float32) * lk2.astype(jnp.float32))) + lam_init)
    scale = d ** -0.5
    kpos = jnp.arange(S)
    to_blocks = lambda a: a.reshape(Bn, H, nb, Q_BLOCK, d).transpose(2, 0, 1, 3, 4)

    def block(args):
        q1b, q2b, bi = args
        qpos = bi * Q_BLOCK + jnp.arange(Q_BLOCK)
        rel = kpos[None, :] - qpos[:, None]
        bias = rel_bias[rel_bucket(rel)].astype(jnp.float32).transpose(2, 0, 1)
        mask = rel <= 0
        s1 = jnp.einsum('bhqd,bhkd->bhqk', q1b, k1).astype(jnp.float32) * scale + bias
        s2 = jnp.einsum('bhqd,bhkd->bhqk', q2b, k2).astype(jnp.float32) * scale + bias
        p1 = jax.nn.softmax(jnp.where(mask, s1, -jnp.inf), axis=-1)
        p2 = jax.nn.softmax(jnp.where(mask, s2, -jnp.inf), axis=-1)
        a = p1 - lam * p2
        return jnp.einsum('bhqk,bhke->bhqe', a.astype(v.dtype), v)

    out = lax.map(block, (to_blocks(q1), to_blocks(q2), jnp.arange(nb)))
    out = out.transpose(1, 2, 0, 3, 4).reshape(Bn, H, S, DA_V_DIM)
    out = rmsnorm(out, subln) * (1.0 - lam_init)
    return out.transpose(0, 2, 1, 3).reshape(Bn, S, DA_WIDTH)

def even_mixer(h, w_in, w_out, ig_b, fg_b, head_norm, rel_bias, lq1, lk1, lq2, lk2, subln, layer):
    Bn, S, _ = h.shape
    p = h @ w_in
    idx = [int(c) for c in np.cumsum(EVEN_SPLITS)[:-1]]
    mq, mk, mv, mo, mi, mf, dq, dk, dv = jnp.split(p, idx, axis=-1)
    f32 = jnp.float32
    shp = (Bn, S, M_HEADS, M_HEAD_DIM)
    hm = mlstm(mq.reshape(shp).astype(f32), mk.reshape(shp).astype(f32), mv.reshape(shp).astype(f32),
               mi.astype(f32) + ig_b.astype(f32), mf.astype(f32) + fg_b.astype(f32))
    mu = jnp.mean(hm, axis=-1, keepdims=True)
    var = jnp.mean(jnp.square(hm - mu), axis=-1, keepdims=True)
    hm = (hm - mu) * lax.rsqrt(var + NORM_EPS) * head_norm.astype(f32).reshape(M_HEADS, M_HEAD_DIM)
    hm = hm.reshape(Bn, S, M_WIDTH) * jax.nn.sigmoid(mo.astype(f32))
    ha = diff_attention(dq, dk, dv, rel_bias, lq1, lk1, lq2, lk2, subln, layer)
    return jnp.concatenate([hm.astype(h.dtype), ha.astype(h.dtype)], axis=-1) @ w_out

def conv_mixer(h, w_in, conv_w, w_out):
    bg, cg, u = jnp.split(h @ w_in, 3, axis=-1)
    z = cg * u
    zc = lax.conv_general_dilated(z, conv_w[:, None, :].astype(z.dtype), window_strides=(1,),
                                  padding=[(CONV_WIDTH - 1, 0)],
                                  dimension_numbers=('NWC', 'WIO', 'NWC'),
                                  feature_group_count=CONV_DIM)
    return (bg * zc) @ w_out

def hier_moe(h, wg, bg, we, be, w_gate, w_up, w_down):
    Bn, S, D = h.shape
    t = h.reshape(-1, D)
    T = t.shape[0]
    glog = (t @ wg).astype(jnp.float32) + bg.astype(jnp.float32)
    gprob = jax.nn.softmax(glog, axis=-1)
    _, gsel = lax.top_k(glog, 1)
    pg = jnp.take_along_axis(gprob, gsel, axis=1)[:, 0]
    elog = ((t @ we).astype(jnp.float32) + be.astype(jnp.float32)).reshape(T, MOE_GROUPS, EXPERTS_PER_GROUP)
    elog_g = jnp.take_along_axis(elog, gsel[:, :, None], axis=1)[:, 0]
    top_v, top_i = lax.top_k(elog_g, EXPERT_TOP_K)
    top_w = jax.nn.softmax(top_v, axis=-1)
    eid = gsel * EXPERTS_PER_GROUP + top_i
    combine = jnp.einsum('tk,tke->te', top_w, jax.nn.one_hot(eid, N_EXPERTS, dtype=jnp.float32)) * pg[:, None]
    combine = combine.astype(t.dtype)
    out = jnp.zeros_like(t)
    for e in range(N_EXPERTS):
        y = (jax.nn.silu(t @ w_gate[e]) * (t @ w_up[e])) @ w_down[e]
        out = out + combine[:, e:e + 1] * y
    return out.reshape(Bn, S, D)

def setup_inputs(seed: int = 0) -> dict:
    key = jax.random.key(seed)
    ks = iter(jax.random.split(key, 32))
    nrm = lambda shape, s: jax.random.normal(next(ks), shape, jnp.float32) * s
    D = D_MODEL
    fg_base = jnp.linspace(3.0, 6.0, M_HEADS, dtype=jnp.float32)
    return {
        "x": nrm((BATCH, SEQ, D), 1.0),
        "rel_bias": nrm((REL_BUCKETS, DA_HEADS), 0.5),
        "norm_mix": 1.0 + nrm((DEPTH, D), 0.02),
        "norm_ffn": 1.0 + nrm((DEPTH, D), 0.02),
        "norm_final": 1.0 + nrm((D,), 0.02),
        "w_in_even": nrm((N_EVEN_LAYERS, D, EVEN_IN), D ** -0.5),
        "w_out_even": nrm((N_EVEN_LAYERS, M_WIDTH + DA_WIDTH, D), (M_WIDTH + DA_WIDTH) ** -0.5),
        "m_igate_b": nrm((N_EVEN_LAYERS, M_HEADS), 0.1),
        "m_fgate_b": fg_base[None, :] + nrm((N_EVEN_LAYERS, M_HEADS), 0.1),
        "m_head_norm": 1.0 + nrm((N_EVEN_LAYERS, M_WIDTH), 0.02),
        "lam_q1": nrm((N_EVEN_LAYERS, DA_HEAD_DIM), 0.1),
        "lam_k1": nrm((N_EVEN_LAYERS, DA_HEAD_DIM), 0.1),
        "lam_q2": nrm((N_EVEN_LAYERS, DA_HEAD_DIM), 0.1),
        "lam_k2": nrm((N_EVEN_LAYERS, DA_HEAD_DIM), 0.1),
        "da_subln": 1.0 + nrm((N_EVEN_LAYERS, DA_V_DIM), 0.02),
        "w_in_odd": nrm((N_ODD_LAYERS, D, 3 * CONV_DIM), D ** -0.5),
        "conv_w": nrm((N_ODD_LAYERS, CONV_WIDTH, CONV_DIM), CONV_WIDTH ** -0.5),
        "w_out_odd": nrm((N_ODD_LAYERS, CONV_DIM, D), CONV_DIM ** -0.5),
        "router_group_w": nrm((DEPTH, D, MOE_GROUPS), D ** -0.5),
        "router_group_b": nrm((DEPTH, MOE_GROUPS), 0.01),
        "router_expert_w": nrm((DEPTH, D, N_EXPERTS), D ** -0.5),
        "router_expert_b": nrm((DEPTH, N_EXPERTS), 0.01),
        "exp_w_gate": nrm((DEPTH, N_EXPERTS, D, EXPERT_FF), D ** -0.5),
        "exp_w_up": nrm((DEPTH, N_EXPERTS, D, EXPERT_FF), D ** -0.5),
        "exp_w_down": nrm((DEPTH, N_EXPERTS, EXPERT_FF, D), EXPERT_FF ** -0.5),
    }

def reference(x, rel_bias, norm_mix, norm_ffn, norm_final, w_in_even, w_out_even, m_igate_b, m_fgate_b,
              m_head_norm, lam_q1, lam_k1, lam_q2, lam_k2, da_subln, w_in_odd, conv_w, w_out_odd,
              router_group_w, router_group_b, router_expert_w, router_expert_b,
              exp_w_gate, exp_w_up, exp_w_down):
    for layer in range(DEPTH):
        h = rmsnorm(x, norm_mix[layer])
        if layer % 2 == 0:
            e = layer // 2
            y = even_mixer(h, w_in_even[e], w_out_even[e], m_igate_b[e], m_fgate_b[e], m_head_norm[e],
                           rel_bias, lam_q1[e], lam_k1[e], lam_q2[e], lam_k2[e], da_subln[e], layer)
        else:
            o = layer // 2
            y = conv_mixer(h, w_in_odd[o], conv_w[o], w_out_odd[o])
        x = x + y.astype(x.dtype)
        h = rmsnorm(x, norm_ffn[layer])
        x = x + hier_moe(h, router_group_w[layer], router_group_b[layer], router_expert_w[layer],
                         router_expert_b[layer], exp_w_gate[layer], exp_w_up[layer],
                         exp_w_down[layer]).astype(x.dtype)
    return rmsnorm(x, norm_final)


_drawn_inputs = setup_inputs


def setup_inputs(seed=0):
    import zlib

    import numpy as np

    out = dict(_drawn_inputs(seed))
    spreads = {}
    factors = {'norm_final': 23.765,
     'm_igate_b': 64.0,
     'm_head_norm': 15.016,
     'lam_q1': 6.454,
     'router_group_b': 14.236,
     'router_expert_b': 42.384,
     'lam_q2': 2.754,
     'da_subln': 4.356,
     'norm_ffn': 4.067}
    for name, (base, spread) in spreads.items():
        noise = np.random.default_rng([zlib.crc32(name.encode()), seed]).standard_normal(out[name].shape)
        drawn = base * np.exp(spread * noise) if base else spread * noise
        out[name] = __import__('jax').numpy.asarray(drawn.astype(out[name].dtype))
    for name, factor in factors.items():
        out[name] = (out[name] * factor).astype(out[name].dtype)
    return out
```

```python
from contextlib import ExitStack

import numpy as np

import concourse.bass as bass
from concourse import mybir

ALU = mybir.AluOpType
ACT = mybir.ActivationFunctionType
AX = mybir.AxisListType.X
F32 = mybir.dt.float32
F16 = mybir.dt.float16
BF16 = mybir.dt.bfloat16
I32 = mybir.dt.int32

P = 128
D = 1024
T = 512
TT = T // P
KD = D // P
HEADS = 4
EPS = 1e-6
BIG = 1e30
FF = 512
KF = FF // P
GROUPS, PER_GROUP = 4, 4
E = GROUPS * PER_GROUP
NR = GROUPS + E
CAP = 128
SMALL = 13 + 8 + 2
OVER = T // CAP - 1
LAM_INIT = 0.8 - 0.6
BUCKETS, MAX_DIST = 32, 128
VROW = 640

RING = 6
EVEN_PIECES, ODD_PIECES, EXPERT_PIECES = 9, 8, 3
MOE_BASE = [EVEN_PIECES, EVEN_PIECES + EXPERT_PIECES * E + ODD_PIECES]
ODD_BASE = EVEN_PIECES + EXPERT_PIECES * E


def bucket_table():
    n = 511 - np.arange(VROW)
    exact = BUCKETS // 2
    far = exact + (np.log(np.maximum(n, 1).astype(np.float32) / np.float32(exact)) / np.float32(np.log(MAX_DIST / exact))
                   * (BUCKETS - exact)).astype(np.int32)
    b = np.where(n < exact, n, np.minimum(far, BUCKETS - 1))
    b = np.where(n < 0, BUCKETS, b)
    return (np.arange(BUCKETS + 1)[:, None] == b[None, :]).astype(np.float32)


def hybrid_trunk(nc, A, out):
    ctx = ExitStack()
    with ctx:
        def sb(name, shape, dt=F32):
            return ctx.enter_context(nc.sbuf_tensor(name, shape, dt))

        def sem(name):
            return ctx.enter_context(nc.semaphore(name))

        x_sb = sb("x_sb", [P, TT, D])
        hT = sb("hT", [P, KD, T])
        ring = sb("ring", [P, RING, 4096])
        arena = sb("arena", [P, 17424])
        ident = sb("ident", [P, P])
        later = sb("later", [P, P], F16)
        ones16 = sb("ones16", [P, P], F16)
        slot_iota = sb("slot_iota", [P, P])
        tok_id = sb("tok_id", [P, TT], F16)
        iota16 = sb("iota16", [P, E])
        iota_slot0 = sb("iota_slot0", [P, E])
        gain = sb("gain", [P, D])
        w_route = sb("w_route", [P, 2, KD, NR])
        b_route = sb("b_route", [P, 2, NR])
        w_gates = sb("w_gates", [P, KD, 36])
        gate_b = sb("gate_b", [P, 1])
        conv_sb = sb("conv_sb", [P, KD, 3])
        head_norm = sb("head_norm", [P, HEADS])
        subln = sb("subln", [P, 1])
        lams = sb("lams", [P, 4, 64])
        minus_half = sb("minus_half", [P, TT])
        st = sb("st", [P, 88])
        overflow_flag = sb("overflow_flag", [P, 2], I32)

        def part(lo, *shape):
            n = int(np.prod(shape))
            v = arena[:, lo:lo + n]
            if len(shape) == 1:
                return v
            names = "abcd"[:len(shape)]
            return v.rearrange(f"p ({' '.join(names)}) -> p {' '.join(names)}", **dict(zip(names, shape)))

        q_cat = part(0, KD, T)
        dkT = part(4096, HEADS, T)
        bias_sb = part(6144, 2, T)
        dv = part(7168, TT, T)
        mkT = part(9216, HEADS, T)
        mv = part(11264, TT, HEADS, P + 1)
        mo = part(13328, TT, T)
        post = part(15376, 2, T)
        neg_m_row = part(16400, T)[0:HEADS, :]
        head_row = part(16912, HEADS, P)[0:HEADS]
        rel_w = part(4096, HEADS)
        table = part(4160, VROW)
        v_row = part(4864, VROW)
        gate_rows = part(11264, 8, T)
        xs = x_sb[:, :, :].rearrange("p t d -> p (t d)")
        e_maps = xs[:, 0:2048].rearrange("p (b m k) -> p b m k", b=2, m=2)
        a_map = xs[:, 2048:3072].rearrange("p (b k) -> p b k", b=2)
        aT = xs[:, 3072:4096].rearrange("p (b k) -> p b k", b=2)
        decay = xs[:, 0:4096].rearrange("p (b k) -> p b k", b=2)
        h_rows = part(11264, TT, D)
        junk = part(15360, D)
        cg_sb = part(0, KF, T)
        z_sb = part(2048, KF, T + 2)
        zc = part(4112, KF, T)
        yT = part(6160, KD, T)
        y_back = part(0, TT, 2, D)
        sel = arena[:, 0:4096].bitcast(F16).rearrange("p (t e c) -> p t e c", t=TT, e=E)
        w_over = part(0, 4096)
        xg = part(8192, 2, D)
        xgT = part(10240, 2, KD, P)
        sg = part(12288, FF)
        act_h = part(12800, FF)
        actT = part(13312, 2, KF, P)
        y_sb = part(14336, 2, D)
        rt = arena[:, 16384:17424]

        ps = ctx.enter_context(nc.psum_tensor("ps", [P, 8, 512], F32))

        h_dram = nc.dram_tensor("h_rows_dram", (T, D), F32, kind="Internal").ap()
        y_dram = nc.dram_tensor("y_rows_dram", (E * T, D), F32, kind="Internal").ap()
        v_dram = nc.dram_tensor("bias_rows_dram", (HEADS, P, VROW), F32, kind="Internal").ap()

        x_loaded, x_reloaded = sem("x_loaded"), sem("x_reloaded")
        x_ready = sem("x_ready")
        sumsq_ready, h_ready = sem("sumsq_ready"), sem("h_ready")
        tr_full = sem("tr_full")
        tr_act, tr_dve = sem("tr_act"), sem("tr_dve")
        h_stored = sem("h_stored")
        gain_loaded = sem("gain_loaded")
        small_loaded = sem("small_loaded")
        consts_ready, zeros_ready = sem("consts_ready"), sem("zeros_ready")
        slot_landed = [sem(f"slot_landed{i}") for i in range(RING)]
        piece_done = sem("piece_done")
        vbias_full, v_row_ready, v_stored = sem("vbias_full"), sem("v_row_ready"), sem("v_stored")
        bias_loaded = [sem("bias_loaded0"), sem("bias_loaded1")]
        bias_used = sem("bias_used")
        gates_full, gate_cols_full = sem("gates_full"), sem("gate_cols_full")
        gate_act, gate_rows_ready, gate_cols_ready = sem("gate_act"), sem("gate_rows_ready"), sem("gate_cols_ready")
        route_read = sem("route_read")
        job_full, job_act, job_dve, mo_exp = sem("job_full"), sem("job_act"), sem("job_dve"), sem("mo_exp")
        lam_sum, lam_exp, subln_ready = sem("lam_sum"), sem("lam_exp"), sem("subln_ready")
        o_unit = sem("o_unit")
        s_full, s_biased, s_max = sem("s_full"), sem("s_biased"), sem("s_max")
        e_ready, a_ready, a_turned, aT_ready = sem("e_ready"), sem("a_ready"), sem("a_turned"), sem("aT_ready")
        o_full, o_square, o_normed = sem("o_full"), sem("o_square"), sem("o_normed")
        on_turned, cat_ready = sem("on_turned"), sem("cat_ready")
        m_full, m_arg, m_exp, m_masked = sem("m_full"), sem("m_arg"), sem("m_exp"), sem("m_masked")
        m_weighted, mo_full, m_centred, m_square = sem("m_weighted"), sem("mo_full"), sem("m_centred"), sem("m_square")
        norm_rstd, o_sums, o_rstd = sem("norm_rstd"), sem("o_sums"), sem("o_rstd")
        m_sums, m_rstd = sem("m_sums"), sem("m_rstd")
        m_normed, m_turned, m_cat = sem("m_normed"), sem("m_turned"), sem("m_cat")
        out_full, out_added = sem("out_full"), sem("out_added")
        odd_full, odd_cg, odd_z, odd_y = sem("odd_full"), sem("odd_cg"), sem("odd_z"), sem("odd_y")
        logits_full, route_arg, route_exp = sem("logits_full"), sem("route_arg"), sem("route_exp")
        picks_ready, rank_full, sel_ready, idx_full, idx_ready = (
            sem("picks_ready"), sem("rank_full"), sem("sel_ready"), sem("idx_full"), sem("idx_ready"))
        xg_landed = [sem("xg_landed0"), sem("xg_landed1")]
        xg_turned, xgT_act, xgT_dve = sem("xg_turned"), sem("xgT_act"), sem("xgT_dve")
        silu_ready, act_ready = sem("silu_ready"), sem("act_ready")
        act_turned, actT_ready, down_full = sem("act_turned"), sem("actT_ready"), sem("down_full")
        y_act, y_dve, y_stored = sem("y_act"), sem("y_dve"), [sem("y_stored0"), sem("y_stored1")]
        y_back_loaded = sem("y_back_loaded")
        flag_ready = sem("flag_ready")
        out_stored = sem("out_stored")
        dve_step, act_step, pool_step = sem("dve_step"), sem("act_step"), sem("pool_step")
        over = [{n: sem(f"over_{n}{l}") for n in ("place", "sel", "idx_full", "idx", "xg", "turned", "xgT", "w",
                                                  "done", "silu", "act", "act_turned", "actT", "y", "stored", "gathers")} for l in range(2)]

        block = ctx.enter_context(nc.Block())

        w_even, w_odd = A["w_in_even"][0], A["w_in_odd"][0]
        dq0 = 4 * 512 + 2 * HEADS
        even_cols = [dq0, dq0 + 512, dq0 + 1024, 0, 512, 1024, 1536]
        odd_cols = [D, 2 * D, 0, D + 512, 2 * D + 512, 512]

        def cols(w, c, n=512):
            return w[:, c:c + n].rearrange("(k p) n -> p k n", p=P)

        def slot(piece):
            return ring[:, piece % RING, :].rearrange("p (k n) -> p k n", k=KD)

        def slot_down(piece):
            return ring[:, piece % RING, :].rearrange("p (k n) -> p k n", k=KF)

        def landed(eng, piece):
            eng.wait_ge(slot_landed[piece % RING], 16 * (piece // RING + 1))

        def expert_weights(l, e):
            e = min(e, E - 1) if isinstance(e, int) else e
            return [A[name][l, bass.ds(e, 1)].rearrange("a (k p) n -> p (a k) n", p=P)
                    for name in ("exp_w_gate", "exp_w_up", "exp_w_down")]

        @block.sync
        def _(sp):
            def load(piece, src):
                if piece >= RING:
                    sp.wait_ge(piece_done, piece - RING + 1)
                dst = slot(piece) if src.shape[1] == KD else slot_down(piece)
                sp.dma_start(dst, src).then_inc(slot_landed[piece % RING], 16)

            def load_step(l, e, first, gate_up=True, down=True):
                e_up = expert_weights(l, e)[:2] if gate_up else ()
                e_down = expert_weights(l, e - 1)[2:] if down else ()
                for k, src in enumerate((*e_up, *e_down)):
                    piece = first[0] + k
                    sp.wait_ge(piece_done, first[1] + (piece - RING + 1))
                    sp.dma_start(slot(piece) if src.shape[1] == KD else slot_down(piece),
                                 src).then_inc(slot_landed[piece % RING], 16)

            def load_experts(l):
                base = MOE_BASE[l]
                load_step(l, 0, (base, 0), down=False)
                with sp.Fori(0, E // 2 - 1) as i:
                    for u in range(2):
                        load_step(l, i * 2 + (1 + u), (base + 2 + 3 * u, i * 6))
                load_step(l, E - 1, (base + 3 * E - 4, 0))
                load_step(l, E, (base + 3 * E - 1, 0), gate_up=False)

            def overflow(l):
                o = over[l]
                sp.wait_ge(flag_ready, l + 1)
                with sp.If(sp.value_load(overflow_flag[0:1, l:l + 1], min_val=0, max_val=1) > 0):
                    with sp.Fori(0, E) as e:
                        with sp.Fori(0, OVER) as j:
                            it = e * OVER + j
                            for k, src in enumerate(expert_weights(l, e)):
                                if k:
                                    sp.wait_ge(o["done"], it * 3 + k)
                                sp.dma_start(w_over.rearrange("p (k n) -> p k n", k=KD if k < 2 else KF),
                                             src).then_inc(o["w"], 16)
                            row = sp.snap(e * CAP + (j + 1) * (E * CAP))
                            sp.wait_ge(o["y"], it + 1)
                            sp.dma_start(y_dram[bass.ds(row, CAP), :],
                                         y_sb[0:CAP, 0, :]).then_inc(o["stored"], 16)
                    sp.wait_ge(o["stored"], 16 * E * OVER)

            sp.dma_start(x_sb[:, :, :], A["x"][0].rearrange("(t p) d -> p t d", p=P)).then_inc(x_loaded, 16)
            for k, c in enumerate(even_cols):
                load(k, cols(w_even, c))
            for half in range(2):
                load(7 + half, cols(A["w_out_even"][0], half * 512))
            load_experts(0)
            overflow(0)
            for k, c in enumerate(odd_cols):
                load(ODD_BASE + k, cols(w_odd, c))
            for half in range(2):
                load(ODD_BASE + 6 + half, cols(A["w_out_odd"][0], half * 512))
            load_experts(1)
            overflow(1)
            for t in range(TT):
                sp.wait_ge(h_ready, 4 * TT + t + 1)
                sp.dma_start(out[0, t * P:(t + 1) * P, :], h_rows[:, t, :]).then_inc(out_stored, 16)
            sp.wait_ge(out_stored, 16 * TT)

        rt = arena[:, 16384:17424]
        lg = rt[:, 0:80].rearrange("p (t n) -> p t n", t=TT)
        top_v = rt[:, 80:88].rearrange("p (k t) -> p k t", k=2)
        low = rt[:, 88:92]
        prob = rt[:, 92:104].rearrange("p (a t) -> p a t", a=3)
        g_cand, g_pick, g_exp, g_pen = (rt[:, 104 + 16 * i:120 + 16 * i].rearrange("p (t n) -> p t n", t=TT)
                                        for i in range(4))
        e_score = rt[:, 168:232].rearrange("p (t n) -> p t n", t=TT)
        picks = rt[:, 232:360].rearrange("p (k t n) -> p k t n", k=2, t=TT)
        wide = rt[:, 360:424].rearrange("p (t n) -> p t n", t=TT)
        top_w = rt[:, 424:432].rearrange("p (t k) -> p t k", t=TT)
        member = rt[:, 432:464].bitcast(F16).rearrange("p (t n) -> p t n", t=TT)
        place = rt[:, 464:528].rearrange("p (t n) -> p t n", t=TT)
        result_row = rt[:, 528:592].rearrange("p (t n) -> p t n", t=TT)
        row_f = rt[:, 592:600].rearrange("p (t k) -> p t k", t=TT)
        slot_tok = rt[:, 600:616].bitcast(I32)
        back_idx = rt[:, 616:624].bitcast(I32)
        over_place, over_tok = rt[:, 624:628], rt[:, 628:629].bitcast(I32)
        most = rt[:, 629:630]
        sel_over = arena[:, 4096:4096 + 256].bitcast(F16).rearrange("p (t c) -> p t c", t=TT)

        EARLY = 12
        UNITS = HEADS * TT

        def job_bank(j):
            return 6 + j % 2

        def act_job(j):
            return j % 2 == 0 or j >= EARLY

        def jobs_before(j, on_act):
            return sum(act_job(i) == on_act for i in range(j))

        @block.gpsimd
        def _(pool):
            g = nc.gpsimd

            def load_gain(n, src):
                if n:
                    pool.wait_ge(h_ready, n * TT)
                pool.dma_start(gain[:, :], src.partition_broadcast(P)).then_inc(gain_loaded, 16)

            load_gain(0, A["norm_mix"][0])
            g.memset(ident[:, :], 0.0).then_inc(zeros_ready, 1)
            g.memset(later[:, :], 0.0).then_inc(zeros_ready, 1)
            g.memset(head_row[:, :, :], 0.0).then_inc(zeros_ready, 1)
            g.memset(w_gates[:, :, :], 0.0).then_inc(zeros_ready, 1)
            g.memset(ones16[:, :], 1.0).then_inc(zeros_ready, 1)
            g.memset(minus_half[:, :], -0.5).then_inc(zeros_ready, 1)
            pool.wait_ge(zeros_ready, 6)
            g.affine_select(out=ident[:, :], in_=ident[:, :], compare_op=ALU.not_equal, fill=1.0, base=0,
                            pattern=[[-1, P]], channel_multiplier=1).then_inc(consts_ready, 1)
            g.affine_select(out=later[:, :], in_=later[:, :], compare_op=ALU.is_ge, fill=1.0, base=0,
                            pattern=[[-1, P]], channel_multiplier=1).then_inc(consts_ready, 1)
            g.affine_select(out=head_row[:, :, :], in_=head_row[:, :, :], compare_op=ALU.not_equal, fill=1.0, base=0,
                            pattern=[[-1, HEADS], [0, P]], channel_multiplier=1).then_inc(consts_ready, 1)
            g.iota(slot_iota[:, :], [[1, P]], base=0, channel_multiplier=0,
                   allow_small_or_imprecise_dtypes=True).then_inc(consts_ready, 1)
            g.iota(tok_id[:, :], [[P, TT]], base=0, channel_multiplier=1,
                   allow_small_or_imprecise_dtypes=True).then_inc(consts_ready, 1)
            g.iota(iota16[:, :], [[1, E]], base=0, channel_multiplier=0,
                   allow_small_or_imprecise_dtypes=True).then_inc(consts_ready, 1)
            g.iota(iota_slot0[:, :], [[CAP, E]], base=0, channel_multiplier=0,
                   allow_small_or_imprecise_dtypes=True).then_inc(consts_ready, 1)

            steps = [0]

            def rstd(dst, src, n, width, ready):
                g.tensor_scalar(dst, src, 1.0 / width, EPS, ALU.mult, ALU.add).then_inc(pool_step, 1)
                steps[0] += 1
                pool.wait_ge(pool_step, steps[0])
                g.tensor_tensor(dst, dst, minus_half[:, 0:n], ALU.pow).then_inc(ready, 1)

            def norm(n):
                for t in range(TT):
                    pool.wait_ge(sumsq_ready, n * TT + t + 1)
                    rstd(st[:, 4 + t:5 + t], st[:, t:t + 1], 1, D, norm_rstd)

            norm(0)
            load_gain(1, A["norm_ffn"][0])
            for h in range(HEADS):
                pool.wait_ge(o_sums, h + 1)
                rstd(st[:, 68:72], st[:, 64:68], TT, P, o_rstd)
            for h in range(HEADS):
                pool.wait_ge(m_exp, h + 1)
                w = decay[:, h % 2, :].rearrange("p (j k) -> p j k", j=TT)
                for j in range(TT):
                    last = g.affine_select(out=w[:, j, 0:P], in_=w[:, j, 0:P], compare_op=ALU.is_ge, fill=0.0, base=0,
                                           pattern=[[1, P]], channel_multiplier=-1)
                last.then_inc(m_masked, 1)
                if h:
                    pool.wait_ge(m_sums, h)
                    rstd(st[:, 84:88], st[:, 80:84], TT, P, m_rstd)
            pool.wait_ge(m_sums, HEADS)
            rstd(st[:, 84:88], st[:, 80:84], TT, P, m_rstd)
            pool.wait_ge(mo_full, HEADS)
            pool.dma_start(x_sb[:, :, :], A["x"][0].rearrange("(t p) d -> p t d", p=P)).then_inc(x_reloaded, 16)

            for l in range(2):
                norm(2 * l + 1)
                for t in range(TT):
                    pool.wait_ge(h_ready, (2 * l + 1) * TT + t + 1)
                    pool.dma_start(h_dram[t * P:(t + 1) * P, :], h_rows[:, t, :]).then_inc(h_stored, 16)
                load_gain(2 * l + 2, A["norm_mix"][1] if l == 0 else A["norm_final"])
                pool.wait_ge(h_stored, 16 * TT * (l + 1))
                pool.wait_ge(idx_ready, l + 1)
                for e in range(E):
                    if e >= 2:
                        pool.wait_ge(xg_turned, E * l + e - 1)
                    g.indirect_dma_start(out=xg[0:CAP, e % 2, :], out_offset=None, in_=h_dram,
                                         in_offset=bass.IndirectOffsetOnAxis(ap=slot_tok[0:CAP, e:e + 1], axis=0)
                                         ).then_inc(xg_landed[e % 2], 16)
                o = over[l]
                pool.wait_ge(flag_ready, l + 1)

                def take_back(rows):
                    for u in range(2):
                        pool.wait_ge(y_stored[u], 16 * (E // 2) * (l + 1))
                    for t in range(TT):
                        for k in range(2):
                            c = 2 * t + k
                            g.indirect_dma_start(out=y_back[:, t, k, :], out_offset=None, in_=y_dram[0:rows, :],
                                                 in_offset=bass.IndirectOffsetOnAxis(ap=back_idx[:, c:c + 1], axis=0)
                                                 ).then_inc(y_back_loaded, 16)

                with pool.If(pool.value_load(overflow_flag[0:1, l:l + 1], min_val=0, max_val=1) > 0):
                    with pool.Fori(0, E * OVER) as it:
                        pool.wait_ge(o["idx"], it + 1)
                        pool.sem_inc(o["gathers"], 1)
                        g.indirect_dma_start(out=xg[0:CAP, 0, :], out_offset=None, in_=h_dram,
                                             in_offset=bass.IndirectOffsetOnAxis(ap=over_tok[0:CAP, :], axis=0)
                                             ).then_inc(o["xg"], 16)
                    pool.wait_ge(o["stored"], 16 * E * OVER)
                    take_back(E * T)
                with pool.Else():
                    take_back(E * CAP)
                norm(2 * l + 2)
                if l == 0:
                    load_gain(3, A["norm_ffn"][1])

        @block.scalar
        def _(act):
            s = nc.scalar

            small = [
                (rel_w[0:BUCKETS, :], A["rel_bias"]),
                (table[0:BUCKETS + 1, :], A["bucket_table"]),
                (lams[:, 0, :], A["lam_q1"][0].partition_broadcast(P)),
                (lams[:, 1, :], A["lam_k1"][0].partition_broadcast(P)),
                (lams[:, 2, :], A["lam_q2"][0].partition_broadcast(P)),
                (lams[:, 3, :], A["lam_k2"][0].partition_broadcast(P)),
                (gate_b[0:HEADS, :], A["m_igate_b"].rearrange("a h -> h a")),
                (gate_b[32:32 + HEADS, :], A["m_fgate_b"].rearrange("a h -> h a")),
                (head_norm[:, :], A["m_head_norm"][0].rearrange("(h p) -> p h", p=P)),
                (subln[:, :], A["da_subln"].rearrange("a p -> p a")),
            ]
            small += [(conv_sb[:, :, i], A["conv_w"][0, i].rearrange("(k p) -> p k", p=P)) for i in range(3)]
            for l in range(2):
                small += [
                    (w_route[:, l, :, 0:GROUPS], A["router_group_w"][l].rearrange("(k p) n -> p k n", p=P)),
                    (w_route[:, l, :, GROUPS:NR], A["router_expert_w"][l].rearrange("(k p) n -> p k n", p=P)),
                    (b_route[:, l, 0:GROUPS], A["router_group_b"][l].partition_broadcast(P)),
                    (b_route[:, l, GROUPS:NR], A["router_expert_b"][l].partition_broadcast(P)),
                ]
            small += [
                (w_gates[:, :, 0:HEADS], cols(w_even, 4 * 512, HEADS)),
                (w_gates[:, :, 32:32 + HEADS], cols(w_even, 4 * 512 + HEADS, HEADS)),
            ]
            assert len(small) == SMALL
            act.wait_ge(zeros_ready, 4)
            for dst, src in small:
                act.dma_start(dst, src, allow_slow_non_contiguous=True).then_inc(small_loaded, 16)

            def norm(n, copies=True):
                for t in range(TT):
                    if n == 0:
                        act.wait_ge(x_loaded, 16)
                    else:
                        act.wait_ge(x_ready, (n - 1) * TT + t + 1)
                    if n or t:
                        act.wait_ge(sumsq_ready, n * TT + t)
                    s.activation(junk, x_sb[:, t, :], ACT.Square, accum_out=st[:, t:t + 1]).then_inc(sumsq_ready, 1)
                for t in range(TT if copies else 0):
                    act.wait_ge(tr_full, 2 * (n * TT + t) + 1)
                    s.copy(hT[:, 0:4, t * P:(t + 1) * P],
                           ps[:, 2 * (t % 2), :].rearrange("p (k c) -> p k c", k=4)).then_inc(tr_act, 1)

            norm(0)
            act.wait_ge(lam_sum, 2)
            s.activation(st[:, 10:12], st[:, 8:10], ACT.Exp).then_inc(lam_exp, 1)
            act.wait_ge(v_row_ready, 2)
            act.dma_start(v_dram, v_row[0:HEADS, :].unsqueeze(1).broadcast_to([HEADS, P, VROW])).then_inc(v_stored, 16)
            act.wait_ge(v_stored, 16)

            def load_bias(h):
                src = bass.AP(v_dram.tensor, h * P * VROW + P - 1, [[VROW - 1, P], [1, T]])
                act.dma_start(bias_sb[:, h % 2, :], src).then_inc(bias_loaded[h % 2], 16)

            load_bias(0)
            load_bias(1)
            act.wait_ge(gate_rows_ready, 1)
            s.activation(gate_rows[0:HEADS, 2, :], gate_rows[0:HEADS, 2, :], ACT.Exp, scale=-1.0).then_inc(act_step, 1)
            act.wait_ge(act_step, 1)
            s.activation(gate_rows[0:HEADS, 2, :], gate_rows[0:HEADS, 2, :], ACT.Ln, bias=1.0).then_inc(gate_act, 1)
            act.wait_ge(gate_rows_ready, 2)
            s.activation(gate_rows[0:HEADS, 7, :], gate_rows[0:HEADS, 7, :], ACT.Exp).then_inc(gate_act, 1)

            def job(j):
                kind, i = j // 4, j % 4
                src = ps[:, job_bank(j), :]
                act.wait_ge(job_full, j + 1)
                if kind == 0:
                    ins = s.copy(q_cat[:, HEADS + i, :], src)
                elif kind == 1:
                    ins = s.copy(dkT[:, i, :], src)
                elif kind == 2:
                    ins = s.copy(dv[:, i, :], src)
                elif kind == 3:
                    ins = s.copy(q_cat[:, i, :], src)
                elif kind == 4:
                    ins = s.activation(mkT[:, i, :], src, ACT.Copy, scale=float(P) ** -0.5)
                elif kind == 5:
                    ins = s.copy(mv[:, i, :, 0:P], src.rearrange("p (h c) -> p h c", h=HEADS))
                else:
                    ins = s.activation(mo[:, i, :], src, ACT.Exp, scale=-1.0)
                ins.then_inc(job_act, 1)

            for j in range(0, EARLY, 2):
                job(j)

            def soft(u):
                n = (u % TT + 1) * P
                act.wait_ge(s_max, u + 1)
                for m in range(2):
                    c = 2 * (u % 2) + m
                    s.activation(e_maps[:, u % 2, m, 0:n], e_maps[:, u % 2, m, 0:n], ACT.Exp,
                                 bias=st[:, 16 + c:17 + c], accum_out=st[:, 20 + c:21 + c]).then_inc(e_ready, 1)

            def copy_aT(u):
                n = (u % TT + 1) * P
                act.wait_ge(a_turned, u + 1)
                if u >= 2:
                    act.wait_ge(o_unit, u - 1)
                s.copy(aT[:, u % 2, 0:n], ps[:, 4, 0:n]).then_inc(aT_ready, 1)

            for step in range(UNITS + 4):
                if step < UNITS:
                    soft(step)
                    job(EARLY + step)
                    if step % TT == TT - 1 and step // TT + 2 < HEADS:
                        act.wait_ge(s_biased, step + 1)
                        load_bias(step // TT + 2)
                if 1 <= step <= UNITS:
                    copy_aT(step - 1)
                if step >= 5 and (step - 5) % TT == 0:
                    h = (step - 5) // TT
                    act.wait_ge(o_full, h + 1)
                    if h >= 1:
                        act.wait_ge(o_normed, h)
                    s.activation(post[:, 0, :], ps[:, 5, :], ACT.Square).then_inc(o_square, 1)
                if step >= 7 and (step - 7) % TT == 0:
                    h = (step - 7) // TT
                    act.wait_ge(on_turned, h + 1)
                    act.wait_ge(subln_ready, 1)
                    s.activation(q_cat[:, HEADS + h, :], ps[:, 4, :], ACT.Copy, scale=subln[:, 0:1]).then_inc(cat_ready, 1)
            act.wait_ge(o_full, HEADS)

            for h in range(HEADS + 2):
                if h < HEADS:
                    act.wait_ge(m_arg, h + 1)
                    for j in range(TT):
                        w = decay[:, h % 2, j * T:j * T + T - j * P]
                        last = s.activation(w, w, ACT.Exp)
                    last.then_inc(m_exp, 1)
                if 1 <= h <= HEADS:
                    act.wait_ge(m_centred, h)
                    s.activation(post[:, 1, :], post[:, 0, :], ACT.Square).then_inc(m_square, 1)
                if h >= 2:
                    act.wait_ge(m_turned, h - 1)
                    s.activation(q_cat[:, h - 2, :], ps[:, 7, :], ACT.Copy,
                                 scale=head_norm[:, h - 2:h - 1]).then_inc(m_cat, 1)

            def copy_xgT(n, u):
                act.wait_ge(xg_turned, n + 1)
                s.copy(xgT[:, u, 0:4, 0:CAP],
                       ps[:, 5, :].rearrange("p (k c) -> p k c", k=4)[:, :, 0:CAP]).then_inc(xgT_act, 1)

            def silu(n, gate_done, first=False):
                act.wait_ge(piece_done, gate_done)
                if not first:
                    act.wait_ge(act_ready, n)
                s.activation(sg[0:CAP, :], ps[0:CAP, 0, :], ACT.Silu).then_inc(silu_ready, 1)

            def finish(l, e, n, u, stored_before):
                act.wait_ge(act_turned, n + 1)
                s.copy(actT[:, u, :, 0:CAP],
                       ps[:, 4, :].rearrange("p (k c) -> p k c", k=KF)[:, :, 0:CAP]).then_inc(actT_ready, 1)
                act.wait_ge(down_full, n + 1)
                if stored_before is not None:
                    act.wait_ge(y_stored[u], stored_before)
                s.copy(y_sb[0:CAP, u, 0:512], ps[0:CAP, 2, :]).then_inc(y_act, 1)
                act.wait_ge(y_act, n + 1)
                act.wait_ge(y_dve, n + 1)
                act.dma_start(y_dram[bass.ds(e * CAP, CAP), :], y_sb[0:CAP, u, :]).then_inc(y_stored[u], 16)

            def experts(l):
                act.wait_ge(route_arg, 2 * l + 1)
                s.activation(g_exp, g_exp, ACT.Exp).then_inc(route_exp, 1)
                act.wait_ge(route_arg, 2 * l + 2)
                s.activation(prob[:, 0, :], prob[:, 0, :], ACT.Exp).then_inc(route_exp, 1)
                n0 = E * l
                copy_xgT(n0, 0)
                base = MOE_BASE[l]
                silu(n0, base + 1, first=(l == 0))
                copy_xgT(n0 + 1, 1)
                for e in (1, 2):
                    n = n0 + e
                    silu(n, base + 3 * e)
                    finish(l, e - 1, n - 1, (e - 1) % 2, 16 * ((n - 1) // 2) or None)
                    copy_xgT(n + 1, (e + 1) % 2)
                with act.Fori(0, E // 2 - 2) as i:
                    for u in range(2):
                        silu(i * 2 + (3 + u + n0), i * 6 + (base + 3 * (3 + u)))
                        finish(l, i * 2 + (2 + u), i * 2 + (2 + u + n0), u, i * 16 + 16 * (1 + n0 // 2))
                        copy_xgT(i * 2 + (4 + u + n0), u)
                n = n0 + E - 1
                silu(n, base + 3 * (E - 1))
                finish(l, E - 2, n - 1, 0, 16 * ((n - 1) // 2))
                finish(l, E - 1, n, 1, 16 * (n // 2))
                o = over[l]
                act.wait_ge(flag_ready, l + 1)
                with act.If(act.value_load(overflow_flag[0:1, l:l + 1], min_val=0, max_val=1) > 0):
                    with act.Fori(0, E * OVER) as it:
                        act.wait_ge(o["done"], it * 3 + 1)
                        s.activation(sg[0:CAP, :], ps[0:CAP, 3, :], ACT.Silu).then_inc(o["silu"], 1)

            norm(1)
            experts(0)
            norm(2)
            for half in range(2):
                for i in range(4):
                    j = half * 12 + i
                    act.wait_ge(odd_full, j + 1)
                    if half:
                        act.wait_ge(odd_z, i + 1)
                    s.copy(cg_sb[:, i, :], ps[:, j % 8, :]).then_inc(odd_cg, 1)
            norm(3)
            experts(1)
            norm(4, copies=False)

        @block.vector
        def _(dve):
            v = nc.vector
            done = [0]

            def link(ins):
                done[0] += 1
                ins.then_inc(dve_step, 1)
                dve.wait_ge(dve_step, done[0])

            def bc(ap, axis, *shape):
                return ap.unsqueeze(axis).broadcast_to(list(shape))

            def norm(n, copies=True):
                def copy(t):
                    dve.wait_ge(tr_full, 2 * (n * TT + t) + 2)
                    v.tensor_copy(hT[:, 4:8, t * P:(t + 1) * P],
                                  ps[:, 2 * (t % 2) + 1, :].rearrange("p (k c) -> p k c", k=4)).then_inc(tr_dve, 1)

                dve.wait_ge(gain_loaded, 16 * (n + 1))
                for t in range(TT):
                    dve.wait_ge(norm_rstd, n * TT + t + 1)
                    ins = v.scalar_tensor_tensor(out=h_rows[:, t, :], in0=x_sb[:, t, :], scalar=st[:, 4 + t:5 + t],
                                                 in1=gain[:, :], op0=ALU.mult, op1=ALU.mult)
                    ins.then_inc(h_ready, 1)
                    if copies and t:
                        copy(t - 1)
                if copies:
                    copy(TT - 1)

            v.memset(rel_w[32:33, :], -BIG).then_inc(v_row_ready, 1)
            for half in range(2):
                dve.wait_ge(vbias_full, half + 1)
                last = v.tensor_copy(v_row[0:HEADS, half * 320:half * 320 + 320], ps[0:HEADS, 6 + half, 0:320])
            last.then_inc(v_row_ready, 1)
            dve.wait_ge(small_loaded, 16 * SMALL)
            v.tensor_scalar(subln[:, :], subln[:, :], 1.0 - LAM_INIT, None, ALU.mult).then_inc(subln_ready, 1)
            for i in range(2):
                link(v.tensor_tensor(lams[:, 2 * i, :], lams[:, 2 * i, :], lams[:, 2 * i + 1, :], ALU.mult))
                v.tensor_reduce(st[:, 8 + i:9 + i], lams[:, 2 * i, :], AX, ALU.add).then_inc(lam_sum, 1)
            norm(0)
            dve.wait_ge(lam_exp, 1)
            link(v.tensor_tensor(st[:, 12:13], st[:, 10:11], st[:, 11:12], ALU.subtract))
            link(v.tensor_scalar(st[:, 13:14], st[:, 12:13], LAM_INIT, None, ALU.add))
            lam = st[:, 13:14]

            dve.wait_ge(gates_full, 1)
            G = lambda k: gate_rows[0:HEADS, k, :]
            ig, f, soft_part, B, a_row, M, neg_mt, thr_row = (G(k) for k in range(8))
            v.tensor_scalar(ig, ps[0:HEADS, 0, :], gate_b[0:HEADS, 0:1], None, ALU.add)
            link(v.tensor_scalar(f, ps[32:32 + HEADS, 0, :], gate_b[32:32 + HEADS, 0:1], None, ALU.add))
            v.scalar_tensor_tensor(out=soft_part, in0=f, scalar=-1.0, in1=f,
                                   op0=ALU.mult, op1=ALU.max).then_inc(gate_rows_ready, 1)
            link(v.tensor_scalar(f, f, 0.0, None, ALU.min))
            dve.wait_ge(gate_act, 1)
            link(v.tensor_tensor(f, f, soft_part, ALU.subtract))
            link(v.memset(thr_row, 1.0))
            link(v.tensor_tensor_scan(B, thr_row, f, 0.0, ALU.mult, ALU.add))
            link(v.tensor_tensor(a_row, ig, B, ALU.subtract))
            link(v.tensor_tensor_scan(M, a_row, a_row, 0.0, ALU.max, ALU.max))
            link(v.tensor_scalar(neg_m_row[:, :], M, -1.0, None, ALU.mult))
            v.tensor_tensor(thr_row, neg_m_row[:, :], B, ALU.subtract).then_inc(gate_rows_ready, 1)

            for j in range(1, EARLY, 2):
                kind, i = j // 4, j % 4
                dst = (q_cat[:, HEADS + i, :], dkT[:, i, :], dv[:, i, :])[kind]
                dve.wait_ge(job_full, j + 1)
                if j == 5:
                    dve.wait_ge(v_stored, 16)
                v.tensor_copy(dst, ps[:, job_bank(j), :]).then_inc(job_dve, 1)
            dve.wait_ge(gate_cols_full, 1)
            v.tensor_copy(st[:, 32:64], ps[:, 1, 0:32]).then_inc(gate_cols_ready, 1)
            a_col = st[:, 32:48].rearrange("p (j h) -> p j h", j=TT)
            thr_col = st[:, 48:64].rearrange("p (j h) -> p j h", j=TT)
            v.memset(mv[:, :, :, P:P + 1], 1.0)

            def biased(u):
                h, i = u // TT, u % TT
                n = (i + 1) * P
                dve.wait_ge(bias_loaded[h % 2], 16 * (h // 2 + 1))
                dve.wait_ge(s_full, u + 1)
                src = ps[:, 2 * (u % 2):2 * (u % 2) + 2, 0:n]
                v.scalar_tensor_tensor(out=e_maps[:, u % 2, :, 0:n], in0=src, scalar=64.0 ** -0.5,
                                       in1=bc(bias_sb[:, h % 2, T - n:T], 1, P, 2, n),
                                       op0=ALU.mult, op1=ALU.add).then_inc(s_biased, 1)
                dve.wait_ge(s_biased, u + 1)
                c = 16 + 2 * (u % 2)
                v.tensor_reduce(st[:, c:c + 2], e_maps[:, u % 2, :, 0:n], AX, ALU.max, negate=True).then_inc(s_max, 1)

            def combined(u):
                n = (u % TT + 1) * P
                b = u % 2
                dve.wait_ge(e_ready, 2 * (u + 1))
                link(v.reciprocal(st[:, 24:26], st[:, 20 + 2 * b:22 + 2 * b]))
                link(v.tensor_tensor(st[:, 26:27], st[:, 25:26], lam, ALU.mult))
                link(v.tensor_scalar(e_maps[:, b, 1, 0:n], e_maps[:, b, 1, 0:n], st[:, 26:27], None, ALU.mult))
                if u >= 2:
                    dve.wait_ge(a_turned, u - 1)
                v.scalar_tensor_tensor(out=a_map[:, b, 0:n], in0=e_maps[:, b, 0, 0:n], scalar=st[:, 24:25],
                                       in1=e_maps[:, b, 1, 0:n], op0=ALU.mult, op1=ALU.subtract).then_inc(a_ready, 1)

            def mo_sigmoid(i):
                dve.wait_ge(job_act, jobs_before(24 + i + 1, True))
                link(v.tensor_scalar(mo[:, i, :], mo[:, i, :], 1.0, None, ALU.add))
                v.reciprocal(mo[:, i, :], mo[:, i, :])

            def rows4(ap):
                return ap.rearrange("p (i c) -> p i c", i=TT)

            for step in range(UNITS + 4):
                if step < UNITS:
                    biased(step)
                if 1 <= step <= UNITS:
                    combined(step - 1)
                if step >= 14 and step - 14 < 4:
                    mo_sigmoid(step - 14)
                if step >= 5 and (step - 5) % TT == 0:
                    h = (step - 5) // TT
                    dve.wait_ge(o_square, h + 1)
                    v.tensor_reduce(st[:, 64:68], rows4(post[:, 0, :]), AX, ALU.add).then_inc(o_sums, 1)
                    dve.wait_ge(o_rstd, h + 1)
                    if h:
                        dve.wait_ge(on_turned, h)
                    v.tensor_tensor(rows4(post[:, 1, :]), rows4(ps[:, 5, :]), bc(st[:, 68:72], 2, P, TT, P),
                                    ALU.mult).then_inc(o_normed, 1)

            def weights_arg(h):
                dve.wait_ge(m_full, 2 * h + 1)
                if h >= 2:
                    dve.wait_ge(mo_full, h - 1)
                for j in range(TT):
                    n = T - j * P
                    last = v.tensor_scalar(decay[:, h % 2, j * T:j * T + n], ps[:, 4, j * P:T], a_col[:, j, h:h + 1], 0.0,
                                           ALU.add, ALU.min)
                last.then_inc(m_arg, 1)

            def weigh(h):
                dve.wait_ge(m_full, 2 * h + 2)
                dve.wait_ge(m_masked, h + 1)
                for j in range(TT):
                    n = T - j * P
                    w = decay[:, h % 2, j * T:j * T + n]
                    last = v.tensor_tensor(w, ps[:, j, 0:n], w, ALU.mult)
                last.then_inc(m_weighted, 1)

            def head_out(h):
                dve.wait_ge(mo_full, h + 1)
                o4 = ps[:, 5:7, 0:2 * (P + 1)].rearrange("p b (i c) -> p b i c", i=2)
                den = st[:, 72:76].rearrange("p (b i) -> p b i", b=2)
                thr = thr_col[:, :, h].rearrange("p (b i) -> p b i", b=2)
                out4 = post[:, 0, :].rearrange("p (b i c) -> p b i c", b=2, i=2)
                link(v.scalar_tensor_tensor(out=den, in0=o4[:, :, :, P], scalar=-1.0, in1=thr, op0=ALU.mult, op1=ALU.max))
                link(v.tensor_tensor(den, o4[:, :, :, P], den, ALU.max))
                link(v.reciprocal(st[:, 72:76], st[:, 72:76]))
                if h:
                    dve.wait_ge(m_turned, h)
                link(v.tensor_tensor(out4, o4[:, :, :, 0:P], bc(den, 3, P, 2, 2, P), ALU.mult))
                link(v.tensor_reduce(st[:, 76:80], rows4(post[:, 0, :]), AX, ALU.add))
                link(v.tensor_scalar(st[:, 76:80], st[:, 76:80], 1.0 / P, None, ALU.mult))
                v.tensor_tensor(rows4(post[:, 0, :]), rows4(post[:, 0, :]), bc(st[:, 76:80], 2, P, TT, P),
                                ALU.subtract).then_inc(m_centred, 1)
                dve.wait_ge(m_square, h + 1)
                v.tensor_reduce(st[:, 80:84], rows4(post[:, 1, :]), AX, ALU.add).then_inc(m_sums, 1)
                dve.wait_ge(m_rstd, h + 1)
                link(v.tensor_tensor(rows4(post[:, 0, :]), rows4(post[:, 0, :]), bc(st[:, 84:88], 2, P, TT, P), ALU.mult))
                v.tensor_tensor(rows4(post[:, 0, :]), rows4(post[:, 0, :]), mo[:, :, h * P:(h + 1) * P],
                                ALU.mult).then_inc(m_normed, 1)

            for h in range(HEADS + 1):
                if h < HEADS:
                    weights_arg(h)
                if h:
                    head_out(h - 1)
                if h < HEADS:
                    weigh(h)

            def residual(l):
                if l == 0:
                    dve.wait_ge(x_reloaded, 16)
                for j in range(2 * TT):
                    half, t = j // TT, j % TT
                    dve.wait_ge(out_full, 8 * l + j + 1)
                    xt = x_sb[:, t, half * 512:half * 512 + 512]
                    ins = v.tensor_tensor(xt, ps[:, j, :], xt, ALU.add)
                    ins.then_inc(x_ready if half else out_added, 1)

            def first_of(eq, n, dst):
                cand = wide if n == E else g_cand
                link(v.scalar_tensor_tensor(out=cand, in0=eq, scalar=-1000.0, in1=bc(iota16[:, 0:n], 1, P, TT, n),
                                            op0=ALU.mult, op1=ALU.add))
                link(v.tensor_reduce(low, cand, AX, ALU.min))
                link(v.tensor_tensor(dst, cand, bc(low, 2, P, TT, n), ALU.is_equal))

            def route(l):
                dve.wait_ge(consts_ready, 7)
                dve.wait_ge(logits_full, l + 1)
                link(v.tensor_tensor(lg, ps[:, 4, 0:TT * NR].rearrange("p (t n) -> p t n", t=TT),
                                     bc(b_route[:, l, :], 1, P, TT, NR), ALU.add))
                gl, el = lg[:, :, 0:GROUPS], lg[:, :, GROUPS:NR]
                link(v.tensor_reduce(top_v[:, 0, :], gl, AX, ALU.max))
                v.tensor_tensor(g_exp, gl, bc(top_v[:, 0, :], 2, P, TT, GROUPS), ALU.subtract).then_inc(route_arg, 1)
                link(v.tensor_tensor(g_cand, gl, bc(top_v[:, 0, :], 2, P, TT, GROUPS), ALU.is_equal))
                first_of(g_cand, GROUPS, g_pick)
                link(v.tensor_scalar(g_pen, g_pick, BIG, -BIG, ALU.mult, ALU.add))
                for t in range(TT):
                    s4 = e_score[:, t, :].rearrange("p (g j) -> p g j", g=GROUPS)
                    e4 = el[:, t, :].rearrange("p (g j) -> p g j", g=GROUPS)
                    link(v.tensor_tensor(s4, e4, bc(g_pick[:, t, :], 2, P, GROUPS, PER_GROUP), ALU.mult))
                    link(v.tensor_tensor(s4, s4, bc(g_pen[:, t, :], 2, P, GROUPS, PER_GROUP), ALU.add))
                for k in range(2):
                    link(v.tensor_reduce(top_v[:, k, :], e_score, AX, ALU.max))
                    link(v.tensor_tensor(wide, e_score, bc(top_v[:, k, :], 2, P, TT, E), ALU.is_equal))
                    first_of(wide, E, picks[:, k, :, :])
                    if k == 0:
                        link(v.scalar_tensor_tensor(out=e_score, in0=picks[:, 0, :, :], scalar=-2 * BIG, in1=e_score,
                                                    op0=ALU.mult, op1=ALU.add))
                v.tensor_tensor(prob[:, 0, :], top_v[:, 1, :], top_v[:, 0, :], ALU.subtract).then_inc(route_arg, 1)
                v.tensor_tensor(member, picks[:, 0, :, :], picks[:, 1, :, :], ALU.add).then_inc(picks_ready, 1)
                dve.wait_ge(route_exp, 2 * l + 1)
                link(v.tensor_reduce(prob[:, 1, :], g_exp, AX, ALU.add))
                dve.wait_ge(route_exp, 2 * l + 2)
                link(v.tensor_scalar(prob[:, 2, :], prob[:, 0, :], 1.0, None, ALU.add))
                link(v.tensor_tensor(prob[:, 1, :], prob[:, 1, :], prob[:, 2, :], ALU.mult))
                link(v.reciprocal(top_w[:, :, 0], prob[:, 1, :]))
                link(v.tensor_tensor(top_w[:, :, 1], top_w[:, :, 0], prob[:, 0, :], ALU.mult))
                dve.wait_ge(rank_full, l + 1)
                rank = ps[:, 5, 0:64].rearrange("p (t n) -> p t n", t=TT)
                link(v.tensor_tensor(place, rank, picks[:, 0, :, :], ALU.mult))
                link(v.tensor_tensor(wide, rank, picks[:, 1, :, :], ALU.mult))
                link(v.tensor_tensor(place, place, wide, ALU.add))
                link(v.tensor_tensor(wide, picks[:, 0, :, :], picks[:, 1, :, :], ALU.add))
                link(v.scalar_tensor_tensor(out=place, in0=wide, scalar=-1.0, in1=place, op0=ALU.add, op1=ALU.add))
                for t in range(TT):
                    v.tensor_tensor(sel[:, t, :, 0:CAP], bc(place[:, t, :], 2, P, E, CAP),
                                    bc(slot_iota[:, 0:CAP], 1, P, E, CAP), ALU.is_equal).then_inc(sel_ready, 1)
                link(v.tensor_reduce(most, ps[:, 5, 64:64 + E], AX, ALU.max))
                v.tensor_scalar(overflow_flag[:, l:l + 1], most, float(CAP), None, ALU.is_gt).then_inc(flag_ready, 1)
                link(v.tensor_tensor(result_row, rank, bc(iota_slot0[:, :], 1, P, TT, E), ALU.add))
                for j in range(1, OVER + 1):
                    link(v.tensor_scalar(wide, rank, float(j * CAP), float((E - 1) * CAP), ALU.is_ge, ALU.mult))
                    link(v.tensor_tensor(result_row, result_row, wide, ALU.add))
                for k in range(2):
                    link(v.tensor_tensor(wide, result_row, picks[:, k, :, :], ALU.mult))
                    link(v.tensor_reduce(row_f[:, :, k], wide, AX, ALU.add))
                link(v.tensor_copy(back_idx, rt[:, 592:600]))
                dve.wait_ge(idx_full, l + 1)
                v.tensor_copy(slot_tok[0:CAP, :], ps[0:CAP, 6, 0:E]).then_inc(idx_ready, 1)

            def copy_xgT(n, u):
                dve.wait_ge(xg_turned, n + 1)
                v.tensor_copy(xgT[:, u, 4:8, 0:CAP],
                              ps[:, 6, :].rearrange("p (k c) -> p k c", k=4)[:, :, 0:CAP]).then_inc(xgT_dve, 1)

            def hidden(n, up_done):
                dve.wait_ge(silu_ready, n + 1)
                dve.wait_ge(piece_done, up_done)
                v.tensor_tensor(act_h[0:CAP, :], sg[0:CAP, :], ps[0:CAP, 1, :], ALU.mult).then_inc(act_ready, 1)

            def finish(n, u, stored_before, down_done):
                dve.wait_ge(piece_done, down_done)
                if stored_before is not None:
                    dve.wait_ge(y_stored[u], stored_before)
                v.tensor_copy(y_sb[0:CAP, u, 512:1024], ps[0:CAP, 3, :]).then_inc(y_dve, 1)

            def experts(l):
                n0 = E * l
                copy_xgT(n0, 0)
                base = MOE_BASE[l]
                hidden(n0, base + 2)
                copy_xgT(n0 + 1, 1)
                for e in (1, 2):
                    n = n0 + e
                    hidden(n, base + 3 * e + 1)
                    finish(n - 1, (e - 1) % 2, 16 * ((n - 1) // 2) or None, base + 3 * e + 2)
                    copy_xgT(n + 1, (e + 1) % 2)
                with dve.Fori(0, E // 2 - 2) as i:
                    for u in range(2):
                        hidden(i * 2 + (3 + u + n0), i * 6 + (base + 3 * (3 + u) + 1))
                        finish(i * 2 + (2 + u + n0), u, i * 16 + 16 * (1 + n0 // 2), i * 6 + (base + 3 * (3 + u) + 2))
                        copy_xgT(i * 2 + (4 + u + n0), u)
                n = n0 + E - 1
                hidden(n, base + 3 * E - 2)
                finish(n - 1, 0, 16 * ((n - 1) // 2), base + 3 * E - 1)
                finish(n, 1, 16 * (n // 2), base + 3 * E)
                o = over[l]
                with dve.If(dve.value_load(overflow_flag[0:1, l:l + 1], min_val=0, max_val=1) > 0):
                    with dve.Fori(0, E) as e:
                        with dve.Fori(0, OVER) as j:
                            it = e * OVER + j
                            v.tensor_scalar(over_place, place[:, :, bass.ds(e, 1)].rearrange("p t n -> p (t n)"),
                                            float(-CAP), None, ALU.add).then_inc(o["place"], 1)
                            dve.wait_ge(o["place"], it * 2 + 1)
                            for t in range(TT):
                                last = v.tensor_scalar(sel_over[:, t, 0:CAP], slot_iota[:, 0:CAP],
                                                       over_place[:, t:t + 1], None, ALU.is_equal)
                            last.then_inc(o["sel"], 1)
                            v.tensor_copy(place[:, :, bass.ds(e, 1)].rearrange("p t n -> p (t n)"),
                                          over_place).then_inc(o["place"], 1)
                            dve.wait_ge(o["place"], it * 2 + 2)
                            dve.wait_ge(o["idx_full"], it + 1)
                            v.tensor_copy(over_tok[0:CAP, :], ps[0:CAP, 0, 0:1]).then_inc(o["idx"], 1)
                            dve.wait_ge(o["turned"], it + 1)
                            v.tensor_copy(xgT[:, 0, :, 0:CAP],
                                          ps[:, 1:3, :].rearrange("p b (k c) -> p (b k) c", k=4)[:, :, 0:CAP]).then_inc(o["xgT"], 1)
                            dve.wait_ge(o["silu"], it + 1)
                            dve.wait_ge(o["done"], it * 3 + 2)
                            v.tensor_tensor(act_h[0:CAP, :], sg[0:CAP, :], ps[0:CAP, 4, :], ALU.mult).then_inc(o["act"], 1)
                            dve.wait_ge(o["act_turned"], it + 1)
                            v.tensor_copy(actT[:, 0, :, 0:CAP],
                                          ps[:, 5, :].rearrange("p (k c) -> p k c", k=KF)[:, :, 0:CAP]).then_inc(o["actT"], 1)
                            dve.wait_ge(o["done"], it * 3 + 3)
                            v.tensor_copy(y_sb[0:CAP, 0, :],
                                          ps[0:CAP, 6:8, :].rearrange("p b n -> p (b n)")).then_inc(o["y"], 1)
                            dve.wait_ge(o["stored"], it * 16 + 16)
                for t in range(TT):
                    for k in range(2):
                        dve.wait_ge(y_back_loaded, 16 * (8 * l + 8))
                        ins = v.scalar_tensor_tensor(out=x_sb[:, t, :], in0=y_back[:, t, k, :], scalar=top_w[:, t, k:k + 1],
                                                     in1=x_sb[:, t, :], op0=ALU.mult, op1=ALU.add)
                        if k == 0:
                            link(ins)
                    ins.then_inc(x_ready, 1)

            residual(0)
            norm(1)
            route(0)
            experts(0)
            norm(2)
            link(v.memset(z_sb[:, :, 0:2], 0.0))
            for half in range(2):
                for i in range(4):
                    j = half * 12 + 4 + i
                    dve.wait_ge(odd_cg, 4 * half + i + 1)
                    dve.wait_ge(odd_full, j + 1)
                    v.tensor_tensor(z_sb[:, i, 2:T + 2], ps[:, j % 8, :], cg_sb[:, i, :], ALU.mult).then_inc(odd_z, 1)
                    dve.wait_ge(odd_z, 4 * half + i + 1)
                    w = conv_sb[:, 4 * half + i, :]
                    link(v.tensor_scalar(zc[:, i, :], z_sb[:, i, 0:T], w[:, 0:1], None, ALU.mult))
                    for tap in (1, 2):
                        link(v.scalar_tensor_tensor(out=zc[:, i, :], in0=z_sb[:, i, tap:tap + T], scalar=w[:, tap:tap + 1],
                                                    in1=zc[:, i, :], op0=ALU.mult, op1=ALU.add))
                for i in range(4):
                    j = half * 12 + 8 + i
                    dve.wait_ge(odd_full, j + 1)
                    v.tensor_tensor(yT[:, 4 * half + i, :], ps[:, j % 8, :], zc[:, i, :], ALU.mult).then_inc(odd_y, 1)
            residual(1)
            norm(3)
            route(1)
            experts(1)
            norm(4, copies=False)

        @block.tensor
        def _(pe):
            mm = nc.tensor.matmul

            def norm(n):
                for t in range(TT):
                    pe.wait_ge(h_ready, n * TT + t + 1)
                    for b in range(2):
                        if t >= 2:
                            pe.wait_ge(tr_dve if b else tr_act, n * TT + t - 1)
                        for k in range(4):
                            c = 4 * b + k
                            last = nc.tensor.transpose(ps[:, 2 * (t % 2) + b, k * P:(k + 1) * P],
                                                       h_rows[:, t, c * P:(c + 1) * P], ident[:, :])
                        last.then_inc(tr_full, 1)

            def h_complete(n):
                pe.wait_ge(tr_act, (n + 1) * TT)
                pe.wait_ge(tr_dve, (n + 1) * TT)

            pe.wait_ge(small_loaded, 16 * SMALL)
            pe.wait_ge(v_row_ready, 1)
            for half in range(2):
                mm(ps[0:HEADS, 6 + half, 0:320], rel_w[0:BUCKETS + 1, :],
                   table[0:BUCKETS + 1, half * 320:half * 320 + 320], start=True, stop=True).then_inc(vbias_full, 1)
            pe.wait_ge(consts_ready, 7)
            norm(0)
            h_complete(0)
            for k in range(KD):
                last = mm(ps[0:36, 0, :], w_gates[:, k, :], hT[:, k, :], start=(k == 0), stop=(k == KD - 1))
            last.then_inc(gates_full, 1)
            pe.wait_ge(v_row_ready, 2)

            def job(j):
                kind, i = j // 4, j % 4
                landed(pe, kind)
                if j >= 2:
                    on_act = act_job(j - 2)
                    pe.wait_ge(job_act if on_act else job_dve, jobs_before(j - 1, on_act))
                for k in range(KD):
                    w, h = slot(kind)[:, k, :], hT[:, k, :]
                    if kind in (0, 1, 3, 4):
                        last = mm(ps[:, job_bank(j), :], w[:, i * P:(i + 1) * P], h, start=(k == 0), stop=(k == KD - 1))
                    else:
                        last = mm(ps[:, job_bank(j), :], h[:, i * P:(i + 1) * P], w, start=(k == 0), stop=(k == KD - 1))
                last.then_inc(job_full, 1)
                if i == 3:
                    return True

            def release():
                pe.sem_inc(piece_done, 1)

            def all_jobs(js):
                for j in js:
                    if job(j):
                        pe.wait_ge(job_full, j + 1)
                        release()

            all_jobs(range(0, EARLY))
            pe.wait_ge(gate_act, 2)
            pe.wait_ge(gate_rows_ready, 2)
            for k, row in enumerate((4, 7)):
                for j in range(TT):
                    c = 16 * k + 4 * j
                    last = nc.tensor.transpose(ps[:, 1, c:c + HEADS], gate_rows[0:HEADS, row, j * P:(j + 1) * P],
                                               ident[0:HEADS, 0:HEADS])
            last.then_inc(gate_cols_full, 1)
            pe.wait_ge(gate_cols_ready, 1)
            pe.wait_ge(job_act, EARLY // 2)
            pe.wait_ge(job_dve, EARLY // 2)

            def scores(u):
                h, i = u // TT, u % TT
                n = (i + 1) * P
                if u >= 2:
                    pe.wait_ge(s_biased, u - 1)
                for m in range(2):
                    r = slice(64 * m, 64 * m + 64)
                    last = mm(ps[:, 2 * (u % 2) + m, 0:n], q_cat[r, HEADS + h, i * P:(i + 1) * P], dkT[r, h, 0:n],
                              start=True, stop=True)
                last.then_inc(s_full, 1)

            def turn_a(u):
                pe.wait_ge(a_ready, u + 1)
                if u:
                    pe.wait_ge(aT_ready, u)
                heads_turned = 0 if u < 7 else (u - 7) // TT + 1
                if u >= 7:
                    pe.wait_ge(cat_ready, heads_turned)
                for j in range(u % TT + 1):
                    last = nc.tensor.transpose(ps[:, 4, j * P:(j + 1) * P], a_map[:, u % 2, j * P:(j + 1) * P], ident[:, :])
                last.then_inc(a_turned, 1)

            def attend(u):
                h, i = u // TT, u % TT
                pe.wait_ge(aT_ready, u + 1)
                if i == 0 and h:
                    pe.wait_ge(o_normed, h)
                for j in range(i + 1):
                    last = mm(ps[:, 5, i * P:(i + 1) * P], aT[:, u % 2, j * P:(j + 1) * P], dv[:, j, h * P:(h + 1) * P],
                              start=(j == 0), stop=(j == i))
                last.then_inc(o_unit, 1)
                if i == TT - 1:
                    pe.wait_ge(o_unit, u + 1)
                    pe.sem_inc(o_full, 1)

            def turn_out(h):
                pe.wait_ge(o_normed, h + 1)
                pe.wait_ge(aT_ready, min(UNITS, 4 * h + 7))
                for i in range(TT):
                    last = nc.tensor.transpose(ps[:, 4, i * P:(i + 1) * P], post[:, 1, i * P:(i + 1) * P], ident[:, :])
                last.then_inc(on_turned, 1)

            for step in range(UNITS + 4):
                if step < UNITS:
                    scores(step)
                    all_jobs([EARLY + step])
                if 1 <= step <= UNITS:
                    turn_a(step - 1)
                if 2 <= step <= UNITS + 1:
                    attend(step - 2)
                if step >= 7 and (step - 7) % TT == 0:
                    turn_out((step - 7) // TT)

            pe.wait_ge(job_act, EARLY // 2 + 16)
            for h in range(HEADS + 2):
                if h < HEADS:
                    if h:
                        pe.wait_ge(m_arg, h)
                    else:
                        pe.wait_ge(cat_ready, HEADS)
                    mm(ps[:, 4, :], head_row[:, h, :], neg_m_row[:, :], start=True, stop=True).then_inc(m_full, 1)
                    if h:
                        pe.wait_ge(m_weighted, h)
                    for j in range(TT):
                        n = T - j * P
                        last = mm(ps[:, j, 0:n], mkT[:, h, j * P:(j + 1) * P], q_cat[:, h, j * P:T], start=True, stop=True)
                    last.then_inc(m_full, 1)
                if 1 <= h + 1 and h >= 1 and h - 1 < HEADS:
                    g = h - 1
                if h < HEADS:
                    pe.wait_ge(m_weighted, h + 1)
                    if h:
                        pe.wait_ge(m_centred, h)
                    for i in range(TT):
                        for j in range(i + 1):
                            c = (i % 2) * (P + 1)
                            last = mm(ps[:, 5 + i // 2, c:c + P + 1],
                                      decay[:, h % 2, j * T + (i - j) * P:j * T + (i - j + 1) * P],
                                      mv[:, j, h, :], start=(j == 0), stop=(j == i))
                    last.then_inc(mo_full, 1)
                if 1 <= h <= HEADS:
                    g = h - 1
                    pe.wait_ge(m_normed, g + 1)
                    if g:
                        pe.wait_ge(m_cat, g)
                    for i in range(TT):
                        last = nc.tensor.transpose(ps[:, 7, i * P:(i + 1) * P], post[:, 0, i * P:(i + 1) * P], ident[:, :])
                    last.then_inc(m_turned, 1)
            pe.wait_ge(m_cat, HEADS)

            def project_out(l, base, src):
                for half in range(2):
                    landed(pe, base + half)
                    for t in range(TT):
                        for k in range(KD):
                            last = mm(ps[:, half * TT + t, :], src[:, k, t * P:(t + 1) * P], slot(base + half)[:, k, :],
                                      start=(k == 0), stop=(k == KD - 1))
                        last.then_inc(out_full, 1)
                    pe.wait_ge(out_full, 8 * l + 4 * half + 4)
                    release()

            def route(l):
                for t in range(TT):
                    for k in range(KD):
                        last = mm(ps[:, 4, t * NR:(t + 1) * NR], hT[:, k, t * P:(t + 1) * P], w_route[:, l, k, :],
                                  start=(k == 0), stop=(k == KD - 1))
                last.then_inc(logits_full, 1)
                pe.wait_ge(picks_ready, l + 1)
                for t in range(TT):
                    for r in range(t + 1):
                        mm(ps[:, 5, t * E:(t + 1) * E], (later if r == t else ones16)[:, :], member[:, r, :],
                           start=(r == 0), stop=(r == t))
                for r in range(TT):
                    last = mm(ps[:, 5, TT * E:(TT + 1) * E], ones16[:, :], member[:, r, :], start=(r == 0), stop=(r == TT - 1))
                last.then_inc(rank_full, 1)
                pe.wait_ge(sel_ready, TT * (l + 1))
                for e in range(E):
                    for t in range(TT):
                        last = mm(ps[0:CAP, 6, e:e + 1], sel[:, t, e, 0:CAP], tok_id[:, t:t + 1],
                                  start=(t == 0), stop=(t == TT - 1))
                last.then_inc(idx_full, 1)
                pe.wait_ge(idx_ready, l + 1)

            def turn_xg(n, u, landed_value):
                pe.wait_ge(xg_landed[u], landed_value)
                for k in range(KD):
                    last = nc.tensor.transpose(ps[:, 5 + k // 4, (k % 4) * P:(k % 4) * P + CAP],
                                               xg[0:CAP, u, k * P:(k + 1) * P], ident[0:CAP, 0:CAP])
                last.then_inc(xg_turned, 1)

            def weights(piece, before):
                pe.wait_ge(slot_landed[piece % RING], before + 16 * (piece // RING + 1))

            def gate(n, u, piece, before):
                weights(piece, before)
                pe.wait_ge(xgT_act, n + 1)
                pe.wait_ge(xgT_dve, n + 1)
                for k in range(KD):
                    last = mm(ps[0:CAP, 0, :], xgT[:, u, k, 0:CAP], slot(piece)[:, k, :], start=(k == 0), stop=(k == KD - 1))
                last.then_inc(piece_done, 1)

            def up(n, u, piece, before):
                weights(piece, before)
                for k in range(KD):
                    last = mm(ps[0:CAP, 1, :], xgT[:, u, k, 0:CAP], slot(piece)[:, k, :], start=(k == 0), stop=(k == KD - 1))
                last.then_inc(piece_done, 1)

            def turn_act(n):
                pe.wait_ge(act_ready, n + 1)
                for k in range(KF):
                    last = nc.tensor.transpose(ps[:, 4, k * P:k * P + CAP], act_h[0:CAP, k * P:(k + 1) * P],
                                               ident[0:CAP, 0:CAP])
                last.then_inc(act_turned, 1)

            def down(n, u, piece, before, first=False):
                weights(piece, before)
                pe.wait_ge(actT_ready, n + 1)
                if not first:
                    pe.wait_ge(y_act, n)
                    pe.wait_ge(y_dve, n)
                for half in range(2):
                    for k in range(KF):
                        last = mm(ps[0:CAP, 2 + half, :], actT[:, u, k, 0:CAP],
                                  slot_down(piece)[:, k, half * 512:half * 512 + 512], start=(k == 0), stop=(k == KF - 1))
                    last.then_inc(piece_done if half else down_full, 1)

            def experts(l):
                n0, base = E * l, MOE_BASE[l]
                turn_xg(n0, 0, 16 * (n0 // 2 + 1))
                gate(n0, 0, base, 0)
                up(n0, 0, base + 1, 0)
                turn_xg(n0 + 1, 1, 16 * (n0 // 2 + 1))

                def step(e, n, u, piece, before, landed_next, first=False, last=False):
                    gate(n, u, piece, before)
                    turn_act(n - 1)
                    up(n, u, piece + 1, before)
                    down(n - 1, 1 - u, piece + 2, before, first)
                    if not last:
                        turn_xg(n + 1, 1 - u, landed_next)

                for e in (1, 2):
                    n = n0 + e
                    step(e, n, e % 2, base + 3 * e - 1, 0, 16 * ((n + 1) // 2 + 1), first=(l == 0 and e == 1))
                with pe.Fori(0, E // 2 - 2) as i:
                    for u in range(2):
                        step(i * 2 + (3 + u), i * 2 + (3 + u + n0), 1 - u, base + 8 + 3 * u, i * 16,
                             i * 16 + 16 * ((4 + u + n0) // 2 + 1))
                n = n0 + E - 1
                step(E - 1, n, 1, base + 3 * E - 4, 0, None, last=True)
                turn_act(n)
                down(n, 1, base + 3 * E - 1, 0)
                o = over[l]
                pe.wait_ge(flag_ready, l + 1)
                with pe.If(pe.value_load(overflow_flag[0:1, l:l + 1], min_val=0, max_val=1) > 0):
                    with pe.Fori(0, E * OVER) as it:
                        w8 = w_over.rearrange("p (k n) -> p k n", k=KD)
                        w4 = w_over.rearrange("p (k n) -> p k n", k=KF)
                        pe.wait_ge(o["sel"], it + 1)
                        for t in range(TT):
                            last = mm(ps[0:CAP, 0, 0:1], sel_over[:, t, 0:CAP], tok_id[:, t:t + 1],
                                      start=(t == 0), stop=(t == TT - 1))
                        last.then_inc(o["idx_full"], 1)
                        pe.wait_ge(o["xg"], it * 16 + 16)
                        for k in range(KD):
                            last = nc.tensor.transpose(ps[:, 1 + k // 4, (k % 4) * P:(k % 4) * P + CAP],
                                                       xg[0:CAP, 0, k * P:(k + 1) * P], ident[0:CAP, 0:CAP])
                        last.then_inc(o["turned"], 1)
                        pe.wait_ge(o["xgT"], it + 1)
                        for m in range(2):
                            pe.wait_ge(o["w"], it * 48 + 16 * (m + 1))
                            for k in range(KD):
                                last = mm(ps[0:CAP, 3 + m, :], xgT[:, 0, k, 0:CAP], w8[:, k, :],
                                          start=(k == 0), stop=(k == KD - 1))
                            last.then_inc(o["done"], 1)
                        pe.wait_ge(o["act"], it + 1)
                        for k in range(KF):
                            last = nc.tensor.transpose(ps[:, 5, k * P:k * P + CAP], act_h[0:CAP, k * P:(k + 1) * P],
                                                       ident[0:CAP, 0:CAP])
                        last.then_inc(o["act_turned"], 1)
                        pe.wait_ge(o["actT"], it + 1)
                        pe.wait_ge(o["w"], it * 48 + 48)
                        for half in range(2):
                            for k in range(KF):
                                last = mm(ps[0:CAP, 6 + half, :], actT[:, 0, k, 0:CAP], w4[:, k, half * 512:half * 512 + 512],
                                          start=(k == 0), stop=(k == KF - 1))
                        last.then_inc(o["done"], 1)

            project_out(0, 7, q_cat)
            norm(1)
            h_complete(1)
            route(0)
            experts(0)
            norm(2)
            h_complete(2)
            for j in range(24):
                if j >= 8:
                    kind, i = (j - 8) // 4 % 3, (j - 8) // 12 * 4 + (j - 8) % 4
                    pe.wait_ge((odd_cg, odd_z, odd_y)[kind], i + 1)
                landed(pe, ODD_BASE + j // 4)
                for k in range(KD):
                    last = mm(ps[:, j % 8, :], slot(ODD_BASE + j // 4)[:, k, (j % 4) * P:(j % 4 + 1) * P], hT[:, k, :],
                              start=(k == 0), stop=(k == KD - 1))
                last.then_inc(odd_full, 1)
                if j % 4 == 3:
                    pe.wait_ge(odd_full, j + 1)
                    release()
            pe.wait_ge(odd_y, 8)
            project_out(1, ODD_BASE + 6, yT)
            norm(3)
            h_complete(3)
            route(1)
            experts(1)


_INS = ["x", "rel_bias", "norm_mix", "norm_ffn", "norm_final", "w_in_even", "w_out_even", "m_igate_b", "m_fgate_b",
        "m_head_norm", "lam_q1", "lam_k1", "lam_q2", "lam_k2", "da_subln", "w_in_odd", "conv_w", "w_out_odd",
        "router_group_w", "router_group_b", "router_expert_w", "router_expert_b",
        "exp_w_gate", "exp_w_up", "exp_w_down"]


def kernel(**inputs):
    import concourse.bacc as bacc
    from concourse.bass_utils import run_bass_kernel_spmd

    nc = bacc.Bacc("TRN2", target_bir_lowering=False, num_devices=1)
    arrays, args = {}, {}
    named = [(name, np.ascontiguousarray(inputs[name])) for name in _INS] + [("bucket_table", bucket_table())]
    for name, a in named:
        arrays[f"in_{name}"] = a
        args[name] = nc.dram_tensor(f"in_{name}", a.shape, mybir.dt.from_np(a.dtype), kind="ExternalInput").ap()
    out = nc.dram_tensor("out", (1, T, D), F32, kind="ExternalOutput").ap()
    hybrid_trunk(nc, args, out)
    return run_bass_kernel_spmd(nc, [arrays], core_ids=[0]).results[0]["out"]
```

```python
from contextlib import ExitStack

import numpy as np

import concourse.bass as bass
from concourse import mybir

ALU = mybir.AluOpType
ACT = mybir.ActivationFunctionType
AX = mybir.AxisListType.X
F32 = mybir.dt.float32
F16 = mybir.dt.float16
BF16 = mybir.dt.bfloat16
I32 = mybir.dt.int32

P = 128
D = 1024
T = 512
TT = T // P
KD = D // P
HEADS = 4
EPS = 1e-6
BIG = 1e30
FF = 512
KF = FF // P
GROUPS, PER_GROUP = 4, 4
E = GROUPS * PER_GROUP
NR = GROUPS + E
CAP = 128
SMALL = 13 + 8 + 2
OVER = T // CAP - 1
LAM_INIT = 0.8 - 0.6
BUCKETS, MAX_DIST = 32, 128
VROW = 640

RING = 6
EVEN_PIECES, ODD_PIECES, EXPERT_PIECES = 9, 8, 3
MOE_BASE = [EVEN_PIECES, EVEN_PIECES + EXPERT_PIECES * E + ODD_PIECES]
ODD_BASE = EVEN_PIECES + EXPERT_PIECES * E


def bucket_table():
    n = 511 - np.arange(VROW)
    exact = BUCKETS // 2
    far = exact + (np.log(np.maximum(n, 1).astype(np.float32) / np.float32(exact)) / np.float32(np.log(MAX_DIST / exact))
                   * (BUCKETS - exact)).astype(np.int32)
    b = np.where(n < exact, n, np.minimum(far, BUCKETS - 1))
    b = np.where(n < 0, BUCKETS, b)
    return (np.arange(BUCKETS + 1)[:, None] == b[None, :]).astype(np.float32)


def hybrid_trunk(nc, A, out):
    ctx = ExitStack()
    with ctx:
        def sb(name, shape, dt=F32):
            return ctx.enter_context(nc.sbuf_tensor(name, shape, dt))

        def sem(name):
            return ctx.enter_context(nc.semaphore(name))

        x_sb = sb("x_sb", [P, TT, D])
        hT = sb("hT", [P, KD, T])
        ring = sb("ring", [P, RING, 4096])
        arena = sb("arena", [P, 17424])
        ident = sb("ident", [P, P])
        later = sb("later", [P, P], F16)
        ones16 = sb("ones16", [P, P], F16)
        slot_iota = sb("slot_iota", [P, P])
        tok_id = sb("tok_id", [P, TT], F16)
        iota16 = sb("iota16", [P, E])
        iota_slot0 = sb("iota_slot0", [P, E])
        gain = sb("gain", [P, D])
        w_route = sb("w_route", [P, 2, KD, NR])
        b_route = sb("b_route", [P, 2, NR])
        w_gates = sb("w_gates", [P, KD, 36])
        gate_b = sb("gate_b", [P, 1])
        conv_sb = sb("conv_sb", [P, KD, 3])
        head_norm = sb("head_norm", [P, HEADS])
        subln = sb("subln", [P, 1])
        lams = sb("lams", [P, 4, 64])
        minus_half = sb("minus_half", [P, TT])
        st = sb("st", [P, 88])
        overflow_flag = sb("overflow_flag", [P, 2], I32)

        def part(lo, *shape):
            n = int(np.prod(shape))
            v = arena[:, lo:lo + n]
            if len(shape) == 1:
                return v
            names = "abcd"[:len(shape)]
            return v.rearrange(f"p ({' '.join(names)}) -> p {' '.join(names)}", **dict(zip(names, shape)))

        q_cat = part(0, KD, T)
        dkT = part(4096, HEADS, T)
        bias_sb = part(6144, 2, T)
        dv = part(7168, TT, T)
        mkT = part(9216, HEADS, T)
        mv = part(11264, TT, HEADS, P + 1)
        moT = part(13328, HEADS, T)
        post = part(15376, 2, T)
        neg_m_row = part(16400, T)[0:HEADS, :]
        head_row = part(16912, HEADS, P)[0:HEADS]
        rel_w = part(4096, HEADS)
        table = part(4160, VROW)
        v_row = part(4864, VROW)
        gate_rows = part(11264, 8, T)
        xs = x_sb[:, :, :].rearrange("p t d -> p (t d)")
        e_maps = xs[:, 0:2048].rearrange("p (b m k) -> p b m k", b=2, m=2)
        a_map = xs[:, 2048:3072].rearrange("p (b k) -> p b k", b=2)
        aT = xs[:, 3072:4096].rearrange("p (b k) -> p b k", b=2)
        decay = xs[:, 0:4096].rearrange("p (b k) -> p b k", b=2)
        h_rows = part(11264, TT, D)
        junk = part(15360, D)
        cg_sb = part(0, KF, T)
        z_sb = part(2048, KF, T + 2)
        zc = part(4112, KF, T)
        yT = part(6160, KD, T)
        y_back = part(0, TT, 2, D)
        sel = arena[:, 0:4096].bitcast(F16).rearrange("p (t e c) -> p t e c", t=TT, e=E)
        w_over = part(0, 4096)
        xg = part(8192, 2, D)
        xgT = part(10240, 2, KD, P)
        sg = part(12288, FF)
        act_h = part(12800, FF)
        actT = part(13312, 2, KF, P)
        y_sb = part(14336, 2, D)
        rt = arena[:, 16384:17424]

        ps = ctx.enter_context(nc.psum_tensor("ps", [P, 8, 512], F32))

        h_dram = nc.dram_tensor("h_rows_dram", (T, D), F32, kind="Internal").ap()
        y_dram = nc.dram_tensor("y_rows_dram", (E * T, D), F32, kind="Internal").ap()
        v_dram = nc.dram_tensor("bias_rows_dram", (HEADS, P, VROW), F32, kind="Internal").ap()

        x_loaded, x_reloaded = [sem(f"x_loaded{t}") for t in range(TT)], sem("x_reloaded")
        x_ready = sem("x_ready")
        sumsq_ready, h_ready = sem("sumsq_ready"), sem("h_ready")
        tr_full = sem("tr_full")
        tr_act, tr_dve = sem("tr_act"), sem("tr_dve")
        h_stored = sem("h_stored")
        gain_loaded = sem("gain_loaded")
        small_loaded = sem("small_loaded")
        consts_ready, zeros_ready = sem("consts_ready"), sem("zeros_ready")
        slot_landed = [sem(f"slot_landed{i}") for i in range(RING)]
        piece_done = sem("piece_done")
        vbias_full, v_row_ready, v_stored = sem("vbias_full"), sem("v_row_ready"), sem("v_stored")
        bias_loaded = [sem("bias_loaded0"), sem("bias_loaded1")]
        gates_full, gate_cols_full = sem("gates_full"), sem("gate_cols_full")
        gate_act, gate_rows_ready, gate_cols_ready = sem("gate_act"), sem("gate_rows_ready"), sem("gate_cols_ready")
        job_full, job_act, job_dve = sem("job_full"), sem("job_act"), sem("job_dve")
        lam_sum, lam_exp, subln_ready = sem("lam_sum"), sem("lam_exp"), sem("subln_ready")
        o_unit = sem("o_unit")
        s_full, s_biased, s_max = sem("s_full"), sem("s_biased"), sem("s_max")
        e_ready, a_ready, a_turned, aT_ready = sem("e_ready"), sem("a_ready"), sem("a_turned"), sem("aT_ready")
        o_full, o_square, o_normed = sem("o_full"), sem("o_square"), sem("o_normed")
        on_turned, cat_ready = sem("on_turned"), sem("cat_ready")
        m_row_full, m_full = sem("m_row_full"), sem("m_full")
        m_arg, m_exp, m_masked = sem("m_arg"), sem("m_exp"), sem("m_masked")
        m_weighted, mo_full, m_centred, m_square = sem("m_weighted"), sem("mo_full"), sem("m_centred"), sem("m_square")
        norm_rstd, o_sums, o_rstd = sem("norm_rstd"), sem("o_sums"), sem("o_rstd")
        m_sums, m_rstd = sem("m_sums"), sem("m_rstd")
        m_normed, m_turned, m_cat = sem("m_normed"), sem("m_turned"), sem("m_cat")
        out_full, out_added = sem("out_full"), sem("out_added")
        odd_full, odd_cg, odd_z, odd_y = sem("odd_full"), sem("odd_cg"), sem("odd_z"), sem("odd_y")
        logits_full, route_arg, route_exp = sem("logits_full"), sem("route_arg"), sem("route_exp")
        picks_ready, rank_full, sel_ready, idx_full, idx_ready = (
            sem("picks_ready"), sem("rank_full"), sem("sel_ready"), sem("idx_full"), sem("idx_ready"))
        xg_landed = [sem("xg_landed0"), sem("xg_landed1")]
        xg_turned, xgT_act, xgT_dve = sem("xg_turned"), sem("xgT_act"), sem("xgT_dve")
        silu_ready, act_ready = sem("silu_ready"), sem("act_ready")
        act_turned, actT_ready, down_full = sem("act_turned"), sem("actT_ready"), sem("down_full")
        y_act, y_dve, y_stored = sem("y_act"), sem("y_dve"), [sem("y_stored0"), sem("y_stored1")]
        y_back_loaded = [sem(f"y_back_loaded{t}") for t in range(TT)]
        flag_ready = sem("flag_ready")
        out_stored = sem("out_stored")
        dve_step, act_step, pool_step = sem("dve_step"), sem("act_step"), sem("pool_step")
        over = [{n: sem(f"over_{n}{l}") for n in ("place", "sel", "idx_full", "idx", "xg", "turned", "xgT", "w",
                                                  "done", "silu", "act", "act_turned", "actT", "y", "stored", "gathers")} for l in range(2)]

        block = ctx.enter_context(nc.Block())

        w_even, w_odd = A["w_in_even"][0], A["w_in_odd"][0]
        dq0 = 4 * 512 + 2 * HEADS
        even_cols = [dq0, dq0 + 512, dq0 + 1024, 0, 512, 1024, 1536]
        odd_cols = [D, 2 * D, 0, D + 512, 2 * D + 512, 512]

        def cols(w, c, n=512):
            return w[:, c:c + n].rearrange("(k p) n -> p k n", p=P)

        def slot(piece):
            return ring[:, piece % RING, :].rearrange("p (k n) -> p k n", k=KD)

        def slot_down(piece):
            return ring[:, piece % RING, :].rearrange("p (k n) -> p k n", k=KF)

        def landed(eng, piece):
            eng.wait_ge(slot_landed[piece % RING], 16 * (piece // RING + 1))

        def expert_weights(l, e):
            e = min(e, E - 1) if isinstance(e, int) else e
            return [A[name][l, bass.ds(e, 1)].rearrange("a (k p) n -> p (a k) n", p=P)
                    for name in ("exp_w_gate", "exp_w_up", "exp_w_down")]

        def load_small(sp):
            small = [
                (rel_w[0:BUCKETS, :], A["rel_bias"]),
                (table[0:BUCKETS + 1, :], A["bucket_table"]),
                (lams[:, 0, :], A["lam_q1"][0].partition_broadcast(P)),
                (lams[:, 1, :], A["lam_k1"][0].partition_broadcast(P)),
                (lams[:, 2, :], A["lam_q2"][0].partition_broadcast(P)),
                (lams[:, 3, :], A["lam_k2"][0].partition_broadcast(P)),
                (gate_b[0:HEADS, :], A["m_igate_b"].rearrange("a h -> h a")),
                (gate_b[32:32 + HEADS, :], A["m_fgate_b"].rearrange("a h -> h a")),
                (head_norm[:, :], A["m_head_norm"][0].rearrange("(h p) -> p h", p=P)),
                (subln[:, :], A["da_subln"].rearrange("a p -> p a")),
            ]
            small += [(conv_sb[:, :, i], A["conv_w"][0, i].rearrange("(k p) -> p k", p=P)) for i in range(3)]
            for l in range(2):
                small += [
                    (w_route[:, l, :, 0:GROUPS], A["router_group_w"][l].rearrange("(k p) n -> p k n", p=P)),
                    (w_route[:, l, :, GROUPS:NR], A["router_expert_w"][l].rearrange("(k p) n -> p k n", p=P)),
                    (b_route[:, l, 0:GROUPS], A["router_group_b"][l].partition_broadcast(P)),
                    (b_route[:, l, GROUPS:NR], A["router_expert_b"][l].partition_broadcast(P)),
                ]
            small += [
                (w_gates[:, :, 0:HEADS], cols(w_even, 4 * 512, HEADS)),
                (w_gates[:, :, 32:32 + HEADS], cols(w_even, 4 * 512 + HEADS, HEADS)),
            ]
            assert len(small) == SMALL
            for k, (dst, src) in enumerate(small):
                if k == SMALL - 2:
                    sp.wait_ge(zeros_ready, 4)
                sp.dma_start(dst, src, allow_slow_non_contiguous=True).then_inc(small_loaded, 16)

        @block.sync
        def _(sp):
            def load(piece, src):
                if piece >= RING:
                    sp.wait_ge(piece_done, piece - RING + 1)
                dst = slot(piece) if src.shape[1] == KD else slot_down(piece)
                sp.dma_start(dst, src).then_inc(slot_landed[piece % RING], 16)

            def load_step(l, e, first, gate_up=True, down=True):
                e_up = expert_weights(l, e)[:2] if gate_up else ()
                e_down = expert_weights(l, e - 1)[2:] if down else ()
                for k, src in enumerate((*e_up, *e_down)):
                    piece = first[0] + k
                    sp.wait_ge(piece_done, first[1] + (piece - RING + 1))
                    sp.dma_start(slot(piece) if src.shape[1] == KD else slot_down(piece),
                                 src).then_inc(slot_landed[piece % RING], 16)

            def load_experts(l):
                base = MOE_BASE[l]
                load_step(l, 0, (base, 0), down=False)
                with sp.Fori(0, E // 2 - 1) as i:
                    for u in range(2):
                        load_step(l, i * 2 + (1 + u), (base + 2 + 3 * u, i * 6))
                load_step(l, E - 1, (base + 3 * E - 4, 0))
                load_step(l, E, (base + 3 * E - 1, 0), gate_up=False)

            def overflow(l):
                o = over[l]
                sp.wait_ge(flag_ready, l + 1)
                with sp.If(sp.value_load(overflow_flag[0:1, l:l + 1], min_val=0, max_val=1) > 0):
                    with sp.Fori(0, E) as e:
                        with sp.Fori(0, OVER) as j:
                            it = e * OVER + j
                            for k, src in enumerate(expert_weights(l, e)):
                                if k:
                                    sp.wait_ge(o["done"], it * 3 + k)
                                sp.dma_start(w_over.rearrange("p (k n) -> p k n", k=KD if k < 2 else KF),
                                             src).then_inc(o["w"], 16)
                            row = sp.snap(e * CAP + (j + 1) * (E * CAP))
                            sp.wait_ge(o["y"], it + 1)
                            sp.dma_start(y_dram[bass.ds(row, CAP), :],
                                         y_sb[0:CAP, 0, :]).then_inc(o["stored"], 16)
                    sp.wait_ge(o["stored"], 16 * E * OVER)

            for t in range(TT):
                sp.dma_start(x_sb[:, t, :], A["x"][0, t * P:(t + 1) * P, :]).then_inc(x_loaded[t], 16)
            load_small(sp)
            for k, c in enumerate(even_cols):
                load(k, cols(w_even, c))
            for half in range(2):
                load(7 + half, cols(A["w_out_even"][0], half * 512))
            load_experts(0)
            overflow(0)
            for k, c in enumerate(odd_cols):
                load(ODD_BASE + k, cols(w_odd, c))
            for half in range(2):
                load(ODD_BASE + 6 + half, cols(A["w_out_odd"][0], half * 512))
            load_experts(1)
            overflow(1)
            for t in range(TT):
                sp.wait_ge(h_ready, 4 * TT + t + 1)
                sp.dma_start(out[0, t * P:(t + 1) * P, :], h_rows[:, t, :]).then_inc(out_stored, 16)
            sp.wait_ge(out_stored, 16 * TT)

        rt = arena[:, 16384:17424]
        lg = rt[:, 0:80].rearrange("p (t n) -> p t n", t=TT)
        top_v = rt[:, 80:88].rearrange("p (k t) -> p k t", k=2)
        low = rt[:, 88:92]
        prob = rt[:, 92:104].rearrange("p (a t) -> p a t", a=3)
        g_cand, g_pick, g_exp, g_pen = (rt[:, 104 + 16 * i:120 + 16 * i].rearrange("p (t n) -> p t n", t=TT)
                                        for i in range(4))
        e_score = rt[:, 168:232].rearrange("p (t n) -> p t n", t=TT)
        picks = rt[:, 232:360].rearrange("p (k t n) -> p k t n", k=2, t=TT)
        wide = rt[:, 360:424].rearrange("p (t n) -> p t n", t=TT)
        top_w = rt[:, 424:432].rearrange("p (t k) -> p t k", t=TT)
        member = rt[:, 432:464].bitcast(F16).rearrange("p (t n) -> p t n", t=TT)
        place = rt[:, 464:528].rearrange("p (t n) -> p t n", t=TT)
        result_row = rt[:, 528:592].rearrange("p (t n) -> p t n", t=TT)
        row_f = rt[:, 592:600].rearrange("p (t k) -> p t k", t=TT)
        slot_tok = rt[:, 600:616].bitcast(I32)
        back_idx = rt[:, 616:624].bitcast(I32)
        over_place, over_tok = rt[:, 624:628], rt[:, 628:629].bitcast(I32)
        most = rt[:, 629:630]
        rank_sb = rt[:, 632:632 + (TT + 1) * E]
        sel_over = arena[:, 4096:4096 + 256].bitcast(F16).rearrange("p (t c) -> p t c", t=TT)

        EARLY, LATE = 12, 24
        IDX_BANK = (6, 7, 2, 3)
        UNITS = HEADS * TT

        def job_bank(j):
            return 6 + j % 2 if j < LATE else 7

        def qk_bank(j):
            return (ps[:, 0, :], ps[:, 1, 0:3 * P], ps[:, 2, 0:2 * P], ps[:, 1, 3 * P:T])[j]

        def act_job(j):
            return j % 2 == 0 or j >= EARLY

        def jobs_before(j, on_act):
            return sum(act_job(i) == on_act for i in range(j))

        @block.gpsimd
        def _(pool):
            g = nc.gpsimd

            def load_gain(n, src):
                if n:
                    pool.wait_ge(h_ready, n * TT)
                pool.dma_start(gain[:, :], src.partition_broadcast(P)).then_inc(gain_loaded, 16)

            load_gain(0, A["norm_mix"][0])
            g.memset(ident[:, :], 0.0).then_inc(zeros_ready, 1)
            g.memset(later[:, :], 0.0).then_inc(zeros_ready, 1)
            g.memset(head_row[:, :, :], 0.0).then_inc(zeros_ready, 1)
            g.memset(w_gates[:, :, :], 0.0).then_inc(zeros_ready, 1)
            g.memset(ones16[:, :], 1.0).then_inc(zeros_ready, 1)
            g.memset(minus_half[:, :], -0.5).then_inc(zeros_ready, 1)
            pool.wait_ge(zeros_ready, 6)
            g.affine_select(out=ident[:, :], in_=ident[:, :], compare_op=ALU.not_equal, fill=1.0, base=0,
                            pattern=[[-1, P]], channel_multiplier=1).then_inc(consts_ready, 1)
            g.affine_select(out=later[:, :], in_=later[:, :], compare_op=ALU.is_ge, fill=1.0, base=0,
                            pattern=[[-1, P]], channel_multiplier=1).then_inc(consts_ready, 1)
            g.affine_select(out=head_row[:, :, :], in_=head_row[:, :, :], compare_op=ALU.not_equal, fill=1.0, base=0,
                            pattern=[[-1, HEADS], [0, P]], channel_multiplier=1).then_inc(consts_ready, 1)
            g.iota(slot_iota[:, :], [[1, P]], base=0, channel_multiplier=0,
                   allow_small_or_imprecise_dtypes=True).then_inc(consts_ready, 1)
            g.iota(tok_id[:, :], [[P, TT]], base=0, channel_multiplier=1,
                   allow_small_or_imprecise_dtypes=True).then_inc(consts_ready, 1)
            g.iota(iota16[:, :], [[1, E]], base=0, channel_multiplier=0,
                   allow_small_or_imprecise_dtypes=True).then_inc(consts_ready, 1)
            g.iota(iota_slot0[:, :], [[CAP, E]], base=0, channel_multiplier=0,
                   allow_small_or_imprecise_dtypes=True).then_inc(consts_ready, 1)

            steps = [0]

            def rstd(dst, src, n, width, ready):
                g.tensor_scalar(dst, src, 1.0 / width, EPS, ALU.mult, ALU.add).then_inc(pool_step, 1)
                steps[0] += 1
                pool.wait_ge(pool_step, steps[0])
                g.tensor_tensor(dst, dst, minus_half[:, 0:n], ALU.pow).then_inc(ready, 1)

            def norm(n):
                for t in range(TT):
                    pool.wait_ge(sumsq_ready, n * TT + t + 1)
                    rstd(st[:, 4 + t:5 + t], st[:, t:t + 1], 1, D, norm_rstd)

            norm(0)
            load_gain(1, A["norm_ffn"][0])
            for h in range(HEADS):
                pool.wait_ge(o_sums, h + 1)
                rstd(st[:, 68:72], st[:, 64:68], TT, P, o_rstd)
            def mask(h):
                pool.wait_ge(m_exp, h + 1)
                w = decay[:, h % 2, :].rearrange("p (j k) -> p j k", j=TT)
                for j in range(TT):
                    last = g.affine_select(out=w[:, j, 0:P], in_=w[:, j, 0:P], compare_op=ALU.is_ge, fill=0.0, base=0,
                                           pattern=[[1, P]], channel_multiplier=-1)
                last.then_inc(m_masked, 1)

            mask(0)
            mask(1)
            for h in range(HEADS):
                pool.wait_ge(m_sums, h + 1)
                rstd(st[:, 84:88], st[:, 80:84], TT, P, m_rstd)
                if h + 2 < HEADS:
                    mask(h + 2)
            pool.wait_ge(mo_full, HEADS)
            pool.dma_start(x_sb[:, :, :], A["x"][0].rearrange("(t p) d -> p t d", p=P)).then_inc(x_reloaded, 16)

            for l in range(2):
                norm(2 * l + 1)
                for t in range(TT):
                    pool.wait_ge(h_ready, (2 * l + 1) * TT + t + 1)
                    pool.dma_start(h_dram[t * P:(t + 1) * P, :], h_rows[:, t, :]).then_inc(h_stored, 16)
                load_gain(2 * l + 2, A["norm_mix"][1] if l == 0 else A["norm_final"])
                pool.wait_ge(h_stored, 16 * TT * (l + 1))
                for e in range(E):
                    if e % 4 == 0:
                        pool.wait_ge(idx_ready, 4 * l + e // 4 + 1)
                    if e >= 2:
                        pool.wait_ge(xg_turned, E * l + e - 1)
                    g.indirect_dma_start(out=xg[0:CAP, e % 2, :], out_offset=None, in_=h_dram,
                                         in_offset=bass.IndirectOffsetOnAxis(ap=slot_tok[0:CAP, e:e + 1], axis=0)
                                         ).then_inc(xg_landed[e % 2], 16)
                o = over[l]
                pool.wait_ge(flag_ready, l + 1)

                def take_back(rows):
                    for u in range(2):
                        pool.wait_ge(y_stored[u], 16 * (E // 2) * (l + 1))
                    for t in range(TT):
                        for k in range(2):
                            c = 2 * t + k
                            g.indirect_dma_start(out=y_back[:, t, k, :], out_offset=None, in_=y_dram[0:rows, :],
                                                 in_offset=bass.IndirectOffsetOnAxis(ap=back_idx[:, c:c + 1], axis=0)
                                                 ).then_inc(y_back_loaded[t], 16)

                with pool.If(pool.value_load(overflow_flag[0:1, l:l + 1], min_val=0, max_val=1) > 0):
                    with pool.Fori(0, E * OVER) as it:
                        pool.wait_ge(o["idx"], it + 1)
                        pool.sem_inc(o["gathers"], 1)
                        g.indirect_dma_start(out=xg[0:CAP, 0, :], out_offset=None, in_=h_dram,
                                             in_offset=bass.IndirectOffsetOnAxis(ap=over_tok[0:CAP, :], axis=0)
                                             ).then_inc(o["xg"], 16)
                    pool.wait_ge(o["stored"], 16 * E * OVER)
                    take_back(E * T)
                with pool.Else():
                    take_back(E * CAP)
                norm(2 * l + 2)
                if l == 0:
                    load_gain(3, A["norm_ffn"][1])

        @block.scalar
        def _(act):
            s = nc.scalar

            def norm(n, copies=True):
                def copy(t):
                    act.wait_ge(tr_full, 2 * (n * TT + t) + 1)
                    s.copy(hT[:, 0:4, t * P:(t + 1) * P],
                           ps[:, 2 * (t % 2), :].rearrange("p (k c) -> p k c", k=4)).then_inc(tr_act, 1)

                for t in range(TT):
                    if n == 0:
                        act.wait_ge(x_loaded[t], 16)
                    else:
                        act.wait_ge(x_ready, (n - 1) * TT + t + 1)
                    if n or t:
                        act.wait_ge(sumsq_ready, n * TT + t)
                    s.activation(junk, x_sb[:, t, :], ACT.Square, accum_out=st[:, t:t + 1]).then_inc(sumsq_ready, 1)
                    if copies and t:
                        copy(t - 1)
                if copies:
                    copy(TT - 1)

            def job(j):
                kind, i = j // 4, j % 4
                src = ps[:, job_bank(j), :]
                act.wait_ge(job_full, j + 1)
                if kind == 0:
                    ins = s.copy(q_cat[:, HEADS + i, :], src)
                elif kind == 1:
                    ins = s.copy(dkT[:, i, :], src)
                elif kind == 2:
                    ins = s.copy(dv[:, i, :], src)
                elif kind == 3:
                    ins = s.copy(q_cat[:, i, :], src)
                elif kind == 4:
                    ins = s.activation(mkT[:, i, :], src, ACT.Copy, scale=float(P) ** -0.5)
                elif kind == 5:
                    ins = s.copy(mv[:, i, :, 0:P], src.rearrange("p (h c) -> p h c", h=HEADS))
                else:
                    ins = s.activation(moT[:, i, :], src, ACT.Exp, scale=-1.0)
                ins.then_inc(job_act, 1)

            norm(0)
            job(0)
            job(2)
            act.wait_ge(lam_sum, 2)
            s.activation(st[:, 10:12], st[:, 8:10], ACT.Exp).then_inc(lam_exp, 1)
            act.wait_ge(v_row_ready, 2)
            act.dma_start(v_dram, v_row[0:HEADS, :].unsqueeze(1).broadcast_to([HEADS, P, VROW])).then_inc(v_stored, 16)
            act.wait_ge(v_stored, 16)

            def load_bias(h):
                src = bass.AP(v_dram.tensor, h * P * VROW + P - 1, [[VROW - 1, P], [1, T]])
                act.dma_start(bias_sb[:, h % 2, :], src).then_inc(bias_loaded[h % 2], 16)

            load_bias(0)
            load_bias(1)
            act.wait_ge(gate_rows_ready, 1)
            s.activation(gate_rows[0:HEADS, 2, :], gate_rows[0:HEADS, 2, :], ACT.Exp, scale=-1.0).then_inc(act_step, 1)
            act.wait_ge(act_step, 1)
            s.activation(gate_rows[0:HEADS, 2, :], gate_rows[0:HEADS, 2, :], ACT.Ln, bias=1.0).then_inc(gate_act, 1)
            act.wait_ge(gate_rows_ready, 2)
            s.activation(gate_rows[0:HEADS, 7, :], gate_rows[0:HEADS, 7, :], ACT.Exp).then_inc(gate_act, 1)

            for j in range(4, EARLY, 2):
                job(j)

            def soft(u):
                n = (u % TT + 1) * P
                act.wait_ge(s_max, u + 1)
                for m in range(2):
                    c = 2 * (u % 2) + m
                    s.activation(e_maps[:, u % 2, m, 0:n], e_maps[:, u % 2, m, 0:n], ACT.Exp,
                                 bias=st[:, 16 + c:17 + c], accum_out=st[:, 20 + c:21 + c]).then_inc(e_ready, 1)

            def copy_aT(u):
                n = (u % TT + 1) * P
                act.wait_ge(a_turned, u + 1)
                if u >= 2:
                    act.wait_ge(o_unit, u - 1)
                s.copy(aT[:, u % 2, 0:n], ps[:, 4, 0:n]).then_inc(aT_ready, 1)

            def weights_exp(h):
                act.wait_ge(m_arg, h + 1)
                for j in range(TT):
                    w = decay[:, h % 2, j * T:j * T + T - j * P]
                    last = s.activation(w, w, ACT.Exp)
                last.then_inc(m_exp, 1)

            for step in range(UNITS + 4):
                if step < UNITS:
                    soft(step)
                    if EARLY + step < LATE:
                        job(EARLY + step)
                    if step % TT == TT - 1 and step // TT + 2 < HEADS:
                        act.wait_ge(s_biased, step + 1)
                        load_bias(step // TT + 2)
                if 1 <= step <= UNITS:
                    copy_aT(step - 1)
                if step >= 5 and (step - 5) % TT == 0:
                    h = (step - 5) // TT
                    act.wait_ge(o_full, h + 1)
                    if h >= 1:
                        act.wait_ge(o_normed, h)
                    s.activation(post[:, 0, :], ps[:, 5, :], ACT.Square).then_inc(o_square, 1)
                    if h == HEADS - 1:
                        weights_exp(0)
                if step == UNITS + 2:
                    job(LATE)
                if step >= 7 and (step - 7) % TT == 0:
                    h = (step - 7) // TT
                    act.wait_ge(on_turned, h + 1)
                    act.wait_ge(subln_ready, 1)
                    s.activation(q_cat[:, HEADS + h, :], ps[:, 4, :], ACT.Copy, scale=subln[:, 0:1]).then_inc(cat_ready, 1)

            weights_exp(1)
            for h in range(HEADS):
                act.wait_ge(m_centred, h + 1)
                s.activation(post[:, 1, :], post[:, 0, :], ACT.Square).then_inc(m_square, 1)
                if h + 2 < HEADS:
                    weights_exp(h + 2)
                if h + 1 < HEADS:
                    job(LATE + h + 1)

            def copy_xgT(n, u):
                act.wait_ge(xg_turned, n + 1)
                s.copy(xgT[:, u, 0:4, 0:CAP],
                       ps[:, 5, :].rearrange("p (k c) -> p k c", k=4)[:, :, 0:CAP]).then_inc(xgT_act, 1)

            def silu(n, gate_done, first=False):
                act.wait_ge(piece_done, gate_done)
                if not first:
                    act.wait_ge(act_ready, n)
                s.activation(sg[0:CAP, :], ps[0:CAP, 0, :], ACT.Silu).then_inc(silu_ready, 1)

            def copy_actT(n, u):
                act.wait_ge(act_turned, n + 1)
                s.copy(actT[:, u, :, 0:CAP],
                       ps[:, 4, :].rearrange("p (k c) -> p k c", k=KF)[:, :, 0:CAP]).then_inc(actT_ready, 1)

            def finish(l, e, n, u, stored_before):
                act.wait_ge(down_full, n + 1)
                if stored_before is not None:
                    act.wait_ge(y_stored[u], stored_before)
                s.copy(y_sb[0:CAP, u, 0:512], ps[0:CAP, 2, :]).then_inc(y_act, 1)
                act.wait_ge(y_act, n + 1)
                act.wait_ge(y_dve, n + 1)
                act.dma_start(y_dram[bass.ds(e * CAP, CAP), :], y_sb[0:CAP, u, :]).then_inc(y_stored[u], 16)

            def experts(l):
                act.wait_ge(route_arg, 2 * l + 1)
                s.activation(g_exp, g_exp, ACT.Exp).then_inc(route_exp, 1)
                act.wait_ge(route_arg, 2 * l + 2)
                s.activation(prob[:, 0, :], prob[:, 0, :], ACT.Exp).then_inc(route_exp, 1)
                n0 = E * l
                copy_xgT(n0, 0)
                base = MOE_BASE[l]
                silu(n0, base + 1, first=(l == 0))
                copy_xgT(n0 + 1, 1)
                for e in (1, 2):
                    n = n0 + e
                    silu(n, base + 3 * e)
                    copy_actT(n - 1, (e - 1) % 2)
                    copy_xgT(n + 1, (e + 1) % 2)
                    finish(l, e - 1, n - 1, (e - 1) % 2, 16 * ((n - 1) // 2) or None)
                with act.Fori(0, E // 2 - 2) as i:
                    for u in range(2):
                        silu(i * 2 + (3 + u + n0), i * 6 + (base + 3 * (3 + u)))
                        copy_actT(i * 2 + (2 + u + n0), u)
                        copy_xgT(i * 2 + (4 + u + n0), u)
                        finish(l, i * 2 + (2 + u), i * 2 + (2 + u + n0), u, i * 16 + 16 * (1 + n0 // 2))
                n = n0 + E - 1
                silu(n, base + 3 * (E - 1))
                copy_actT(n - 1, 0)
                finish(l, E - 2, n - 1, 0, 16 * ((n - 1) // 2))
                copy_actT(n, 1)
                finish(l, E - 1, n, 1, 16 * (n // 2))
                o = over[l]
                act.wait_ge(flag_ready, l + 1)
                with act.If(act.value_load(overflow_flag[0:1, l:l + 1], min_val=0, max_val=1) > 0):
                    with act.Fori(0, E * OVER) as it:
                        act.wait_ge(o["done"], it * 3 + 1)
                        s.activation(sg[0:CAP, :], ps[0:CAP, 3, :], ACT.Silu).then_inc(o["silu"], 1)

            norm(1)
            experts(0)
            norm(2)
            for half in range(2):
                for i in range(4):
                    j = half * 12 + i
                    act.wait_ge(odd_full, j + 1)
                    if half:
                        act.wait_ge(odd_z, i + 1)
                    s.copy(cg_sb[:, i, :], ps[:, j % 8, :]).then_inc(odd_cg, 1)
            norm(3)
            experts(1)
            norm(4, copies=False)

        @block.vector
        def _(dve):
            v = nc.vector
            done = [0]

            def link(ins):
                done[0] += 1
                ins.then_inc(dve_step, 1)
                dve.wait_ge(dve_step, done[0])

            def bc(ap, axis, *shape):
                return ap.unsqueeze(axis).broadcast_to(list(shape))

            def norm(n, finish_x=None, ahead=0, copies=True):
                def copy(t):
                    dve.wait_ge(tr_full, 2 * (n * TT + t) + 2)
                    v.tensor_copy(hT[:, 4:8, t * P:(t + 1) * P],
                                  ps[:, 2 * (t % 2) + 1, :].rearrange("p (k c) -> p k c", k=4)).then_inc(tr_dve, 1)

                if finish_x and ahead:
                    finish_x(0)
                for t in range(TT):
                    if finish_x and t + ahead < TT:
                        finish_x(t + ahead)
                    if t == 0:
                        dve.wait_ge(gain_loaded, 16 * (n + 1))
                    dve.wait_ge(norm_rstd, n * TT + t + 1)
                    ins = v.scalar_tensor_tensor(out=h_rows[:, t, :], in0=x_sb[:, t, :], scalar=st[:, 4 + t:5 + t],
                                                 in1=gain[:, :], op0=ALU.mult, op1=ALU.mult)
                    ins.then_inc(h_ready, 1)
                    if copies and t:
                        copy(t - 1)
                if copies:
                    copy(TT - 1)

            v.memset(rel_w[32:33, :], -BIG).then_inc(v_row_ready, 1)
            norm(0)

            def job(j):
                kind, i = j // 4, j % 4
                dst = (q_cat[:, HEADS + i, :], dkT[:, i, :], dv[:, i, :])[kind]
                dve.wait_ge(job_full, j + 1)
                if j == 5:
                    dve.wait_ge(v_stored, 16)
                v.tensor_copy(dst, ps[:, job_bank(j), :]).then_inc(job_dve, 1)

            job(1)
            job(3)
            for half in range(2):
                dve.wait_ge(vbias_full, half + 1)
                last = v.tensor_copy(v_row[0:HEADS, half * 320:half * 320 + 320], ps[0:HEADS, 4 + half, 0:320])
            last.then_inc(v_row_ready, 1)
            dve.wait_ge(small_loaded, 16 * SMALL)
            v.tensor_scalar(subln[:, :], subln[:, :], 1.0 - LAM_INIT, None, ALU.mult).then_inc(subln_ready, 1)
            for i in range(2):
                link(v.tensor_tensor(lams[:, 2 * i, :], lams[:, 2 * i, :], lams[:, 2 * i + 1, :], ALU.mult))
                v.tensor_reduce(st[:, 8 + i:9 + i], lams[:, 2 * i, :], AX, ALU.add).then_inc(lam_sum, 1)
            dve.wait_ge(lam_exp, 1)
            link(v.tensor_tensor(st[:, 12:13], st[:, 10:11], st[:, 11:12], ALU.subtract))
            link(v.tensor_scalar(st[:, 13:14], st[:, 12:13], LAM_INIT, None, ALU.add))
            lam = st[:, 13:14]

            dve.wait_ge(gates_full, 1)
            G = lambda k: gate_rows[0:HEADS, k, :]
            ig, f, soft_part, B, a_row, M, neg_mt, thr_row = (G(k) for k in range(8))
            v.tensor_scalar(ig, ps[0:HEADS, 0, :], gate_b[0:HEADS, 0:1], None, ALU.add)
            link(v.tensor_scalar(f, ps[32:32 + HEADS, 0, :], gate_b[32:32 + HEADS, 0:1], None, ALU.add))
            v.scalar_tensor_tensor(out=soft_part, in0=f, scalar=-1.0, in1=f,
                                   op0=ALU.mult, op1=ALU.max).then_inc(gate_rows_ready, 1)
            link(v.tensor_scalar(f, f, 0.0, None, ALU.min))
            dve.wait_ge(gate_act, 1)
            link(v.tensor_tensor(f, f, soft_part, ALU.subtract))
            link(v.memset(thr_row, 1.0))
            link(v.tensor_tensor_scan(B, thr_row, f, 0.0, ALU.mult, ALU.add))
            link(v.tensor_tensor(a_row, ig, B, ALU.subtract))
            link(v.tensor_tensor_scan(M, a_row, a_row, 0.0, ALU.max, ALU.max))
            link(v.tensor_scalar(neg_m_row[:, :], M, -1.0, None, ALU.mult))
            v.tensor_tensor(thr_row, neg_m_row[:, :], B, ALU.subtract).then_inc(gate_rows_ready, 1)

            for j in range(5, EARLY, 2):
                job(j)
            dve.wait_ge(gate_cols_full, 1)
            v.tensor_copy(st[:, 32:64], ps[:, 1, 0:32]).then_inc(gate_cols_ready, 1)
            a_col = st[:, 32:48].rearrange("p (j h) -> p j h", j=TT)
            thr_col = st[:, 48:64].rearrange("p (j h) -> p j h", j=TT)
            v.memset(mv[:, :, :, P:P + 1], 1.0)

            def biased(u):
                h, i = u // TT, u % TT
                n = (i + 1) * P
                dve.wait_ge(bias_loaded[h % 2], 16 * (h // 2 + 1))
                dve.wait_ge(s_full, u + 1)
                src = ps[:, 2 * (u % 2):2 * (u % 2) + 2, 0:n]
                v.scalar_tensor_tensor(out=e_maps[:, u % 2, :, 0:n], in0=src, scalar=64.0 ** -0.5,
                                       in1=bc(bias_sb[:, h % 2, T - n:T], 1, P, 2, n),
                                       op0=ALU.mult, op1=ALU.add).then_inc(s_biased, 1)
                dve.wait_ge(s_biased, u + 1)
                c = 16 + 2 * (u % 2)
                v.tensor_reduce(st[:, c:c + 2], e_maps[:, u % 2, :, 0:n], AX, ALU.max, negate=True).then_inc(s_max, 1)

            def combined(u):
                n = (u % TT + 1) * P
                b = u % 2
                dve.wait_ge(e_ready, 2 * (u + 1))
                if u:
                    dve.wait_ge(a_ready, u)
                link(v.reciprocal(st[:, 24:26], st[:, 20 + 2 * b:22 + 2 * b]))
                link(v.tensor_tensor(st[:, 26:27], st[:, 25:26], lam, ALU.mult))
                link(v.tensor_scalar(e_maps[:, b, 1, 0:n], e_maps[:, b, 1, 0:n], st[:, 26:27], None, ALU.mult))
                if u >= 2:
                    dve.wait_ge(a_turned, u - 1)
                v.scalar_tensor_tensor(out=a_map[:, b, 0:n], in0=e_maps[:, b, 0, 0:n], scalar=st[:, 24:25],
                                       in1=e_maps[:, b, 1, 0:n], op0=ALU.mult, op1=ALU.subtract).then_inc(a_ready, 1)

            def rows4(ap):
                return ap.rearrange("p (i c) -> p i c", i=TT)

            def weights_arg(h):
                dve.wait_ge(m_row_full, h + 1)
                if h >= 2:
                    dve.wait_ge(mo_full, h - 1)
                elif h == 0:
                    dve.wait_ge(a_ready, UNITS)
                else:
                    dve.wait_ge(o_unit, UNITS)
                for j in range(TT):
                    n = T - j * P
                    last = v.tensor_scalar(decay[:, h % 2, j * T:j * T + n], ps[:, 3, j * P:T], a_col[:, j, h:h + 1], 0.0,
                                           ALU.add, ALU.min)
                last.then_inc(m_arg, 1)

            def weigh(h):
                dve.wait_ge(m_full, h + 1)
                dve.wait_ge(m_masked, h + 1)
                for j in range(TT):
                    n = T - j * P
                    w = decay[:, h % 2, j * T:j * T + n]
                    last = v.tensor_tensor(w, qk_bank(j), w, ALU.mult)
                last.then_inc(m_weighted, 1)

            def head_out(h):
                dve.wait_ge(mo_full, h + 1)
                o4 = ps[:, 5:7, 0:2 * (P + 1)].rearrange("p b (i c) -> p b i c", i=2)
                den = st[:, 72:76].rearrange("p (b i) -> p b i", b=2)
                thr = thr_col[:, :, h].rearrange("p (b i) -> p b i", b=2)
                out4 = post[:, 0, :].rearrange("p (b i c) -> p b i c", b=2, i=2)
                link(v.scalar_tensor_tensor(out=den, in0=o4[:, :, :, P], scalar=-1.0, in1=thr, op0=ALU.mult, op1=ALU.max))
                link(v.tensor_tensor(den, o4[:, :, :, P], den, ALU.max))
                link(v.reciprocal(st[:, 72:76], st[:, 72:76]))
                link(v.tensor_tensor(out4, o4[:, :, :, 0:P], bc(den, 3, P, 2, 2, P), ALU.mult))
                link(v.tensor_reduce(st[:, 76:80], rows4(post[:, 0, :]), AX, ALU.add))
                link(v.tensor_scalar(st[:, 76:80], st[:, 76:80], 1.0 / P, None, ALU.mult))
                v.tensor_tensor(rows4(post[:, 0, :]), rows4(post[:, 0, :]), bc(st[:, 76:80], 2, P, TT, P),
                                ALU.subtract).then_inc(m_centred, 1)

            def head_norm_gate(h):
                dve.wait_ge(m_rstd, h + 1)
                v.tensor_tensor(rows4(post[:, 0, :]), rows4(post[:, 0, :]), bc(st[:, 84:88], 2, P, TT, P),
                                ALU.mult).then_inc(m_normed, 1)
                dve.wait_ge(job_act, jobs_before(LATE + h + 1, True))
                link(v.tensor_scalar(moT[:, h, :], moT[:, h, :], 1.0, None, ALU.add))
                link(v.reciprocal(moT[:, h, :], moT[:, h, :]))
                dve.wait_ge(m_turned, h + 1)
                v.scalar_tensor_tensor(out=q_cat[:, h, :], in0=ps[:, 4, :], scalar=head_norm[:, h:h + 1],
                                       in1=moT[:, h, :], op0=ALU.mult, op1=ALU.mult).then_inc(m_cat, 1)

            for step in range(UNITS + 4):
                if step < UNITS:
                    biased(step)
                if 1 <= step <= UNITS:
                    combined(step - 1)
                if step == UNITS + 1:
                    weights_arg(0)
                if step >= 5 and (step - 5) % TT == 0:
                    h = (step - 5) // TT
                    dve.wait_ge(o_square, h + 1)
                    v.tensor_reduce(st[:, 64:68], rows4(post[:, 0, :]), AX, ALU.add).then_inc(o_sums, 1)
                    dve.wait_ge(o_rstd, h + 1)
                    if h:
                        dve.wait_ge(on_turned, h)
                    v.tensor_tensor(rows4(post[:, 1, :]), rows4(ps[:, 5, :]), bc(st[:, 68:72], 2, P, TT, P),
                                    ALU.mult).then_inc(o_normed, 1)

            weights_arg(1)
            weigh(0)
            for h in range(HEADS):
                head_out(h)
                if h + 2 < HEADS:
                    weights_arg(h + 2)
                dve.wait_ge(m_square, h + 1)
                v.tensor_reduce(st[:, 80:84], rows4(post[:, 1, :]), AX, ALU.add).then_inc(m_sums, 1)
                if h + 1 < HEADS:
                    weigh(h + 1)
                head_norm_gate(h)

            def add_output(l, half, t):
                j = half * TT + t
                dve.wait_ge(out_full, 8 * l + j + 1)
                xt = x_sb[:, t, half * 512:half * 512 + 512]
                v.tensor_tensor(xt, ps[:, j, :], xt, ALU.add).then_inc(x_ready if half else out_added, 1)

            def mixer_norm(l):
                if l == 0:
                    dve.wait_ge(x_reloaded, 16)
                for t in range(TT):
                    add_output(l, 0, t)
                norm(2 * l + 1, lambda t: add_output(l, 1, t))

            def combine(l, t):
                dve.wait_ge(y_back_loaded[t], 32 * (l + 1))
                for k in range(2):
                    ins = v.scalar_tensor_tensor(out=x_sb[:, t, :], in0=y_back[:, t, k, :], scalar=top_w[:, t, k:k + 1],
                                                 in1=x_sb[:, t, :], op0=ALU.mult, op1=ALU.add)
                    if k == 0:
                        link(ins)
                ins.then_inc(x_ready, 1)

            def first_of(eq, n, dst):
                cand = wide if n == E else g_cand
                link(v.scalar_tensor_tensor(out=cand, in0=eq, scalar=-1000.0, in1=bc(iota16[:, 0:n], 1, P, TT, n),
                                            op0=ALU.mult, op1=ALU.add))
                link(v.tensor_reduce(low, cand, AX, ALU.min))
                link(v.tensor_tensor(dst, cand, bc(low, 2, P, TT, n), ALU.is_equal))

            def route(l):
                dve.wait_ge(consts_ready, 7)
                dve.wait_ge(logits_full, TT * (l + 1))
                link(v.tensor_tensor(lg, ps[:, 4, 0:TT * NR].rearrange("p (t n) -> p t n", t=TT),
                                     bc(b_route[:, l, :], 1, P, TT, NR), ALU.add))
                gl, el = lg[:, :, 0:GROUPS], lg[:, :, GROUPS:NR]
                link(v.tensor_reduce(top_v[:, 0, :], gl, AX, ALU.max))
                v.tensor_tensor(g_exp, gl, bc(top_v[:, 0, :], 2, P, TT, GROUPS), ALU.subtract).then_inc(route_arg, 1)
                link(v.tensor_tensor(g_cand, gl, bc(top_v[:, 0, :], 2, P, TT, GROUPS), ALU.is_equal))
                first_of(g_cand, GROUPS, g_pick)
                link(v.tensor_scalar(g_pen, g_pick, BIG, -BIG, ALU.mult, ALU.add))
                for t in range(TT):
                    s4 = e_score[:, t, :].rearrange("p (g j) -> p g j", g=GROUPS)
                    e4 = el[:, t, :].rearrange("p (g j) -> p g j", g=GROUPS)
                    link(v.tensor_tensor(s4, e4, bc(g_pick[:, t, :], 2, P, GROUPS, PER_GROUP), ALU.mult))
                    link(v.tensor_tensor(s4, s4, bc(g_pen[:, t, :], 2, P, GROUPS, PER_GROUP), ALU.add))
                for k in range(2):
                    link(v.tensor_reduce(top_v[:, k, :], e_score, AX, ALU.max))
                    link(v.tensor_tensor(wide, e_score, bc(top_v[:, k, :], 2, P, TT, E), ALU.is_equal))
                    first_of(wide, E, picks[:, k, :, :])
                    if k == 0:
                        link(v.scalar_tensor_tensor(out=e_score, in0=picks[:, 0, :, :], scalar=-2 * BIG, in1=e_score,
                                                    op0=ALU.mult, op1=ALU.add))
                v.tensor_tensor(prob[:, 0, :], top_v[:, 1, :], top_v[:, 0, :], ALU.subtract).then_inc(route_arg, 1)
                v.tensor_tensor(member, picks[:, 0, :, :], picks[:, 1, :, :], ALU.add).then_inc(picks_ready, 1)
                dve.wait_ge(route_exp, 2 * l + 1)
                link(v.tensor_reduce(prob[:, 1, :], g_exp, AX, ALU.add))
                dve.wait_ge(route_exp, 2 * l + 2)
                link(v.tensor_scalar(prob[:, 2, :], prob[:, 0, :], 1.0, None, ALU.add))
                link(v.tensor_tensor(prob[:, 1, :], prob[:, 1, :], prob[:, 2, :], ALU.mult))
                link(v.reciprocal(top_w[:, :, 0], prob[:, 1, :]))
                link(v.tensor_tensor(top_w[:, :, 1], top_w[:, :, 0], prob[:, 0, :], ALU.mult))
                dve.wait_ge(rank_full, l + 1)
                link(v.tensor_copy(rank_sb, ps[:, 5, 0:(TT + 1) * E]))
                rank = rank_sb[:, 0:TT * E].rearrange("p (t n) -> p t n", t=TT)
                link(v.tensor_tensor(place, rank, picks[:, 0, :, :], ALU.mult))
                link(v.tensor_tensor(wide, rank, picks[:, 1, :, :], ALU.mult))
                link(v.tensor_tensor(place, place, wide, ALU.add))
                link(v.tensor_tensor(wide, picks[:, 0, :, :], picks[:, 1, :, :], ALU.add))
                link(v.scalar_tensor_tensor(out=place, in0=wide, scalar=-1.0, in1=place, op0=ALU.add, op1=ALU.add))
                def slot_tokens(g):
                    dve.wait_ge(idx_full, 4 * l + g + 1)
                    v.tensor_copy(slot_tok[0:CAP, 4 * g:4 * g + 4], ps[0:CAP, IDX_BANK[g], 4 * g:4 * g + 4]).then_inc(idx_ready, 1)

                for g in range(4):
                    for t in range(TT):
                        ins = v.tensor_tensor(sel[:, t, 4 * g:4 * g + 4, 0:CAP], bc(place[:, t, 4 * g:4 * g + 4], 2, P, 4, CAP),
                                              bc(slot_iota[:, 0:CAP], 1, P, 4, CAP), ALU.is_equal)
                    ins.then_inc(sel_ready, 1)
                    if g:
                        slot_tokens(g - 1)
                slot_tokens(3)
                link(v.tensor_reduce(most, rank_sb[:, TT * E:(TT + 1) * E], AX, ALU.max))
                v.tensor_scalar(overflow_flag[:, l:l + 1], most, float(CAP), None, ALU.is_gt).then_inc(flag_ready, 1)
                link(v.tensor_tensor(result_row, rank, bc(iota_slot0[:, :], 1, P, TT, E), ALU.add))
                for j in range(1, OVER + 1):
                    link(v.tensor_scalar(wide, rank, float(j * CAP), float((E - 1) * CAP), ALU.is_ge, ALU.mult))
                    link(v.tensor_tensor(result_row, result_row, wide, ALU.add))
                for k in range(2):
                    link(v.tensor_tensor(wide, result_row, picks[:, k, :, :], ALU.mult))
                    link(v.tensor_reduce(row_f[:, :, k], wide, AX, ALU.add))
                link(v.tensor_copy(back_idx, rt[:, 592:600]))

            def copy_xgT(n, u):
                dve.wait_ge(xg_turned, n + 1)
                v.tensor_copy(xgT[:, u, 4:8, 0:CAP],
                              ps[:, 6, :].rearrange("p (k c) -> p k c", k=4)[:, :, 0:CAP]).then_inc(xgT_dve, 1)

            def hidden(n, up_done):
                dve.wait_ge(silu_ready, n + 1)
                dve.wait_ge(piece_done, up_done)
                v.tensor_tensor(act_h[0:CAP, :], sg[0:CAP, :], ps[0:CAP, 1, :], ALU.mult).then_inc(act_ready, 1)

            def finish(n, u, stored_before, down_done):
                dve.wait_ge(piece_done, down_done)
                if stored_before is not None:
                    dve.wait_ge(y_stored[u], stored_before)
                v.tensor_copy(y_sb[0:CAP, u, 512:1024], ps[0:CAP, 3, :]).then_inc(y_dve, 1)

            def experts(l):
                n0 = E * l
                copy_xgT(n0, 0)
                base = MOE_BASE[l]
                hidden(n0, base + 2)
                copy_xgT(n0 + 1, 1)
                for e in (1, 2):
                    n = n0 + e
                    hidden(n, base + 3 * e + 1)
                    copy_xgT(n + 1, (e + 1) % 2)
                    finish(n - 1, (e - 1) % 2, 16 * ((n - 1) // 2) or None, base + 3 * e + 2)
                with dve.Fori(0, E // 2 - 2) as i:
                    for u in range(2):
                        hidden(i * 2 + (3 + u + n0), i * 6 + (base + 3 * (3 + u) + 1))
                        copy_xgT(i * 2 + (4 + u + n0), u)
                        finish(i * 2 + (2 + u + n0), u, i * 16 + 16 * (1 + n0 // 2), i * 6 + (base + 3 * (3 + u) + 2))
                n = n0 + E - 1
                hidden(n, base + 3 * E - 2)
                finish(n - 1, 0, 16 * ((n - 1) // 2), base + 3 * E - 1)
                finish(n, 1, 16 * (n // 2), base + 3 * E)
                o = over[l]
                with dve.If(dve.value_load(overflow_flag[0:1, l:l + 1], min_val=0, max_val=1) > 0):
                    dve.wait_ge(y_stored[0], 8 * E * (l + 1))
                    with dve.Fori(0, E) as e:
                        with dve.Fori(0, OVER) as j:
                            it = e * OVER + j
                            v.tensor_scalar(over_place, place[:, :, bass.ds(e, 1)].rearrange("p t n -> p (t n)"),
                                            float(-CAP), None, ALU.add).then_inc(o["place"], 1)
                            dve.wait_ge(o["place"], it * 2 + 1)
                            for t in range(TT):
                                last = v.tensor_scalar(sel_over[:, t, 0:CAP], slot_iota[:, 0:CAP],
                                                       over_place[:, t:t + 1], None, ALU.is_equal)
                            last.then_inc(o["sel"], 1)
                            v.tensor_copy(place[:, :, bass.ds(e, 1)].rearrange("p t n -> p (t n)"),
                                          over_place).then_inc(o["place"], 1)
                            dve.wait_ge(o["place"], it * 2 + 2)
                            dve.wait_ge(o["idx_full"], it + 1)
                            v.tensor_copy(over_tok[0:CAP, :], ps[0:CAP, 0, 0:1]).then_inc(o["idx"], 1)
                            dve.wait_ge(o["turned"], it + 1)
                            v.tensor_copy(xgT[:, 0, :, 0:CAP],
                                          ps[:, 1:3, :].rearrange("p b (k c) -> p (b k) c", k=4)[:, :, 0:CAP]).then_inc(o["xgT"], 1)
                            dve.wait_ge(o["silu"], it + 1)
                            dve.wait_ge(o["done"], it * 3 + 2)
                            v.tensor_tensor(act_h[0:CAP, :], sg[0:CAP, :], ps[0:CAP, 4, :], ALU.mult).then_inc(o["act"], 1)
                            dve.wait_ge(o["act_turned"], it + 1)
                            v.tensor_copy(actT[:, 0, :, 0:CAP],
                                          ps[:, 5, :].rearrange("p (k c) -> p k c", k=KF)[:, :, 0:CAP]).then_inc(o["actT"], 1)
                            dve.wait_ge(o["done"], it * 3 + 3)
                            v.tensor_copy(y_sb[0:CAP, 0, :],
                                          ps[0:CAP, 6:8, :].rearrange("p b n -> p (b n)")).then_inc(o["y"], 1)
                            dve.wait_ge(o["stored"], it * 16 + 16)

            mixer_norm(0)
            route(0)
            experts(0)
            norm(2, lambda t: combine(0, t), ahead=1)
            link(v.memset(z_sb[:, :, 0:2], 0.0))
            for half in range(2):
                for i in range(4):
                    j = half * 12 + 4 + i
                    dve.wait_ge(odd_cg, 4 * half + i + 1)
                    dve.wait_ge(odd_full, j + 1)
                    v.tensor_tensor(z_sb[:, i, 2:T + 2], ps[:, j % 8, :], cg_sb[:, i, :], ALU.mult).then_inc(odd_z, 1)
                    dve.wait_ge(odd_z, 4 * half + i + 1)
                    w = conv_sb[:, 4 * half + i, :]
                    link(v.tensor_scalar(zc[:, i, :], z_sb[:, i, 0:T], w[:, 0:1], None, ALU.mult))
                    for tap in (1, 2):
                        link(v.scalar_tensor_tensor(out=zc[:, i, :], in0=z_sb[:, i, tap:tap + T], scalar=w[:, tap:tap + 1],
                                                    in1=zc[:, i, :], op0=ALU.mult, op1=ALU.add))
                for i in range(4):
                    j = half * 12 + 8 + i
                    dve.wait_ge(odd_full, j + 1)
                    v.tensor_tensor(yT[:, 4 * half + i, :], ps[:, j % 8, :], zc[:, i, :], ALU.mult).then_inc(odd_y, 1)
            mixer_norm(1)
            route(1)
            experts(1)
            norm(4, lambda t: combine(1, t), ahead=1, copies=False)

        @block.tensor
        def _(pe):
            mm = nc.tensor.matmul

            def turn_h(n, t):
                pe.wait_ge(h_ready, n * TT + t + 1)
                for b in range(2):
                    if t >= 2:
                        pe.wait_ge(tr_dve if b else tr_act, n * TT + t - 1)
                    for k in range(4):
                        c = 4 * b + k
                        last = nc.tensor.transpose(ps[:, 2 * (t % 2) + b, k * P:(k + 1) * P],
                                                   h_rows[:, t, c * P:(c + 1) * P], ident[:, :])
                    last.then_inc(tr_full, 1)

            def norm(n):
                for t in range(TT):
                    turn_h(n, t)

            def h_complete(n):
                pe.wait_ge(tr_act, (n + 1) * TT)
                pe.wait_ge(tr_dve, (n + 1) * TT)

            pe.wait_ge(consts_ready, 7)
            norm(0)
            h_complete(0)

            def job(j):
                kind, i = j // 4, j % 4
                landed(pe, kind)
                if j == LATE:
                    pe.wait_ge(job_act, jobs_before(LATE, True))
                elif j > LATE:
                    pe.wait_ge(job_act, jobs_before(j, True))
                elif j >= 2:
                    on_act = act_job(j - 2)
                    pe.wait_ge(job_act if on_act else job_dve, jobs_before(j - 1, on_act))
                for k in range(KD):
                    w, h = slot(kind)[:, k, :], hT[:, k, :]
                    if kind in (0, 1, 3, 4, 6):
                        last = mm(ps[:, job_bank(j), :], w[:, i * P:(i + 1) * P], h, start=(k == 0), stop=(k == KD - 1))
                    else:
                        last = mm(ps[:, job_bank(j), :], h[:, i * P:(i + 1) * P], w, start=(k == 0), stop=(k == KD - 1))
                last.then_inc(job_full, 1)
                if i == 3:
                    return True

            def release():
                pe.sem_inc(piece_done, 1)

            def all_jobs(js):
                for j in js:
                    if job(j):
                        pe.wait_ge(job_full, j + 1)
                        release()

            all_jobs(range(0, 4))
            pe.wait_ge(small_loaded, 16 * SMALL)
            pe.wait_ge(v_row_ready, 1)
            for half in range(2):
                mm(ps[0:HEADS, 4 + half, 0:320], rel_w[0:BUCKETS + 1, :],
                   table[0:BUCKETS + 1, half * 320:half * 320 + 320], start=True, stop=True).then_inc(vbias_full, 1)
            for k in range(KD):
                last = mm(ps[0:36, 0, :], w_gates[:, k, :], hT[:, k, :], start=(k == 0), stop=(k == KD - 1))
            last.then_inc(gates_full, 1)
            all_jobs(range(4, EARLY))
            pe.wait_ge(gate_act, 2)
            pe.wait_ge(gate_rows_ready, 2)
            for k, row in enumerate((4, 7)):
                for j in range(TT):
                    c = 16 * k + 4 * j
                    last = nc.tensor.transpose(ps[:, 1, c:c + HEADS], gate_rows[0:HEADS, row, j * P:(j + 1) * P],
                                               ident[0:HEADS, 0:HEADS])
            last.then_inc(gate_cols_full, 1)
            pe.wait_ge(gate_cols_ready, 1)
            pe.wait_ge(job_act, EARLY // 2)
            pe.wait_ge(job_dve, EARLY // 2)

            def scores(u):
                h, i = u // TT, u % TT
                n = (i + 1) * P
                if u >= 2:
                    pe.wait_ge(s_biased, u - 1)
                for m in range(2):
                    r = slice(64 * m, 64 * m + 64)
                    last = mm(ps[:, 2 * (u % 2) + m, 0:n], q_cat[r, HEADS + h, i * P:(i + 1) * P], dkT[r, h, 0:n],
                              start=True, stop=True)
                last.then_inc(s_full, 1)

            def turn_a(u):
                pe.wait_ge(a_ready, u + 1)
                if u:
                    pe.wait_ge(aT_ready, u)
                heads_turned = 0 if u < 7 else (u - 7) // TT + 1
                if u >= 7:
                    pe.wait_ge(cat_ready, heads_turned)
                for j in range(u % TT + 1):
                    last = nc.tensor.transpose(ps[:, 4, j * P:(j + 1) * P], a_map[:, u % 2, j * P:(j + 1) * P], ident[:, :])
                last.then_inc(a_turned, 1)

            def attend(u):
                h, i = u // TT, u % TT
                pe.wait_ge(aT_ready, u + 1)
                if i == 0 and h:
                    pe.wait_ge(o_normed, h)
                for j in range(i + 1):
                    last = mm(ps[:, 5, i * P:(i + 1) * P], aT[:, u % 2, j * P:(j + 1) * P], dv[:, j, h * P:(h + 1) * P],
                              start=(j == 0), stop=(j == i))
                last.then_inc(o_unit, 1)
                if i == TT - 1:
                    pe.wait_ge(o_unit, u + 1)
                    pe.sem_inc(o_full, 1)

            def turn_out(h):
                pe.wait_ge(o_normed, h + 1)
                pe.wait_ge(aT_ready, min(UNITS, 4 * h + 7))
                for i in range(TT):
                    last = nc.tensor.transpose(ps[:, 4, i * P:(i + 1) * P], post[:, 1, i * P:(i + 1) * P], ident[:, :])
                last.then_inc(on_turned, 1)

            def weights_row(h):
                if h:
                    pe.wait_ge(m_arg, h)
                else:
                    pe.wait_ge(s_biased, UNITS)
                mm(ps[:, 3, :], head_row[:, h, :], neg_m_row[:, :], start=True, stop=True).then_inc(m_row_full, 1)

            def queries_keys(h):
                for j in range(TT):
                    last = mm(qk_bank(j), mkT[:, h, j * P:(j + 1) * P], q_cat[:, h, j * P:T], start=True, stop=True)
                last.then_inc(m_full, 1)

            for step in range(UNITS + 4):
                if step < UNITS:
                    scores(step)
                    if EARLY + step < LATE:
                        all_jobs([EARLY + step])
                if 1 <= step <= UNITS:
                    turn_a(step - 1)
                if 2 <= step <= UNITS + 1:
                    attend(step - 2)
                if step == UNITS:
                    weights_row(0)
                    queries_keys(0)
                if step == UNITS + 2:
                    all_jobs([LATE])
                if step >= 7 and (step - 7) % TT == 0:
                    turn_out((step - 7) // TT)

            weights_row(1)
            pe.wait_ge(o_normed, HEADS)
            pe.wait_ge(cat_ready, HEADS)
            for h in range(HEADS):
                pe.wait_ge(m_weighted, h + 1)
                if h:
                    pe.wait_ge(m_centred, h)
                for i in range(TT):
                    for j in range(i + 1):
                        c = (i % 2) * (P + 1)
                        last = mm(ps[:, 5 + i // 2, c:c + P + 1],
                                  decay[:, h % 2, j * T + (i - j) * P:j * T + (i - j + 1) * P],
                                  mv[:, j, h, :], start=(j == 0), stop=(j == i))
                last.then_inc(mo_full, 1)
                if h + 1 < HEADS:
                    queries_keys(h + 1)
                if h + 2 < HEADS:
                    weights_row(h + 2)
                if h + 1 < HEADS:
                    all_jobs([LATE + h + 1])
                pe.wait_ge(m_normed, h + 1)
                if h:
                    pe.wait_ge(m_cat, h)
                for i in range(TT):
                    last = nc.tensor.transpose(ps[:, 4, i * P:(i + 1) * P], post[:, 0, i * P:(i + 1) * P], ident[:, :])
                last.then_inc(m_turned, 1)
            pe.wait_ge(m_cat, HEADS)

            def project_out(l, base, src):
                n = 2 * l + 1

                def project(half, t):
                    for k in range(KD):
                        last = mm(ps[:, half * TT + t, :], src[:, k, t * P:(t + 1) * P], slot(base + half)[:, k, :],
                                  start=(k == 0), stop=(k == KD - 1))
                    last.then_inc(out_full, 1)

                def logits(t):
                    pe.wait_ge(tr_act, n * TT + t + 1)
                    pe.wait_ge(tr_dve, n * TT + t + 1)
                    for k in range(KD):
                        last = mm(ps[:, 4, t * NR:(t + 1) * NR], hT[:, k, t * P:(t + 1) * P], w_route[:, l, k, :],
                                  start=(k == 0), stop=(k == KD - 1))
                    last.then_inc(logits_full, 1)

                landed(pe, base)
                for t in range(TT):
                    project(0, t)
                pe.wait_ge(out_full, 8 * l + 4)
                release()
                landed(pe, base + 1)
                project(1, 0)
                project(1, 1)
                turn_h(n, 0)
                project(1, 2)
                turn_h(n, 1)
                logits(0)
                project(1, 3)
                turn_h(n, 2)
                pe.wait_ge(out_full, 8 * l + 8)
                release()
                logits(1)
                turn_h(n, 3)
                logits(2)
                logits(3)

            def route(l):
                pe.wait_ge(picks_ready, l + 1)
                for t in range(TT):
                    for r in range(t + 1):
                        mm(ps[:, 5, t * E:(t + 1) * E], (later if r == t else ones16)[:, :], member[:, r, :],
                           start=(r == 0), stop=(r == t))
                for r in range(TT):
                    last = mm(ps[:, 5, TT * E:(TT + 1) * E], ones16[:, :], member[:, r, :], start=(r == 0), stop=(r == TT - 1))
                last.then_inc(rank_full, 1)
                for e in range(E):
                    if e % 4 == 0:
                        pe.wait_ge(sel_ready, 4 * l + e // 4 + 1)
                    for t in range(TT):
                        last = mm(ps[0:CAP, IDX_BANK[e // 4], e:e + 1], sel[:, t, e, 0:CAP], tok_id[:, t:t + 1],
                                  start=(t == 0), stop=(t == TT - 1))
                    if e % 4 == 3:
                        last.then_inc(idx_full, 1)
                pe.wait_ge(idx_ready, 4 * l + 4)

            def turn_xg(n, u, landed_value):
                pe.wait_ge(xg_landed[u], landed_value)
                for k in range(KD):
                    last = nc.tensor.transpose(ps[:, 5 + k // 4, (k % 4) * P:(k % 4) * P + CAP],
                                               xg[0:CAP, u, k * P:(k + 1) * P], ident[0:CAP, 0:CAP])
                last.then_inc(xg_turned, 1)

            def weights(piece, before):
                pe.wait_ge(slot_landed[piece % RING], before + 16 * (piece // RING + 1))

            def gate(n, u, piece, before):
                weights(piece, before)
                pe.wait_ge(xgT_act, n + 1)
                pe.wait_ge(xgT_dve, n + 1)
                for k in range(KD):
                    last = mm(ps[0:CAP, 0, :], xgT[:, u, k, 0:CAP], slot(piece)[:, k, :], start=(k == 0), stop=(k == KD - 1))
                last.then_inc(piece_done, 1)

            def up(n, u, piece, before):
                weights(piece, before)
                for k in range(KD):
                    last = mm(ps[0:CAP, 1, :], xgT[:, u, k, 0:CAP], slot(piece)[:, k, :], start=(k == 0), stop=(k == KD - 1))
                last.then_inc(piece_done, 1)

            def turn_act(n):
                pe.wait_ge(act_ready, n + 1)
                for k in range(KF):
                    last = nc.tensor.transpose(ps[:, 4, k * P:k * P + CAP], act_h[0:CAP, k * P:(k + 1) * P],
                                               ident[0:CAP, 0:CAP])
                last.then_inc(act_turned, 1)

            def down(n, u, piece, before, first=False):
                weights(piece, before)
                pe.wait_ge(actT_ready, n + 1)
                if not first:
                    pe.wait_ge(y_act, n)
                    pe.wait_ge(y_dve, n)
                for half in range(2):
                    for k in range(KF):
                        last = mm(ps[0:CAP, 2 + half, :], actT[:, u, k, 0:CAP],
                                  slot_down(piece)[:, k, half * 512:half * 512 + 512], start=(k == 0), stop=(k == KF - 1))
                    last.then_inc(piece_done if half else down_full, 1)

            def experts(l):
                n0, base = E * l, MOE_BASE[l]
                turn_xg(n0, 0, 16 * (n0 // 2 + 1))
                gate(n0, 0, base, 0)
                up(n0, 0, base + 1, 0)
                turn_xg(n0 + 1, 1, 16 * (n0 // 2 + 1))

                def step(e, n, u, piece, before, landed_next, first=False, last=False):
                    gate(n, u, piece, before)
                    turn_act(n - 1)
                    up(n, u, piece + 1, before)
                    if not last:
                        turn_xg(n + 1, 1 - u, landed_next)
                    down(n - 1, 1 - u, piece + 2, before, first)

                for e in (1, 2):
                    n = n0 + e
                    step(e, n, e % 2, base + 3 * e - 1, 0, 16 * ((n + 1) // 2 + 1), first=(l == 0 and e == 1))
                with pe.Fori(0, E // 2 - 2) as i:
                    for u in range(2):
                        step(i * 2 + (3 + u), i * 2 + (3 + u + n0), 1 - u, base + 8 + 3 * u, i * 16,
                             i * 16 + 16 * ((4 + u + n0) // 2 + 1))
                n = n0 + E - 1
                step(E - 1, n, 1, base + 3 * E - 4, 0, None, last=True)
                turn_act(n)
                down(n, 1, base + 3 * E - 1, 0)
                o = over[l]
                pe.wait_ge(flag_ready, l + 1)
                with pe.If(pe.value_load(overflow_flag[0:1, l:l + 1], min_val=0, max_val=1) > 0):
                    pe.wait_ge(y_act, n0 + E)
                    pe.wait_ge(y_dve, n0 + E)
                    with pe.Fori(0, E * OVER) as it:
                        w8 = w_over.rearrange("p (k n) -> p k n", k=KD)
                        w4 = w_over.rearrange("p (k n) -> p k n", k=KF)
                        pe.wait_ge(o["sel"], it + 1)
                        for t in range(TT):
                            last = mm(ps[0:CAP, 0, 0:1], sel_over[:, t, 0:CAP], tok_id[:, t:t + 1],
                                      start=(t == 0), stop=(t == TT - 1))
                        last.then_inc(o["idx_full"], 1)
                        pe.wait_ge(o["xg"], it * 16 + 16)
                        for k in range(KD):
                            last = nc.tensor.transpose(ps[:, 1 + k // 4, (k % 4) * P:(k % 4) * P + CAP],
                                                       xg[0:CAP, 0, k * P:(k + 1) * P], ident[0:CAP, 0:CAP])
                        last.then_inc(o["turned"], 1)
                        pe.wait_ge(o["xgT"], it + 1)
                        for m in range(2):
                            pe.wait_ge(o["w"], it * 48 + 16 * (m + 1))
                            for k in range(KD):
                                last = mm(ps[0:CAP, 3 + m, :], xgT[:, 0, k, 0:CAP], w8[:, k, :],
                                          start=(k == 0), stop=(k == KD - 1))
                            last.then_inc(o["done"], 1)
                        pe.wait_ge(o["act"], it + 1)
                        for k in range(KF):
                            last = nc.tensor.transpose(ps[:, 5, k * P:k * P + CAP], act_h[0:CAP, k * P:(k + 1) * P],
                                                       ident[0:CAP, 0:CAP])
                        last.then_inc(o["act_turned"], 1)
                        pe.wait_ge(o["actT"], it + 1)
                        pe.wait_ge(o["w"], it * 48 + 48)
                        for half in range(2):
                            for k in range(KF):
                                last = mm(ps[0:CAP, 6 + half, :], actT[:, 0, k, 0:CAP], w4[:, k, half * 512:half * 512 + 512],
                                          start=(k == 0), stop=(k == KF - 1))
                        last.then_inc(o["done"], 1)

            project_out(0, 7, q_cat)
            route(0)
            experts(0)
            norm(2)
            h_complete(2)
            for j in range(24):
                if j >= 8:
                    kind, i = (j - 8) // 4 % 3, (j - 8) // 12 * 4 + (j - 8) % 4
                    pe.wait_ge((odd_cg, odd_z, odd_y)[kind], i + 1)
                landed(pe, ODD_BASE + j // 4)
                for k in range(KD):
                    last = mm(ps[:, j % 8, :], slot(ODD_BASE + j // 4)[:, k, (j % 4) * P:(j % 4 + 1) * P], hT[:, k, :],
                              start=(k == 0), stop=(k == KD - 1))
                last.then_inc(odd_full, 1)
                if j % 4 == 3:
                    pe.wait_ge(odd_full, j + 1)
                    release()
            pe.wait_ge(odd_y, 8)
            project_out(1, ODD_BASE + 6, yT)
            route(1)
            experts(1)


_INS = ["x", "rel_bias", "norm_mix", "norm_ffn", "norm_final", "w_in_even", "w_out_even", "m_igate_b", "m_fgate_b",
        "m_head_norm", "lam_q1", "lam_k1", "lam_q2", "lam_k2", "da_subln", "w_in_odd", "conv_w", "w_out_odd",
        "router_group_w", "router_group_b", "router_expert_w", "router_expert_b",
        "exp_w_gate", "exp_w_up", "exp_w_down"]


def kernel(**inputs):
    import concourse.bacc as bacc
    from concourse.bass_utils import run_bass_kernel_spmd

    nc = bacc.Bacc("TRN2", target_bir_lowering=False, num_devices=1)
    arrays, args = {}, {}
    named = [(name, np.ascontiguousarray(inputs[name])) for name in _INS] + [("bucket_table", bucket_table())]
    for name, a in named:
        arrays[f"in_{name}"] = a
        args[name] = nc.dram_tensor(f"in_{name}", a.shape, mybir.dt.from_np(a.dtype), kind="ExternalInput").ap()
    out = nc.dram_tensor("out", (1, T, D), F32, kind="ExternalOutput").ap()
    hybrid_trunk(nc, args, out)
    return run_bass_kernel_spmd(nc, [arrays], core_ids=[0]).results[0]["out"]
```

```python
from contextlib import ExitStack

import numpy as np

import concourse.bass as bass
from concourse import mybir

ALU = mybir.AluOpType
ACT = mybir.ActivationFunctionType
AX = mybir.AxisListType.X
F32 = mybir.dt.float32
F16 = mybir.dt.float16
I32 = mybir.dt.int32
F32R = mybir.dt.float32r

P = 128
D = 1024
T = 512
TT = T // P
KD = D // P
HEADS = 4
EPS = 1e-6
BIG = 1e30
FF = 512
KF = FF // P
GROUPS, PER_GROUP = 4, 4
E = GROUPS * PER_GROUP
NR = GROUPS + E
CAP = 96
SMALL = 13 + 8 + 2
OVER = -(-T // CAP) - 1
LAM_INIT = 0.8 - 0.6
BUCKETS, MAX_DIST = 32, 128
VROW = 640

PIECE = 4
RING = 6
SPLIT_RING = 6
CHUNK = 1024
EVEN_PIECES, ODD_PIECES, EXPERT_PIECES = 9, 8, 3
MOE_BASE = [EVEN_PIECES, EVEN_PIECES + EXPERT_PIECES * E + ODD_PIECES]
ODD_BASE = EVEN_PIECES + EXPERT_PIECES * E
CHUNKS = PIECE * (EVEN_PIECES + ODD_PIECES + 2 * EXPERT_PIECES * E)


def bucket_table():
    n = 511 - np.arange(VROW)
    exact = BUCKETS // 2
    far = exact + (np.log(np.maximum(n, 1).astype(np.float32) / np.float32(exact)) / np.float32(np.log(MAX_DIST / exact))
                   * (BUCKETS - exact)).astype(np.int32)
    b = np.where(n < exact, n, np.minimum(far, BUCKETS - 1))
    b = np.where(n < 0, BUCKETS, b)
    return (np.arange(BUCKETS + 1)[:, None] == b[None, :]).astype(np.float32)


def hybrid_trunk(nc, A, out):
    ctx = ExitStack()
    with ctx:
        def sb(name, shape, dt=F32):
            return ctx.enter_context(nc.sbuf_tensor(name, shape, dt))

        def sem(name):
            return ctx.enter_context(nc.semaphore(name))

        x_sb = sb("x_sb", [P, TT, D])
        hT_flat = sb("hT", [P, 2 * KD * T], F32R)
        ring = sb("ring", [P, RING, 2 * CHUNK])
        w_split = sb("w_split", [P, SPLIT_RING, 2, CHUNK], F32R)
        arena = sb("arena", [P, 14352])
        ident = sb("ident", [P, P])
        later = sb("later", [P, P], F16)
        ones16 = sb("ones16", [P, P], F16)
        slot_iota = sb("slot_iota", [P, P])
        tok_id = sb("tok_id", [P, TT], F16)
        iota16 = sb("iota16", [P, E])
        iota_slot0 = sb("iota_slot0", [P, E])
        w_route = sb("w_route", [P, 2, KD, NR])
        b_route = sb("b_route", [P, 2, NR])
        w_gates = sb("w_gates", [P, KD, 36])
        w_gates_split = sb("w_gates_split", [P, 2, KD, 36], F32R)
        gate_b = sb("gate_b", [P, 1])
        conv_sb = sb("conv_sb", [P, KD, 3])
        head_norm = sb("head_norm", [P, HEADS])
        subln = sb("subln", [P, 1])
        minus_half = sb("minus_half", [P, TT])
        st = sb("st", [P, 88])
        overflow_flag = sb("overflow_flag", [P, 2], I32)

        def part(lo, *shape):
            n = int(np.prod(shape))
            v = arena[:, lo:lo + n]
            if len(shape) == 1:
                return v
            names = "abcd"[:len(shape)]
            return v.rearrange(f"p ({' '.join(names)}) -> p {' '.join(names)}", **dict(zip(names, shape)))

        hT = hT_flat[:, :].rearrange("p (s k n) -> p s k n", s=2, k=KD)
        xgT = hT_flat[:, 0:4096].rearrange("p (u s k c) -> p u s k c", u=2, s=2, k=KD)
        actT = hT_flat[:, 4096:6144].rearrange("p (u s k c) -> p u s k c", u=2, s=2, k=KF)
        q_cat = part(0, KD, T)
        dkT = part(4096, HEADS, T)
        moT = part(4096, HEADS, T)
        dv = part(6144, TT, T)
        head_row = part(8192, HEADS, P)[0:HEADS]
        neg_m_row = part(8704, T)[0:HEADS, :]
        bias_sb = part(9216, 2, T)
        mkT = part(10240, HEADS, T)
        mv = part(12288, TT, HEADS, P + 1)
        rel_w = part(4096, HEADS)
        table = part(4160, VROW)
        v_row = part(4864, VROW)
        lams = part(5504, 4, 64)
        gate_rows = part(10240, 8, T)
        xs = x_sb[:, :, :].rearrange("p t d -> p (t d)")
        e_maps = xs[:, 0:2048].rearrange("p (b m k) -> p b m k", b=2, m=2)
        a_map = e_maps[:, :, 0, :]
        aT = xs[:, 2048:3072].rearrange("p (b k) -> p b k", b=2)
        post = xs[:, 3072:4096].rearrange("p (b k) -> p b k", b=2)

        def decay(h, j, lo=0, hi=None):
            start = 1280 * (h % 2) + (0, 512, 896, 1152)[j]
            return xs[:, start + lo:start + (T - j * P if hi is None else hi)]

        h_rows = part(0, TT, D)
        hT_route = part(4096, KD, T)
        gain = part(9216, D)
        junk = part(10240, D)
        cg_sb = part(0, KF, T)
        z_sb = part(2048, KF, T + 2)
        yT = part(4104, KD, T)
        y_back = part(0, TT, 2, D)
        sel = arena[:, 4096:8192].bitcast(F16).rearrange("p (t e c) -> p t e c", t=TT, e=E)
        w_over = part(0, 4096)
        xgT_over = part(4096, KD, P)
        actT_over = part(5120, KF, P)
        sel_over = arena[:, 5632:5632 + 256].bitcast(F16).rearrange("p (t c) -> p t c", t=TT)
        xg = part(8192, 2, D)
        sg = part(10240, FF)
        act_h = part(10752, FF)
        y_sb = part(11264, 2, D)
        rt = arena[:, 13312:14352]

        ps = ctx.enter_context(nc.psum_tensor("ps", [P, 8, 512], F32))

        h_dram = nc.dram_tensor("h_rows_dram", (T, D), F32, kind="Internal").ap()
        y_dram = nc.dram_tensor("y_rows_dram", ((OVER + 1) * E * CAP, D), F32, kind="Internal").ap()
        v_dram = nc.dram_tensor("bias_rows_dram", (HEADS, P, VROW), F32, kind="Internal").ap()

        x_loaded, x_reloaded = [sem(f"x_loaded{t}") for t in range(TT)], sem("x_reloaded")
        x_ready = sem("x_ready")
        sumsq_ready, h_ready = sem("sumsq_ready"), sem("h_ready")
        tr_full = sem("tr_full")
        tr_act, tr_dve = sem("tr_act"), sem("tr_dve")
        h_stored = sem("h_stored")
        gain_loaded = sem("gain_loaded")
        small_loaded = sem("small_loaded")
        consts_ready, zeros_ready = sem("consts_ready"), sem("zeros_ready")
        slot_landed = [sem(f"slot_landed{i}") for i in range(RING)]
        hi_ready, lo_ready = sem("hi_ready"), sem("lo_ready")
        chunk_done = sem("chunk_done")
        gates_hi, gates_split = sem("gates_hi"), sem("gates_split")
        cat_hi, cat_split = sem("cat_hi"), sem("cat_split")
        vbias_full, v_row_ready, v_stored = sem("vbias_full"), sem("v_row_ready"), sem("v_stored")
        bias_loaded = [sem("bias_loaded0"), sem("bias_loaded1")]
        gates_full, gate_cols_full = sem("gates_full"), sem("gate_cols_full")
        gate_act, gate_rows_ready, gate_cols_ready = sem("gate_act"), sem("gate_rows_ready"), sem("gate_cols_ready")
        job_full, job_act, job_dve = sem("job_full"), sem("job_act"), sem("job_dve")
        lam_sum, lam_exp, subln_ready = sem("lam_sum"), sem("lam_exp"), sem("subln_ready")
        o_unit = sem("o_unit")
        s_full, s_biased, s_max = sem("s_full"), sem("s_biased"), sem("s_max")
        e_ready, a_ready, a_turned, aT_ready = sem("e_ready"), sem("a_ready"), sem("a_turned"), sem("aT_ready")
        o_full, o_square, o_normed = sem("o_full"), sem("o_square"), sem("o_normed")
        on_turned, cat_ready = sem("on_turned"), sem("cat_ready")
        m_row_full, m_full = sem("m_row_full"), sem("m_full")
        m_arg, m_exp, m_masked = sem("m_arg"), sem("m_exp"), sem("m_masked")
        m_weighted, mo_full, m_centred, m_square = sem("m_weighted"), sem("mo_full"), sem("m_centred"), sem("m_square")
        norm_rstd, o_sums, o_rstd = sem("norm_rstd"), sem("o_sums"), sem("o_rstd")
        m_sums, m_rstd = sem("m_sums"), sem("m_rstd")
        m_normed, m_turned, m_cat = sem("m_normed"), sem("m_turned"), sem("m_cat")
        out_full, out_added = sem("out_full"), sem("out_added")
        odd_full, odd_cg, odd_z, odd_y = sem("odd_full"), sem("odd_cg"), sem("odd_z"), sem("odd_y")
        logits_full, route_arg, route_exp = sem("logits_full"), sem("route_arg"), sem("route_exp")
        picks_ready, rank_full, sel_ready, idx_full, idx_ready = (
            sem("picks_ready"), sem("rank_full"), sem("sel_ready"), sem("idx_full"), sem("idx_ready"))
        xg_landed = [sem("xg_landed0"), sem("xg_landed1")]
        xg_turned, xgT_act, xgT_dve = sem("xg_turned"), sem("xgT_act"), sem("xgT_dve")
        silu_ready, act_ready = sem("silu_ready"), sem("act_ready")
        act_turned, actT_hi, actT_ready = sem("act_turned"), sem("actT_hi"), sem("actT_ready")
        y_act, y_dve, y_stored = sem("y_act"), sem("y_dve"), [sem("y_stored0"), sem("y_stored1")]
        y_back_loaded = [sem(f"y_back_loaded{t}") for t in range(TT)]
        flag_ready = sem("flag_ready")
        out_stored = sem("out_stored")
        dve_step, act_step, pool_step = sem("dve_step"), sem("act_step"), sem("pool_step")
        over = [{n: sem(f"over_{n}{l}") for n in ("place", "sel", "idx_full", "idx", "xg", "turned", "xgT", "w",
                                                  "done", "silu", "act", "act_turned", "actT", "y", "stored", "gathers")} for l in range(2)]

        block = ctx.enter_context(nc.Block())

        w_even, w_odd = A["w_in_even"][0], A["w_in_odd"][0]
        dq0 = 4 * 512 + 2 * HEADS
        even_cols = [dq0, dq0 + 512, dq0 + 1024, 0, 512, 1024, 1536]
        odd_cols = [D, 2 * D, 0, D + 512, 2 * D + 512, 512]

        def cols(w, c, n=512):
            return w[:, c:c + n].rearrange("(k p) n -> p k n", p=P)

        def raw(c):
            return ring[:, c // 2 % RING, c % 2 * CHUNK:(c % 2 + 1) * CHUNK]

        def plus(c, i, per_turn):
            return c if i is None else i * per_turn + c

        def expert_weights(l, e):
            e = min(e, E - 1) if isinstance(e, int) else e
            return [A[name][l, bass.ds(e, 1)].rearrange("a (k p) n -> p (a k) n", p=P)
                    for name in ("exp_w_gate", "exp_w_up", "exp_w_down")]

        def load_small(sp):
            small = [
                (rel_w[0:BUCKETS, :], A["rel_bias"]),
                (table[0:BUCKETS + 1, :], A["bucket_table"]),
                (lams[:, 0, :], A["lam_q1"][0].partition_broadcast(P)),
                (lams[:, 1, :], A["lam_k1"][0].partition_broadcast(P)),
                (lams[:, 2, :], A["lam_q2"][0].partition_broadcast(P)),
                (lams[:, 3, :], A["lam_k2"][0].partition_broadcast(P)),
                (gate_b[0:HEADS, :], A["m_igate_b"].rearrange("a h -> h a")),
                (gate_b[32:32 + HEADS, :], A["m_fgate_b"].rearrange("a h -> h a")),
                (head_norm[:, :], A["m_head_norm"][0].rearrange("(h p) -> p h", p=P)),
                (subln[:, :], A["da_subln"].rearrange("a p -> p a")),
            ]
            small += [(conv_sb[:, :, i], A["conv_w"][0, i].rearrange("(k p) -> p k", p=P)) for i in range(3)]
            for l in range(2):
                small += [
                    (w_route[:, l, :, 0:GROUPS], A["router_group_w"][l].rearrange("(k p) n -> p k n", p=P)),
                    (w_route[:, l, :, GROUPS:NR], A["router_expert_w"][l].rearrange("(k p) n -> p k n", p=P)),
                    (b_route[:, l, 0:GROUPS], A["router_group_b"][l].partition_broadcast(P)),
                    (b_route[:, l, GROUPS:NR], A["router_expert_b"][l].partition_broadcast(P)),
                ]
            small += [
                (w_gates[:, :, 0:HEADS], cols(w_even, 4 * 512, HEADS)),
                (w_gates[:, :, 32:32 + HEADS], cols(w_even, 4 * 512 + HEADS, HEADS)),
            ]
            assert len(small) == SMALL
            for k, (dst, src) in enumerate(small):
                if k == SMALL - 2:
                    sp.wait_ge(zeros_ready, 4)
                sp.dma_start(dst, src, allow_slow_non_contiguous=True).then_inc(small_loaded, 16)

        @block.sync
        def _(sp):
            def load(piece, src, i=None):
                rows = src.shape[1] // 2
                for half in range(2):
                    n = 2 * piece + half
                    if n >= RING:
                        sp.wait_ge(lo_ready, plus(2 * (n - RING) + 2, i, 24))
                    sp.dma_start(ring[:, n % RING, :].rearrange("p (k n) -> p k n", k=rows),
                                 src[:, half * rows:(half + 1) * rows, :]).then_inc(slot_landed[n % RING], 16)

            def load_step(l, e, first, i=None, gate_up=True, down=True):
                e_up = expert_weights(l, e)[:2] if gate_up else ()
                e_down = expert_weights(l, e - 1)[2:] if down else ()
                for k, src in enumerate((*e_up, *e_down)):
                    load(first + k, src, i)

            def load_experts(l):
                base = MOE_BASE[l]
                load_step(l, 0, base, down=False)
                with sp.Fori(0, E // 2 - 1) as i:
                    for u in range(2):
                        load_step(l, i * 2 + (1 + u), base + 2 + 3 * u, i)
                load_step(l, E - 1, base + 3 * E - 4)
                load_step(l, E, base + 3 * E - 1, gate_up=False)

            def overflow(l):
                o = over[l]
                sp.wait_ge(flag_ready, l + 1)
                with sp.If(sp.value_load(overflow_flag[0:1, l:l + 1], min_val=0, max_val=1) > 0):
                    with sp.Fori(0, E) as e:
                        with sp.Fori(0, OVER) as j:
                            it = e * OVER + j
                            for k, src in enumerate(expert_weights(l, e)):
                                if k:
                                    sp.wait_ge(o["done"], it * 3 + k)
                                sp.dma_start(w_over.rearrange("p (k n) -> p k n", k=KD if k < 2 else KF),
                                             src).then_inc(o["w"], 16)
                            row = sp.snap(e * CAP + (j + 1) * (E * CAP))
                            sp.wait_ge(o["y"], it + 1)
                            sp.dma_start(y_dram[bass.ds(row, CAP), :],
                                         y_sb[0:CAP, 0, :]).then_inc(o["stored"], 16)
                    sp.wait_ge(o["stored"], 16 * E * OVER)

            for t in range(TT):
                sp.dma_start(x_sb[:, t, :], A["x"][0, t * P:(t + 1) * P, :]).then_inc(x_loaded[t], 16)
            load_small(sp)
            for k, c in enumerate(even_cols):
                load(k, cols(w_even, c))
            for half in range(2):
                load(7 + half, cols(A["w_out_even"][0], half * 512))
            load_experts(0)
            for k, c in enumerate(odd_cols):
                if k == 1:
                    overflow(0)
                    sp.wait_ge(y_back_loaded[TT - 1], 32)
                load(ODD_BASE + k, cols(w_odd, c))
            for half in range(2):
                load(ODD_BASE + 6 + half, cols(A["w_out_odd"][0], half * 512))
            load_experts(1)
            overflow(1)
            for t in range(TT):
                sp.wait_ge(h_ready, 4 * TT + t + 1)
                sp.dma_start(out[0, t * P:(t + 1) * P, :], h_rows[:, t, :]).then_inc(out_stored, 16)
            sp.wait_ge(out_stored, 16 * TT)

        lg = rt[:, 0:80].rearrange("p (t n) -> p t n", t=TT)
        top_v = rt[:, 80:88].rearrange("p (k t) -> p k t", k=2)
        low = rt[:, 88:92]
        prob = rt[:, 92:104].rearrange("p (a t) -> p a t", a=3)
        g_cand, g_pick, g_exp, g_pen = (rt[:, 104 + 16 * i:120 + 16 * i].rearrange("p (t n) -> p t n", t=TT)
                                        for i in range(4))
        e_score = rt[:, 168:232].rearrange("p (t n) -> p t n", t=TT)
        picks = rt[:, 232:360].rearrange("p (k t n) -> p k t n", k=2, t=TT)
        wide = rt[:, 360:424].rearrange("p (t n) -> p t n", t=TT)
        top_w = rt[:, 424:432].rearrange("p (t k) -> p t k", t=TT)
        member = rt[:, 432:464].bitcast(F16).rearrange("p (t n) -> p t n", t=TT)
        place = rt[:, 464:528].rearrange("p (t n) -> p t n", t=TT)
        result_row = rt[:, 528:592].rearrange("p (t n) -> p t n", t=TT)
        row_f = rt[:, 592:600].rearrange("p (t k) -> p t k", t=TT)
        slot_tok = rt[:, 600:616].bitcast(I32)
        back_idx = rt[:, 616:624].bitcast(I32)
        over_place, over_tok = rt[:, 624:628], rt[:, 628:629].bitcast(I32)
        most = rt[:, 629:630]
        rank_sb = rt[:, 632:632 + (TT + 1) * E]

        EARLY, LATE = 12, 24
        IDX_BANK = (7, 4, 2, 3)
        UNITS = HEADS * TT

        def job_bank(j):
            return 6 + j % 2 if j < LATE else 7

        def qk_bank(j):
            return (ps[:, 0, :], ps[:, 1, 0:3 * P], ps[:, 2, 0:2 * P], ps[:, 1, 3 * P:T])[j]

        def act_job(j):
            return j % 2 == 0 or j >= EARLY

        def jobs_before(j, on_act):
            return sum(act_job(i) == on_act for i in range(j))

        def lo_of(c):
            return w_split[:, c % SPLIT_RING, 1, :]

        def hi_of(c):
            return w_split[:, c % SPLIT_RING, 0, :]

        def at_start(p):
            return PIECE * p + 6

        def at_last_job(p):
            return PIECE * p + 8

        def step_chunk(l, e):
            return PIECE * (MOE_BASE[l] + (3 * e - 1 if e else 0))

        @block.gpsimd
        def _(pool):
            g = nc.gpsimd

            def load_gain(n, src):
                if n:
                    pool.wait_ge(h_ready, n * TT)
                pool.dma_start(gain[:, :], src.partition_broadcast(P)).then_inc(gain_loaded, 16)

            load_gain(0, A["norm_mix"][0])
            g.memset(ident[:, :], 0.0).then_inc(zeros_ready, 1)
            g.memset(later[:, :], 0.0).then_inc(zeros_ready, 1)
            g.memset(head_row[:, :, :], 0.0).then_inc(zeros_ready, 1)
            g.memset(w_gates[:, :, :], 0.0).then_inc(zeros_ready, 1)
            g.memset(ones16[:, :], 1.0).then_inc(zeros_ready, 1)
            g.memset(minus_half[:, :], -0.5).then_inc(zeros_ready, 1)
            pool.wait_ge(zeros_ready, 6)
            g.affine_select(out=ident[:, :], in_=ident[:, :], compare_op=ALU.not_equal, fill=1.0, base=0,
                            pattern=[[-1, P]], channel_multiplier=1).then_inc(consts_ready, 1)
            g.affine_select(out=later[:, :], in_=later[:, :], compare_op=ALU.is_ge, fill=1.0, base=0,
                            pattern=[[-1, P]], channel_multiplier=1).then_inc(consts_ready, 1)
            g.affine_select(out=head_row[:, :, :], in_=head_row[:, :, :], compare_op=ALU.not_equal, fill=1.0, base=0,
                            pattern=[[-1, HEADS], [0, P]], channel_multiplier=1).then_inc(consts_ready, 1)
            g.iota(slot_iota[:, :], [[1, P]], base=0, channel_multiplier=0,
                   allow_small_or_imprecise_dtypes=True).then_inc(consts_ready, 1)
            g.iota(tok_id[:, :], [[P, TT]], base=0, channel_multiplier=1,
                   allow_small_or_imprecise_dtypes=True).then_inc(consts_ready, 1)
            g.iota(iota16[:, :], [[1, E]], base=0, channel_multiplier=0,
                   allow_small_or_imprecise_dtypes=True).then_inc(consts_ready, 1)
            g.iota(iota_slot0[:, :], [[CAP, E]], base=0, channel_multiplier=0,
                   allow_small_or_imprecise_dtypes=True).then_inc(consts_ready, 1)

            steps = [0]

            def rstd(dst, src, n, width, ready):
                g.tensor_scalar(dst, src, 1.0 / width, EPS, ALU.mult, ALU.add).then_inc(pool_step, 1)
                steps[0] += 1
                pool.wait_ge(pool_step, steps[0])
                g.tensor_tensor(dst, dst, minus_half[:, 0:n], ALU.pow).then_inc(ready, 1)

            def norm(n):
                for t in range(TT):
                    pool.wait_ge(sumsq_ready, n * TT + t + 1)
                    rstd(st[:, 4 + t:5 + t], st[:, t:t + 1], 1, D, norm_rstd)

            norm(0)
            for h in range(HEADS):
                pool.wait_ge(o_sums, h + 1)
                rstd(st[:, 68:72], st[:, 64:68], TT, P, o_rstd)
            pool.wait_ge(s_biased, UNITS)
            load_gain(1, A["norm_ffn"][0])
            def mask(h):
                pool.wait_ge(m_exp, h + 1)
                for j in range(TT):
                    last = g.affine_select(out=decay(h, j, 0, P), in_=decay(h, j, 0, P), compare_op=ALU.is_ge, fill=0.0, base=0,
                                           pattern=[[1, P]], channel_multiplier=-1)
                last.then_inc(m_masked, 1)

            mask(0)
            mask(1)
            for h in range(HEADS):
                pool.wait_ge(m_sums, h + 1)
                rstd(st[:, 84:88], st[:, 80:84], TT, P, m_rstd)
                if h + 2 < HEADS:
                    mask(h + 2)
            pool.wait_ge(m_turned, HEADS)
            pool.dma_start(x_sb[:, :, :], A["x"][0].rearrange("(t p) d -> p t d", p=P)).then_inc(x_reloaded, 16)

            for l in range(2):
                norm(2 * l + 1)
                for t in range(TT):
                    pool.wait_ge(h_ready, (2 * l + 1) * TT + t + 1)
                    pool.dma_start(h_dram[t * P:(t + 1) * P, :], h_rows[:, t, :]).then_inc(h_stored, 16)
                pool.wait_ge(h_stored, 16 * TT * (l + 1))
                for e in range(E):
                    if e % 4 == 0:
                        pool.wait_ge(idx_ready, 4 * l + e // 4 + 1)
                    if e >= 2:
                        pool.wait_ge(xg_turned, E * l + e - 1)
                    g.indirect_dma_start(out=xg[0:CAP, e % 2, :], out_offset=None, in_=h_dram,
                                         in_offset=bass.IndirectOffsetOnAxis(ap=slot_tok[0:CAP, e:e + 1], axis=0)
                                         ).then_inc(xg_landed[e % 2], 16)
                pool.wait_ge(xg_turned, E * (l + 1))
                load_gain(2 * l + 2, A["norm_mix"][1] if l == 0 else A["norm_final"])
                o = over[l]
                pool.wait_ge(flag_ready, l + 1)

                def take_back(rows):
                    for u in range(2):
                        pool.wait_ge(y_stored[u], 16 * (E // 2) * (l + 1))
                    for t in range(TT):
                        for k in range(2):
                            c = 2 * t + k
                            g.indirect_dma_start(out=y_back[:, t, k, :], out_offset=None, in_=y_dram[0:rows, :],
                                                 in_offset=bass.IndirectOffsetOnAxis(ap=back_idx[:, c:c + 1], axis=0)
                                                 ).then_inc(y_back_loaded[t], 16)

                with pool.If(pool.value_load(overflow_flag[0:1, l:l + 1], min_val=0, max_val=1) > 0):
                    with pool.Fori(0, E * OVER) as it:
                        pool.wait_ge(o["idx"], it + 1)
                        pool.sem_inc(o["gathers"], 1)
                        g.indirect_dma_start(out=xg[0:CAP, 0, :], out_offset=None, in_=h_dram,
                                             in_offset=bass.IndirectOffsetOnAxis(ap=over_tok[0:CAP, :], axis=0)
                                             ).then_inc(o["xg"], 16)
                    pool.wait_ge(o["stored"], 16 * E * OVER)
                    take_back((OVER + 1) * E * CAP)
                with pool.Else():
                    take_back(E * CAP)
                norm(2 * l + 2)
                if l == 0:
                    load_gain(3, A["norm_ffn"][1])

        @block.scalar
        def _(act):
            s = nc.scalar

            split = [0]

            def splits(upto, i=None):
                for c in range(split[0], min(upto, CHUNKS)):
                    n = c // 2
                    act.wait_ge(slot_landed[n % RING], plus(16 * (n // RING + 1), i, 32))
                    if c >= SPLIT_RING:
                        act.wait_ge(chunk_done, plus(c - SPLIT_RING + 1, i, 24))
                    s.copy(hi_of(c), raw(c)).then_inc(hi_ready, 1)
                    split[0] = c + 1

            def norm(n, copies=True, before_last=None):
                def copy(t):
                    act.wait_ge(tr_full, 2 * (n * TT + t) + 2)
                    b = 2 * (t % 2)
                    if n % 2 == 0:
                        ins = s.copy(hT[:, 0, :, t * P:(t + 1) * P], ps[:, b:b + 2, :].rearrange("p b (k c) -> p (b k) c", k=4))
                    else:
                        ins = s.copy(hT_route[:, 0:4, t * P:(t + 1) * P], ps[:, b, :].rearrange("p (k c) -> p k c", k=4))
                    ins.then_inc(tr_act, 1)

                for t in range(TT):
                    if t == TT - 1 and before_last:
                        before_last()
                    if n == 0:
                        act.wait_ge(x_loaded[t], 16)
                    else:
                        act.wait_ge(x_ready, (n - 1) * TT + t + 1)
                    if n or t:
                        act.wait_ge(sumsq_ready, n * TT + t)
                    s.activation(junk, x_sb[:, t, :], ACT.Square, accum_out=st[:, t:t + 1]).then_inc(sumsq_ready, 1)
                    if copies and t:
                        copy(t - 1)
                if copies:
                    copy(TT - 1)

            def job(j):
                kind, i = j // 4, j % 4
                src = ps[:, job_bank(j), :]
                act.wait_ge(job_full, j + 1)
                if kind == 0:
                    ins = s.copy(q_cat[:, HEADS + i, :], src)
                elif kind == 1:
                    ins = s.copy(dkT[:, i, :], src)
                elif kind == 2:
                    ins = s.copy(dv[:, i, :], src)
                elif kind == 3:
                    ins = s.copy(q_cat[:, i, :], src)
                elif kind == 4:
                    ins = s.activation(mkT[:, i, :], src, ACT.Copy, scale=float(P) ** -0.5)
                elif kind == 5:
                    ins = s.copy(mv[:, i, :, 0:P], src.rearrange("p (h c) -> p h c", h=HEADS))
                else:
                    s.activation(moT[:, i, :], src, ACT.Exp, scale=-1.0).then_inc(act_step, 1)
                    act.wait_ge(act_step, 2 * i + 2)
                    s.activation(moT[:, i, :], moT[:, i, :], ACT.Ln, bias=1.0).then_inc(act_step, 1)
                    act.wait_ge(act_step, 2 * i + 3)
                    ins = s.activation(moT[:, i, :], moT[:, i, :], ACT.Exp, scale=-1.0)
                ins.then_inc(job_act, 1)

            norm(0)
            splits(at_start(0))
            job(0)
            job(2)
            splits(at_last_job(0))
            act.wait_ge(small_loaded, 16 * SMALL)
            s.copy(w_gates_split[:, 0, :, :], w_gates[:, :, :]).then_inc(gates_hi, 1)
            splits(at_start(1))
            act.wait_ge(lam_sum, 2)
            s.activation(st[:, 10:12], st[:, 8:10], ACT.Exp).then_inc(lam_exp, 1)
            act.wait_ge(v_row_ready, 2)
            act.dma_start(v_dram, v_row[0:HEADS, :].unsqueeze(1).broadcast_to([HEADS, P, VROW])).then_inc(v_stored, 16)
            act.wait_ge(v_stored, 16)

            def load_bias(h):
                src = bass.AP(v_dram.tensor, h * P * VROW + P - 1, [[VROW - 1, P], [1, T]])
                act.dma_start(bias_sb[:, h % 2, :], src).then_inc(bias_loaded[h % 2], 16)

            load_bias(0)
            load_bias(1)
            act.wait_ge(gate_rows_ready, 1)
            s.activation(gate_rows[0:HEADS, 2, :], gate_rows[0:HEADS, 2, :], ACT.Exp, scale=-1.0).then_inc(act_step, 1)
            act.wait_ge(act_step, 1)
            s.activation(gate_rows[0:HEADS, 2, :], gate_rows[0:HEADS, 2, :], ACT.Ln, bias=1.0).then_inc(gate_act, 1)
            act.wait_ge(gate_rows_ready, 2)
            s.activation(gate_rows[0:HEADS, 7, :], gate_rows[0:HEADS, 7, :], ACT.Exp).then_inc(gate_act, 1)

            for j in range(4, EARLY, 2):
                job(j)
                if j % 4 == 2:
                    splits(at_last_job(j // 4))
                    splits(at_start(j // 4 + 1))

            def soft(u):
                n = (u % TT + 1) * P
                act.wait_ge(s_max, u + 1)
                for m in range(2):
                    c = 2 * (u % 2) + m
                    s.activation(e_maps[:, u % 2, m, 0:n], e_maps[:, u % 2, m, 0:n], ACT.Exp,
                                 bias=st[:, 16 + c:17 + c], accum_out=st[:, 20 + c:21 + c]).then_inc(e_ready, 1)

            def copy_aT(u):
                n = (u % TT + 1) * P
                act.wait_ge(a_turned, u + 1)
                if u >= 2:
                    act.wait_ge(o_unit, u - 1)
                s.copy(aT[:, u % 2, 0:n], ps[:, 4, 0:n]).then_inc(aT_ready, 1)

            def cat(k, l=0):
                s.copy(hT[:, 0, k, :], (yT if l else q_cat)[:, k, :]).then_inc(cat_hi, 1)

            def weights_exp(h):
                act.wait_ge(m_arg, h + 1)
                w = xs[:, 1280 * (h % 2):1280 * (h % 2 + 1)]
                s.activation(w, w, ACT.Exp).then_inc(m_exp, 1)

            for step in range(UNITS + 4):
                if step < UNITS:
                    soft(step)
                    j = EARLY + step
                    if j < LATE:
                        if j % 4 == 3:
                            splits(at_last_job(j // 4))
                        job(j)
                        if j % 4 == 3:
                            splits(at_start(j // 4 + 1))
                    if step % TT == TT - 1 and step // TT + 2 < HEADS:
                        act.wait_ge(s_biased, step + 1)
                        load_bias(step // TT + 2)
                if 1 <= step <= UNITS:
                    copy_aT(step - 1)
                if step >= 5 and (step - 5) % TT == 0:
                    h = (step - 5) // TT
                    act.wait_ge(o_full, h + 1)
                    if h >= 1:
                        act.wait_ge(o_normed, h)
                    s.activation(post[:, 0, :], ps[:, 5, :], ACT.Square).then_inc(o_square, 1)
                    if h == HEADS - 1:
                        weights_exp(0)
                if step == UNITS + 2:
                    job(LATE)
                if step >= 7 and (step - 7) % TT == 0:
                    h = (step - 7) // TT
                    act.wait_ge(on_turned, h + 1)
                    act.wait_ge(subln_ready, 1)
                    s.activation(q_cat[:, HEADS + h, :], ps[:, 4, :], ACT.Copy, scale=subln[:, 0:1]).then_inc(cat_ready, 1)

            weights_exp(1)
            for h in range(HEADS):
                act.wait_ge(m_centred, h + 1)
                s.activation(post[:, 1, :], post[:, 0, :], ACT.Square).then_inc(m_square, 1)
                if h + 2 < HEADS:
                    weights_exp(h + 2)
                if h + 2 == HEADS:
                    splits(at_last_job(6))
                if h + 1 < HEADS:
                    job(LATE + h + 1)
                if h + 2 == HEADS:
                    act.wait_ge(cat_ready, HEADS)
                    for k in range(HEADS, KD):
                        cat(k)
                    splits(at_start(7))
                    for k in range(h):
                        act.wait_ge(m_cat, k + 1)
                        cat(k)
            for k in range(HEADS - 2, HEADS):
                act.wait_ge(m_cat, k + 1)
                cat(k)
            splits(at_last_job(7))
            splits(at_start(8))

            def copy_xgT(n, u):
                act.wait_ge(xg_turned, n + 1)
                s.copy(xgT[:, u, 0, :, 0:CAP],
                       ps[:, 5:7, :].rearrange("p b (k c) -> p (b k) c", k=4)[:, :, 0:CAP]).then_inc(xgT_act, 1)

            def silu(n, gate_done, first=False):
                act.wait_ge(chunk_done, gate_done)
                if not first:
                    act.wait_ge(act_ready, n)
                s.activation(sg[0:CAP, :], ps[0:CAP, 0, :], ACT.Silu).then_inc(silu_ready, 1)

            def copy_actT(n, u):
                act.wait_ge(act_turned, n + 1)
                s.copy(actT[:, u, 0, :, 0:CAP],
                       ps[:, 4, :].rearrange("p (k c) -> p k c", k=KF)[:, :, 0:CAP]).then_inc(actT_hi, 1)

            def copy_y(u, down_done, stored_before):
                act.wait_ge(chunk_done, down_done)
                if stored_before is not None:
                    act.wait_ge(y_stored[u], stored_before)
                s.copy(y_sb[0:CAP, u, 0:512], ps[0:CAP, 2, :]).then_inc(y_act, 1)

            def store_y(e, n, u):
                act.wait_ge(y_act, n + 1)
                act.wait_ge(y_dve, n + 1)
                act.dma_start(y_dram[bass.ds(e * CAP, CAP), :], y_sb[0:CAP, u, :]).then_inc(y_stored[u], 16)

            def experts(l):
                act.wait_ge(route_arg, 2 * l + 1)
                s.activation(g_exp, g_exp, ACT.Exp).then_inc(route_exp, 1)
                act.wait_ge(route_arg, 2 * l + 2)
                s.activation(prob[:, 0, :], prob[:, 0, :], ACT.Exp).then_inc(route_exp, 1)
                n0 = E * l
                c0 = step_chunk(l, 0)
                copy_xgT(n0, 0)
                splits(c0 + 10)
                silu(n0, c0 + 4, first=(l == 0))
                copy_xgT(n0 + 1, 1)
                splits(c0 + 14)

                def step(e, n, u, c, i, y_stored_before, with_y=True):
                    if with_y:
                        copy_y(u, plus(c, i, 24), y_stored_before)
                    splits(c + 8, i)
                    if with_y:
                        store_y(e - 2, n - 2, u)
                    splits(c + 10, i)
                    silu(n, plus(c + 4, i, 24))
                    copy_actT(n - 1, 1 - u)
                    splits(c + 14, i)
                    if not (isinstance(e, int) and e == E - 1):
                        copy_xgT(n + 1, 1 - u)
                    splits(c + 18, i)

                step(1, n0 + 1, 1, step_chunk(l, 1), None, None, with_y=False)
                for e in (2, 3, 4):
                    step(e, n0 + e, e % 2, step_chunk(l, e), None, 16 * ((n0 + e - 2) // 2) or None)
                c = step_chunk(l, 5)
                with act.Fori(0, E // 2 - 3) as i:
                    for u in range(2):
                        step(i * 2 + (5 + u), i * 2 + (5 + u + n0), 1 - u, c + 12 * u, i,
                             i * 16 + 16 * ((n0 + 3 + u) // 2))
                split[0] += 24 * (E // 2 - 4)
                step(E - 1, n0 + E - 1, 1, step_chunk(l, E - 1), None, 16 * ((n0 + E - 3) // 2))
                c = step_chunk(l, E)
                copy_y(0, c, 16 * ((n0 + E - 2) // 2))
                store_y(E - 2, n0 + E - 2, 0)
                copy_actT(n0 + E - 1, 1)
                copy_y(1, c + 4, 16 * ((n0 + E - 1) // 2))
                store_y(E - 1, n0 + E - 1, 1)
                o = over[l]
                act.wait_ge(flag_ready, l + 1)
                with act.If(act.value_load(overflow_flag[0:1, l:l + 1], min_val=0, max_val=1) > 0):
                    with act.Fori(0, E * OVER) as it:
                        act.wait_ge(o["done"], it * 3 + 1)
                        s.activation(sg[0:CAP, :], ps[0:CAP, 3, :], ACT.Silu).then_inc(o["silu"], 1)

            norm(1, before_last=lambda: splits(at_last_job(8)))
            splits(at_start(9))
            experts(0)
            splits(PIECE * (ODD_BASE + 1))
            norm(2)
            splits(at_start(ODD_BASE))
            for p in range(ODD_BASE, ODD_BASE + 6):
                half, kind = divmod(p - ODD_BASE, 3)
                for i in range(4 if kind == 0 else 0):
                    j = half * 12 + i
                    if i == 3:
                        splits(at_last_job(p))
                    act.wait_ge(odd_full, j + 1)
                    if half:
                        act.wait_ge(odd_z, i + 1)
                    s.copy(cg_sb[:, i, :], ps[:, j % 8, :]).then_inc(odd_cg, 1)
                splits(at_last_job(p))
                if p < ODD_BASE + 5:
                    splits(at_start(p + 1))
            act.wait_ge(odd_full, 24)
            for k in range(KD):
                act.wait_ge(odd_y, k + 1)
                cat(k, 1)
            p = ODD_BASE + 6
            splits(at_start(p))
            splits(at_last_job(p))
            splits(at_start(p + 1))
            norm(3, before_last=lambda: splits(at_last_job(p + 1)))
            splits(at_start(p + 2))
            experts(1)
            norm(4, copies=False)

        @block.vector
        def _(dve):
            v = nc.vector
            done = [0]

            def link(ins):
                done[0] += 1
                ins.then_inc(dve_step, 1)
                dve.wait_ge(dve_step, done[0])

            def bc(ap, axis, *shape):
                return ap.unsqueeze(axis).broadcast_to(list(shape))

            split = [0]

            def splits(upto, i=None):
                for c in range(split[0], min(upto, CHUNKS)):
                    dve.wait_ge(hi_ready, plus(c + 1, i, 24))
                    v.tensor_tensor(lo_of(c), raw(c), hi_of(c).bitcast(F32), ALU.subtract).then_inc(lo_ready, 1)
                    split[0] = c + 1

            def cat(k, n, l=0):
                dve.wait_ge(cat_hi, KD * l + n + 1)
                v.tensor_tensor(hT[:, 1, k, :], (yT if l else q_cat)[:, k, :], hT[:, 0, k, :].bitcast(F32),
                                ALU.subtract).then_inc(cat_split, 1)

            def norm(n, finish_x=None, ahead=0, copies=True):
                def copy(t):
                    b, cs = 2 * (t % 2), slice(t * P, (t + 1) * P)
                    if n % 2 == 0:
                        dve.wait_ge(tr_act, n * TT + t + 1)
                        ins = v.tensor_tensor(hT[:, 1, :, cs], ps[:, b:b + 2, :].rearrange("p b (k c) -> p (b k) c", k=4),
                                              hT[:, 0, :, cs].bitcast(F32), ALU.subtract)
                    else:
                        dve.wait_ge(tr_full, 2 * (n * TT + t) + 2)
                        ins = v.tensor_copy(hT_route[:, 4:8, cs], ps[:, b + 1, :].rearrange("p (k c) -> p k c", k=4))
                    ins.then_inc(tr_dve, 1)

                if finish_x and ahead:
                    finish_x(0)
                for t in range(TT):
                    if finish_x and t + ahead < TT:
                        finish_x(t + ahead)
                    if t == 0:
                        dve.wait_ge(gain_loaded, 16 * (n + 1))
                    dve.wait_ge(norm_rstd, n * TT + t + 1)
                    ins = v.scalar_tensor_tensor(out=h_rows[:, t, :], in0=x_sb[:, t, :], scalar=st[:, 4 + t:5 + t],
                                                 in1=gain[:, :], op0=ALU.mult, op1=ALU.mult)
                    ins.then_inc(h_ready, 1)
                    if copies and t:
                        copy(t - 1)
                if copies:
                    copy(TT - 1)

            v.memset(rel_w[32:33, :], -BIG).then_inc(v_row_ready, 1)
            norm(0)

            def job(j):
                kind, i = j // 4, j % 4
                dst = (q_cat[:, HEADS + i, :], dkT[:, i, :], dv[:, i, :])[kind]
                dve.wait_ge(job_full, j + 1)
                if j == 5:
                    dve.wait_ge(v_stored, 16)
                v.tensor_copy(dst, ps[:, job_bank(j), :]).then_inc(job_dve, 1)

            splits(at_start(0))
            job(1)
            splits(at_last_job(0))
            job(3)
            dve.wait_ge(gates_hi, 1)
            v.tensor_tensor(w_gates_split[:, 1, :, :], w_gates[:, :, :], w_gates_split[:, 0, :, :].bitcast(F32),
                            ALU.subtract).then_inc(gates_split, 1)
            splits(at_start(1))
            for half in range(2):
                dve.wait_ge(vbias_full, half + 1)
                last = v.tensor_copy(v_row[0:HEADS, half * 320:half * 320 + 320], ps[0:HEADS, 4 + half, 0:320])
            last.then_inc(v_row_ready, 1)
            dve.wait_ge(small_loaded, 16 * SMALL)
            v.tensor_scalar(subln[:, :], subln[:, :], 1.0 - LAM_INIT, None, ALU.mult).then_inc(subln_ready, 1)
            for i in range(2):
                link(v.tensor_tensor(lams[:, 2 * i, :], lams[:, 2 * i, :], lams[:, 2 * i + 1, :], ALU.mult))
                v.tensor_reduce(st[:, 8 + i:9 + i], lams[:, 2 * i, :], AX, ALU.add).then_inc(lam_sum, 1)
            dve.wait_ge(lam_exp, 1)
            link(v.tensor_tensor(st[:, 12:13], st[:, 10:11], st[:, 11:12], ALU.subtract))
            link(v.tensor_scalar(st[:, 13:14], st[:, 12:13], LAM_INIT, None, ALU.add))
            lam = st[:, 13:14]

            dve.wait_ge(gates_full, 1)
            G = lambda k: gate_rows[0:HEADS, k, :]
            ig, f, soft_part, B, a_row, M, neg_mt, thr_row = (G(k) for k in range(8))
            v.tensor_scalar(ig, ps[0:HEADS, 0, :], gate_b[0:HEADS, 0:1], None, ALU.add)
            link(v.tensor_scalar(f, ps[32:32 + HEADS, 0, :], gate_b[32:32 + HEADS, 0:1], None, ALU.add))
            v.scalar_tensor_tensor(out=soft_part, in0=f, scalar=-1.0, in1=f,
                                   op0=ALU.mult, op1=ALU.max).then_inc(gate_rows_ready, 1)
            link(v.tensor_scalar(f, f, 0.0, None, ALU.min))
            dve.wait_ge(gate_act, 1)
            link(v.tensor_tensor(f, f, soft_part, ALU.subtract))
            link(v.memset(thr_row, 1.0))
            link(v.tensor_tensor_scan(B, thr_row, f, 0.0, ALU.mult, ALU.add))
            link(v.tensor_tensor(a_row, ig, B, ALU.subtract))
            link(v.tensor_tensor_scan(M, a_row, a_row, 0.0, ALU.max, ALU.max))
            link(v.tensor_scalar(neg_m_row[:, :], M, -1.0, None, ALU.mult))
            v.tensor_tensor(thr_row, neg_m_row[:, :], B, ALU.subtract).then_inc(gate_rows_ready, 1)

            for j in range(5, EARLY, 2):
                if j % 4 == 3:
                    splits(at_last_job(j // 4))
                job(j)
                if j % 4 == 3:
                    splits(at_start(j // 4 + 1))
            dve.wait_ge(gate_cols_full, 1)
            v.tensor_copy(st[:, 32:64], ps[:, 1, 0:32]).then_inc(gate_cols_ready, 1)
            a_col = st[:, 32:48].rearrange("p (j h) -> p j h", j=TT)
            thr_col = st[:, 48:64].rearrange("p (j h) -> p j h", j=TT)
            v.memset(mv[:, :, :, P:P + 1], 1.0)

            def biased(u):
                h, i = u // TT, u % TT
                n = (i + 1) * P
                if u >= 2:
                    dve.wait_ge(a_turned, u - 1)
                dve.wait_ge(bias_loaded[h % 2], 16 * (h // 2 + 1))
                dve.wait_ge(s_full, u + 1)
                src = ps[:, 2 * (u % 2):2 * (u % 2) + 2, 0:n]
                v.scalar_tensor_tensor(out=e_maps[:, u % 2, :, 0:n], in0=src, scalar=64.0 ** -0.5,
                                       in1=bc(bias_sb[:, h % 2, T - n:T], 1, P, 2, n),
                                       op0=ALU.mult, op1=ALU.add).then_inc(s_biased, 1)
                dve.wait_ge(s_biased, u + 1)
                c = 16 + 2 * (u % 2)
                v.tensor_reduce(st[:, c:c + 2], e_maps[:, u % 2, :, 0:n], AX, ALU.max, negate=True).then_inc(s_max, 1)

            def combined(u):
                n = (u % TT + 1) * P
                b = u % 2
                dve.wait_ge(e_ready, 2 * (u + 1))
                if u:
                    dve.wait_ge(a_ready, u)
                link(v.reciprocal(st[:, 24:26], st[:, 20 + 2 * b:22 + 2 * b]))
                link(v.tensor_tensor(st[:, 26:27], st[:, 25:26], lam, ALU.mult))
                link(v.tensor_scalar(e_maps[:, b, 1, 0:n], e_maps[:, b, 1, 0:n], st[:, 26:27], None, ALU.mult))
                v.scalar_tensor_tensor(out=a_map[:, b, 0:n], in0=e_maps[:, b, 0, 0:n], scalar=st[:, 24:25],
                                       in1=e_maps[:, b, 1, 0:n], op0=ALU.mult, op1=ALU.subtract).then_inc(a_ready, 1)

            def rows4(ap):
                return ap.rearrange("p (i c) -> p i c", i=TT)

            def weights_arg(h):
                dve.wait_ge(m_row_full, h + 1)
                if h >= 2:
                    dve.wait_ge(mo_full, h - 1)
                elif h == 0:
                    dve.wait_ge(a_turned, UNITS)
                else:
                    dve.wait_ge(o_unit, UNITS)
                for j in range(TT):
                    n = T - j * P
                    last = v.tensor_scalar(decay(h, j), ps[:, 3, j * P:T], a_col[:, j, h:h + 1], 0.0,
                                           ALU.add, ALU.min)
                last.then_inc(m_arg, 1)

            def weigh(h):
                dve.wait_ge(m_full, h + 1)
                dve.wait_ge(m_masked, h + 1)
                for j in range(TT):
                    n = T - j * P
                    w = decay(h, j)
                    last = v.tensor_tensor(w, qk_bank(j), w, ALU.mult)
                last.then_inc(m_weighted, 1)

            def head_out(h):
                dve.wait_ge(mo_full, h + 1)
                o4 = ps[:, 5:7, 0:2 * (P + 1)].rearrange("p b (i c) -> p b i c", i=2)
                den = st[:, 72:76].rearrange("p (b i) -> p b i", b=2)
                thr = thr_col[:, :, h].rearrange("p (b i) -> p b i", b=2)
                out4 = post[:, 0, :].rearrange("p (b i c) -> p b i c", b=2, i=2)
                link(v.scalar_tensor_tensor(out=den, in0=o4[:, :, :, P], scalar=-1.0, in1=thr, op0=ALU.mult, op1=ALU.max))
                link(v.tensor_tensor(den, o4[:, :, :, P], den, ALU.max))
                link(v.reciprocal(st[:, 72:76], st[:, 72:76]))
                link(v.tensor_tensor(out4, o4[:, :, :, 0:P], bc(den, 3, P, 2, 2, P), ALU.mult))
                link(v.tensor_reduce(st[:, 76:80], rows4(post[:, 0, :]), AX, ALU.add))
                link(v.tensor_scalar(st[:, 76:80], st[:, 76:80], 1.0 / P, None, ALU.mult))
                v.tensor_tensor(rows4(post[:, 0, :]), rows4(post[:, 0, :]), bc(st[:, 76:80], 2, P, TT, P),
                                ALU.subtract).then_inc(m_centred, 1)

            def head_norm_gate(h):
                dve.wait_ge(m_rstd, h + 1)
                v.tensor_tensor(rows4(post[:, 0, :]), rows4(post[:, 0, :]), bc(st[:, 84:88], 2, P, TT, P),
                                ALU.mult).then_inc(m_normed, 1)
                if h == HEADS - 1:
                    cat(KD - 1, 3)
                dve.wait_ge(job_act, jobs_before(LATE + h + 1, True))
                dve.wait_ge(m_turned, h + 1)
                v.scalar_tensor_tensor(out=q_cat[:, h, :], in0=ps[:, 4, :], scalar=head_norm[:, h:h + 1],
                                       in1=moT[:, h, :], op0=ALU.mult, op1=ALU.mult).then_inc(m_cat, 1)

            for step in range(UNITS + 4):
                if step < UNITS:
                    biased(step)
                if 1 <= step <= UNITS:
                    combined(step - 1)
                j = EARLY + step
                if j < LATE and j % 4 == 3:
                    splits(at_last_job(j // 4))
                if EARLY < j <= LATE and j % 4 == 0:
                    splits(at_start(j // 4))
                if step == UNITS + 1:
                    weights_arg(0)
                if step >= 5 and (step - 5) % TT == 0:
                    h = (step - 5) // TT
                    dve.wait_ge(o_square, h + 1)
                    v.tensor_reduce(st[:, 64:68], rows4(post[:, 0, :]), AX, ALU.add).then_inc(o_sums, 1)
                    dve.wait_ge(o_rstd, h + 1)
                    if h:
                        dve.wait_ge(on_turned, h)
                    v.tensor_tensor(rows4(post[:, 1, :]), rows4(ps[:, 5, :]), bc(st[:, 68:72], 2, P, TT, P),
                                    ALU.mult).then_inc(o_normed, 1)

            weights_arg(1)
            weigh(0)
            for h in range(HEADS):
                head_out(h)
                if h + 2 < HEADS:
                    weights_arg(h + 2)
                dve.wait_ge(m_square, h + 1)
                v.tensor_reduce(st[:, 80:84], rows4(post[:, 1, :]), AX, ALU.add).then_inc(m_sums, 1)
                if h + 1 < HEADS:
                    weigh(h + 1)
                if h + 1 == HEADS:
                    cat(HEADS + 2, 2)
                head_norm_gate(h)
                if h + 2 == HEADS:
                    splits(at_last_job(6))
                    for n in range(2):
                        cat(HEADS + n, n)
            for n in range(HEADS, KD):
                cat((HEADS + n) % KD, n)
            splits(at_start(7))

            def add_output(l, half, t):
                j, p = half * TT + t, (ODD_BASE + 6 if l else 7) + half
                if t == TT - 1:
                    splits(at_last_job(p))
                dve.wait_ge(out_full, 8 * l + j + 1)
                xt = x_sb[:, t, half * 512:half * 512 + 512]
                v.tensor_tensor(xt, ps[:, j, :], xt, ALU.add).then_inc(x_ready if half else out_added, 1)
                if t == TT - 1 and half == 0:
                    splits(at_start(p + 1))

            def mixer_norm(l):
                if l == 0:
                    dve.wait_ge(x_reloaded, 16)
                for t in range(TT):
                    add_output(l, 0, t)
                norm(2 * l + 1, lambda t: add_output(l, 1, t))
                splits(at_start(MOE_BASE[l]))

            def combine(l, t):
                dve.wait_ge(y_back_loaded[t], 32 * (l + 1))
                for k in range(2):
                    ins = v.scalar_tensor_tensor(out=x_sb[:, t, :], in0=y_back[:, t, k, :], scalar=top_w[:, t, k:k + 1],
                                                 in1=x_sb[:, t, :], op0=ALU.mult, op1=ALU.add)
                    if k == 0:
                        link(ins)
                ins.then_inc(x_ready, 1)

            def first_of(eq, n, dst):
                cand = wide if n == E else g_cand
                link(v.scalar_tensor_tensor(out=cand, in0=eq, scalar=-1000.0, in1=bc(iota16[:, 0:n], 1, P, TT, n),
                                            op0=ALU.mult, op1=ALU.add))
                link(v.tensor_reduce(low, cand, AX, ALU.min))
                link(v.tensor_tensor(dst, cand, bc(low, 2, P, TT, n), ALU.is_equal))

            def route(l):
                dve.wait_ge(consts_ready, 7)
                dve.wait_ge(logits_full, TT * (l + 1))
                link(v.tensor_tensor(lg, ps[:, 4, 0:TT * NR].rearrange("p (t n) -> p t n", t=TT),
                                     bc(b_route[:, l, :], 1, P, TT, NR), ALU.add))
                gl, el = lg[:, :, 0:GROUPS], lg[:, :, GROUPS:NR]
                link(v.tensor_reduce(top_v[:, 0, :], gl, AX, ALU.max))
                v.tensor_tensor(g_exp, gl, bc(top_v[:, 0, :], 2, P, TT, GROUPS), ALU.subtract).then_inc(route_arg, 1)
                link(v.tensor_tensor(g_cand, gl, bc(top_v[:, 0, :], 2, P, TT, GROUPS), ALU.is_equal))
                first_of(g_cand, GROUPS, g_pick)
                link(v.tensor_scalar(g_pen, g_pick, BIG, -BIG, ALU.mult, ALU.add))
                for t in range(TT):
                    s4 = e_score[:, t, :].rearrange("p (g j) -> p g j", g=GROUPS)
                    e4 = el[:, t, :].rearrange("p (g j) -> p g j", g=GROUPS)
                    link(v.tensor_tensor(s4, e4, bc(g_pick[:, t, :], 2, P, GROUPS, PER_GROUP), ALU.mult))
                    link(v.tensor_tensor(s4, s4, bc(g_pen[:, t, :], 2, P, GROUPS, PER_GROUP), ALU.add))
                for k in range(2):
                    link(v.tensor_reduce(top_v[:, k, :], e_score, AX, ALU.max))
                    link(v.tensor_tensor(wide, e_score, bc(top_v[:, k, :], 2, P, TT, E), ALU.is_equal))
                    first_of(wide, E, picks[:, k, :, :])
                    if k == 0:
                        link(v.scalar_tensor_tensor(out=e_score, in0=picks[:, 0, :, :], scalar=-2 * BIG, in1=e_score,
                                                    op0=ALU.mult, op1=ALU.add))
                v.tensor_tensor(prob[:, 0, :], top_v[:, 1, :], top_v[:, 0, :], ALU.subtract).then_inc(route_arg, 1)
                v.tensor_tensor(member, picks[:, 0, :, :], picks[:, 1, :, :], ALU.add).then_inc(picks_ready, 1)
                dve.wait_ge(route_exp, 2 * l + 1)
                link(v.tensor_reduce(prob[:, 1, :], g_exp, AX, ALU.add))
                dve.wait_ge(route_exp, 2 * l + 2)
                link(v.tensor_scalar(prob[:, 2, :], prob[:, 0, :], 1.0, None, ALU.add))
                link(v.tensor_tensor(prob[:, 1, :], prob[:, 1, :], prob[:, 2, :], ALU.mult))
                link(v.reciprocal(top_w[:, :, 0], prob[:, 1, :]))
                link(v.tensor_tensor(top_w[:, :, 1], top_w[:, :, 0], prob[:, 0, :], ALU.mult))
                dve.wait_ge(rank_full, l + 1)
                link(v.tensor_copy(rank_sb, ps[:, 5, 0:(TT + 1) * E]))
                rank = rank_sb[:, 0:TT * E].rearrange("p (t n) -> p t n", t=TT)
                link(v.tensor_tensor(place, rank, picks[:, 0, :, :], ALU.mult))
                link(v.tensor_tensor(wide, rank, picks[:, 1, :, :], ALU.mult))
                link(v.tensor_tensor(place, place, wide, ALU.add))
                link(v.tensor_tensor(wide, picks[:, 0, :, :], picks[:, 1, :, :], ALU.add))
                link(v.scalar_tensor_tensor(out=place, in0=wide, scalar=-1.0, in1=place, op0=ALU.add, op1=ALU.add))
                def slot_tokens(g):
                    dve.wait_ge(idx_full, 4 * l + g + 1)
                    v.tensor_copy(slot_tok[0:CAP, 4 * g:4 * g + 4], ps[0:CAP, IDX_BANK[g], 4 * g:4 * g + 4]).then_inc(idx_ready, 1)

                for g in range(4):
                    for t in range(TT):
                        ins = v.tensor_tensor(sel[:, t, 4 * g:4 * g + 4, 0:CAP], bc(place[:, t, 4 * g:4 * g + 4], 2, P, 4, CAP),
                                              bc(slot_iota[:, 0:CAP], 1, P, 4, CAP), ALU.is_equal)
                    ins.then_inc(sel_ready, 1)
                    if g:
                        slot_tokens(g - 1)
                slot_tokens(3)
            def result_rows(l):
                rank = rank_sb[:, 0:TT * E].rearrange("p (t n) -> p t n", t=TT)
                link(v.tensor_reduce(most, rank_sb[:, TT * E:(TT + 1) * E], AX, ALU.max))
                v.tensor_scalar(overflow_flag[:, l:l + 1], most, float(CAP), None, ALU.is_gt).then_inc(flag_ready, 1)
                link(v.tensor_tensor(result_row, rank, bc(iota_slot0[:, :], 1, P, TT, E), ALU.add))
                for j in range(1, OVER + 1):
                    link(v.tensor_scalar(wide, rank, float(j * CAP), float((E - 1) * CAP), ALU.is_ge, ALU.mult))
                    link(v.tensor_tensor(result_row, result_row, wide, ALU.add))
                for k in range(2):
                    link(v.tensor_tensor(wide, result_row, picks[:, k, :, :], ALU.mult))
                    link(v.tensor_reduce(row_f[:, :, k], wide, AX, ALU.add))
                link(v.tensor_copy(back_idx, rt[:, 592:600]))

            def copy_xgT(n, u):
                dve.wait_ge(xgT_act, n + 1)
                v.tensor_tensor(xgT[:, u, 1, :, 0:CAP],
                                ps[:, 5:7, :].rearrange("p b (k c) -> p (b k) c", k=4)[:, :, 0:CAP],
                                xgT[:, u, 0, :, 0:CAP].bitcast(F32), ALU.subtract).then_inc(xgT_dve, 1)

            def copy_actT(n, u):
                dve.wait_ge(actT_hi, n + 1)
                v.tensor_tensor(actT[:, u, 1, :, 0:CAP],
                                ps[:, 4, :].rearrange("p (k c) -> p k c", k=KF)[:, :, 0:CAP],
                                actT[:, u, 0, :, 0:CAP].bitcast(F32), ALU.subtract).then_inc(actT_ready, 1)

            def hidden(n, up_done):
                dve.wait_ge(silu_ready, n + 1)
                dve.wait_ge(chunk_done, up_done)
                v.tensor_tensor(act_h[0:CAP, :], sg[0:CAP, :], ps[0:CAP, 1, :], ALU.mult).then_inc(act_ready, 1)

            def copy_y(u, down_done, stored_before):
                dve.wait_ge(chunk_done, down_done)
                if stored_before is not None:
                    dve.wait_ge(y_stored[u], stored_before)
                v.tensor_copy(y_sb[0:CAP, u, 512:1024], ps[0:CAP, 3, :]).then_inc(y_dve, 1)

            def experts(l):
                n0 = E * l
                c0 = step_chunk(l, 0)
                copy_xgT(n0, 0)
                splits(c0 + 10)
                copy_xgT(n0 + 1, 1)
                result_rows(l)
                splits(c0 + 14)
                hidden(n0, c0 + 8)

                def step(e, n, u, c, i, y_stored_before, with_y=True):
                    if with_y:
                        copy_y(u, plus(c, i, 24), y_stored_before)
                    splits(c + 10, i)
                    copy_actT(n - 1, 1 - u)
                    splits(c + 14, i)
                    hidden(n, plus(c + 8, i, 24))
                    if not (isinstance(e, int) and e == E - 1):
                        copy_xgT(n + 1, 1 - u)
                    splits(c + 18, i)

                step(1, n0 + 1, 1, step_chunk(l, 1), None, None, with_y=False)
                for e in (2, 3, 4):
                    step(e, n0 + e, e % 2, step_chunk(l, e), None, 16 * ((n0 + e - 2) // 2) or None)
                c = step_chunk(l, 5)
                with dve.Fori(0, E // 2 - 3) as i:
                    for u in range(2):
                        step(i * 2 + (5 + u), i * 2 + (5 + u + n0), 1 - u, c + 12 * u, i,
                             i * 16 + 16 * ((n0 + 3 + u) // 2))
                split[0] += 24 * (E // 2 - 4)
                step(E - 1, n0 + E - 1, 1, step_chunk(l, E - 1), None, 16 * ((n0 + E - 3) // 2))
                c = step_chunk(l, E)
                copy_y(0, c, 16 * ((n0 + E - 2) // 2))
                copy_actT(n0 + E - 1, 1)
                copy_y(1, c + 4, 16 * ((n0 + E - 1) // 2))
                o = over[l]
                with dve.If(dve.value_load(overflow_flag[0:1, l:l + 1], min_val=0, max_val=1) > 0):
                    dve.wait_ge(y_stored[0], 8 * E * (l + 1))
                    with dve.Fori(0, E) as e:
                        with dve.Fori(0, OVER) as j:
                            it = e * OVER + j
                            v.tensor_scalar(over_place, place[:, :, bass.ds(e, 1)].rearrange("p t n -> p (t n)"),
                                            float(-CAP), None, ALU.add).then_inc(o["place"], 1)
                            dve.wait_ge(o["place"], it * 2 + 1)
                            for t in range(TT):
                                last = v.tensor_scalar(sel_over[:, t, 0:CAP], slot_iota[:, 0:CAP],
                                                       over_place[:, t:t + 1], None, ALU.is_equal)
                            last.then_inc(o["sel"], 1)
                            v.tensor_copy(place[:, :, bass.ds(e, 1)].rearrange("p t n -> p (t n)"),
                                          over_place).then_inc(o["place"], 1)
                            dve.wait_ge(o["place"], it * 2 + 2)
                            dve.wait_ge(o["idx_full"], it + 1)
                            v.tensor_copy(over_tok[0:CAP, :], ps[0:CAP, 0, 0:1]).then_inc(o["idx"], 1)
                            dve.wait_ge(o["turned"], it + 1)
                            v.tensor_copy(xgT_over[:, :, 0:CAP],
                                          ps[:, 1:3, :].rearrange("p b (k c) -> p (b k) c", k=4)[:, :, 0:CAP]).then_inc(o["xgT"], 1)
                            dve.wait_ge(o["silu"], it + 1)
                            dve.wait_ge(o["done"], it * 3 + 2)
                            v.tensor_tensor(act_h[0:CAP, :], sg[0:CAP, :], ps[0:CAP, 4, :], ALU.mult).then_inc(o["act"], 1)
                            dve.wait_ge(o["act_turned"], it + 1)
                            v.tensor_copy(actT_over[:, :, 0:CAP],
                                          ps[:, 5, :].rearrange("p (k c) -> p k c", k=KF)[:, :, 0:CAP]).then_inc(o["actT"], 1)
                            dve.wait_ge(o["done"], it * 3 + 3)
                            v.tensor_copy(y_sb[0:CAP, 0, :],
                                          ps[0:CAP, 6:8, :].rearrange("p b n -> p (b n)")).then_inc(o["y"], 1)
                            dve.wait_ge(o["stored"], it * 16 + 16)

            mixer_norm(0)
            route(0)
            experts(0)
            splits(PIECE * (ODD_BASE + 1))
            norm(2, lambda t: combine(0, t), ahead=1)
            splits(at_start(ODD_BASE))
            link(v.memset(z_sb[:, :, 0:2], 0.0))
            for half in range(2):
                p = ODD_BASE + 3 * half
                splits(at_last_job(p))
                splits(at_start(p + 1))
                for i in range(4):
                    j = half * 12 + 4 + i
                    if i == 3:
                        splits(at_last_job(p + 1))
                    dve.wait_ge(odd_cg, 4 * half + i + 1)
                    dve.wait_ge(odd_full, j + 1)
                    v.tensor_tensor(z_sb[:, i, 2:T + 2], ps[:, j % 8, :], cg_sb[:, i, :], ALU.mult).then_inc(odd_z, 1)
                    dve.wait_ge(odd_z, 4 * half + i + 1)
                    w, k = conv_sb[:, 4 * half + i, :], 4 * half + i
                    link(v.tensor_scalar(yT[:, k, :], z_sb[:, i, 0:T], w[:, 0:1], None, ALU.mult))
                    for tap in (1, 2):
                        link(v.scalar_tensor_tensor(out=yT[:, k, :], in0=z_sb[:, i, tap:tap + T], scalar=w[:, tap:tap + 1],
                                                    in1=yT[:, k, :], op0=ALU.mult, op1=ALU.add))
                splits(at_start(p + 2))
                for i in range(4):
                    j, k = half * 12 + 8 + i, 4 * half + i
                    if i == 3:
                        splits(at_last_job(p + 2))
                    dve.wait_ge(odd_full, j + 1)
                    v.tensor_tensor(yT[:, k, :], ps[:, j % 8, :], yT[:, k, :], ALU.mult).then_inc(odd_y, 1)
                if half == 0:
                    splits(at_start(p + 3))
            for k in range(KD):
                cat(k, k, 1)
            splits(at_start(ODD_BASE + 6))
            mixer_norm(1)
            route(1)
            experts(1)
            norm(4, lambda t: combine(1, t), ahead=1, copies=False)

        @block.tensor
        def _(pe):
            mm = nc.tensor.matmul

            def turn_h(n, t):
                pe.wait_ge(h_ready, n * TT + t + 1)
                if t >= 2:
                    pe.wait_ge(tr_act, n * TT + t - 1)
                    pe.wait_ge(tr_dve, n * TT + t - 1)
                for b in range(2):
                    for k in range(4):
                        c = 4 * b + k
                        last = nc.tensor.transpose(ps[:, 2 * (t % 2) + b, k * P:(k + 1) * P],
                                                   h_rows[:, t, c * P:(c + 1) * P], ident[:, :])
                    last.then_inc(tr_full, 1)

            def norm(n):
                for t in range(TT):
                    turn_h(n, t)

            def h_complete(n):
                pe.wait_ge(tr_act, (n + 1) * TT)
                pe.wait_ge(tr_dve, (n + 1) * TT)

            pe.wait_ge(consts_ready, 7)
            norm(0)
            h_complete(0)

            def mm3(out, a, b, start, stop):
                mm(out, a[0], b[0], start=start, stop=False)
                mm(out, a[1], b[0], start=False, stop=False)
                return mm(out, a[0], b[1], start=False, stop=stop)

            def w_rows(c, row, cs=slice(0, 512), width=512):
                return [part_of(c)[:, row * width + cs.start:row * width + cs.stop] for part_of in (hi_of, lo_of)]

            def project(p, i, out, operands, full, order=range(KD), before_k=None):
                for n, k in enumerate(order):
                    c = PIECE * p + k // 2
                    if i == 0:
                        pe.wait_ge(lo_ready, c + 1)
                    if before_k:
                        before_k(n)
                    a, b = operands(k, c)
                    last = mm3(out, a, b, n == 0, n == KD - 1)
                    if i == 3 and k % 2 == 1:
                        last.then_inc(chunk_done, 1)
                if i < 3:
                    last.then_inc(full, 1)
                else:
                    pe.wait_ge(chunk_done, PIECE * (p + 1))
                    pe.sem_inc(full, 1)

            def job(j):
                p, i = j // 4, j % 4
                if j == LATE:
                    pe.wait_ge(job_act, jobs_before(LATE, True))
                elif j > LATE:
                    pe.wait_ge(job_act, jobs_before(j, True))
                elif j >= 2:
                    on_act = act_job(j - 2)
                    pe.wait_ge(job_act if on_act else job_dve, jobs_before(j - 1, on_act))
                cs = slice(i * P, (i + 1) * P)

                def operands(k, c):
                    if p in (0, 1, 3, 4, 6):
                        return w_rows(c, k % 2, cs), (hT[:, 0, k, :], hT[:, 1, k, :])
                    return (hT[:, 0, k, cs], hT[:, 1, k, cs]), w_rows(c, k % 2)

                project(p, i, ps[:, job_bank(j), :], operands, job_full)

            def all_jobs(js):
                for j in js:
                    job(j)

            all_jobs(range(0, 4))
            pe.wait_ge(small_loaded, 16 * SMALL)
            pe.wait_ge(v_row_ready, 1)
            for half in range(2):
                mm(ps[0:HEADS, 4 + half, 0:320], rel_w[0:BUCKETS + 1, :],
                   table[0:BUCKETS + 1, half * 320:half * 320 + 320], start=True, stop=True).then_inc(vbias_full, 1)
            pe.wait_ge(gates_split, 1)
            for k in range(KD):
                last = mm3(ps[0:36, 0, :], (w_gates_split[:, 0, k, :], w_gates_split[:, 1, k, :]),
                           (hT[:, 0, k, :], hT[:, 1, k, :]), k == 0, k == KD - 1)
            last.then_inc(gates_full, 1)
            all_jobs(range(4, EARLY))
            pe.wait_ge(gate_act, 2)
            pe.wait_ge(gate_rows_ready, 2)
            for k, row in enumerate((4, 7)):
                for j in range(TT):
                    c = 16 * k + 4 * j
                    last = nc.tensor.transpose(ps[:, 1, c:c + HEADS], gate_rows[0:HEADS, row, j * P:(j + 1) * P],
                                               ident[0:HEADS, 0:HEADS])
            last.then_inc(gate_cols_full, 1)
            pe.wait_ge(gate_cols_ready, 1)
            pe.wait_ge(job_act, EARLY // 2)
            pe.wait_ge(job_dve, EARLY // 2)

            def scores(u):
                h, i = u // TT, u % TT
                n = (i + 1) * P
                if u >= 2:
                    pe.wait_ge(s_biased, u - 1)
                for m in range(2):
                    r = slice(64 * m, 64 * m + 64)
                    last = mm(ps[:, 2 * (u % 2) + m, 0:n], q_cat[r, HEADS + h, i * P:(i + 1) * P], dkT[r, h, 0:n],
                              start=True, stop=True)
                last.then_inc(s_full, 1)

            def turn_a(u):
                pe.wait_ge(a_ready, u + 1)
                if u:
                    pe.wait_ge(aT_ready, u)
                heads_turned = 0 if u < 7 else (u - 7) // TT + 1
                if u >= 7:
                    pe.wait_ge(cat_ready, heads_turned)
                for j in range(u % TT + 1):
                    last = nc.tensor.transpose(ps[:, 4, j * P:(j + 1) * P], a_map[:, u % 2, j * P:(j + 1) * P], ident[:, :])
                last.then_inc(a_turned, 1)

            def attend(u):
                h, i = u // TT, u % TT
                pe.wait_ge(aT_ready, u + 1)
                if i == 0 and h:
                    pe.wait_ge(o_normed, h)
                for j in range(i + 1):
                    last = mm(ps[:, 5, i * P:(i + 1) * P], aT[:, u % 2, j * P:(j + 1) * P], dv[:, j, h * P:(h + 1) * P],
                              start=(j == 0), stop=(j == i))
                last.then_inc(o_unit, 1)
                if i == TT - 1:
                    pe.wait_ge(o_unit, u + 1)
                    pe.sem_inc(o_full, 1)

            def turn_out(h):
                pe.wait_ge(o_normed, h + 1)
                pe.wait_ge(aT_ready, min(UNITS, 4 * h + 7))
                for i in range(TT):
                    last = nc.tensor.transpose(ps[:, 4, i * P:(i + 1) * P], post[:, 1, i * P:(i + 1) * P], ident[:, :])
                last.then_inc(on_turned, 1)

            def weights_row(h):
                if h:
                    pe.wait_ge(m_arg, h)
                else:
                    pe.wait_ge(s_biased, UNITS)
                mm(ps[:, 3, :], head_row[:, h, :], neg_m_row[:, :], start=True, stop=True).then_inc(m_row_full, 1)

            def queries_keys(h):
                for j in range(TT):
                    last = mm(qk_bank(j), mkT[:, h, j * P:(j + 1) * P], q_cat[:, h, j * P:T], start=True, stop=True)
                last.then_inc(m_full, 1)

            for step in range(UNITS + 4):
                if step < UNITS:
                    scores(step)
                    if EARLY + step < LATE:
                        all_jobs([EARLY + step])
                if 1 <= step <= UNITS:
                    turn_a(step - 1)
                if 2 <= step <= UNITS + 1:
                    attend(step - 2)
                if step == UNITS:
                    weights_row(0)
                    queries_keys(0)
                if step == UNITS + 2:
                    all_jobs([LATE])
                if step >= 7 and (step - 7) % TT == 0:
                    turn_out((step - 7) // TT)

            weights_row(1)
            pe.wait_ge(o_normed, HEADS)
            pe.wait_ge(cat_ready, HEADS)
            for h in range(HEADS):
                pe.wait_ge(m_weighted, h + 1)
                if h:
                    pe.wait_ge(m_centred, h)
                for i in range(TT):
                    for j in range(i + 1):
                        c = (i % 2) * (P + 1)
                        last = mm(ps[:, 5 + i // 2, c:c + P + 1],
                                  decay(h, j, (i - j) * P, (i - j + 1) * P),
                                  mv[:, j, h, :], start=(j == 0), stop=(j == i))
                last.then_inc(mo_full, 1)
                if h + 1 < HEADS:
                    queries_keys(h + 1)
                if h + 2 < HEADS:
                    weights_row(h + 2)
                if h + 1 < HEADS:
                    all_jobs([LATE + h + 1])
                pe.wait_ge(m_normed, h + 1)
                if h:
                    pe.wait_ge(m_cat, h)
                for i in range(TT):
                    last = nc.tensor.transpose(ps[:, 4, i * P:(i + 1) * P], post[:, 0, i * P:(i + 1) * P], ident[:, :])
                last.then_inc(m_turned, 1)

            def project_out(l, base):
                n = 2 * l + 1

                def tile(half, t):
                    first = half == 0 and t == 0
                    order = (4, 5, 6, 7, 0, 1, 2, 3) if first and l == 0 else range(KD)
                    rows = slice(t * P, (t + 1) * P)
                    project(base + half, t, ps[:, half * TT + t, :],
                            lambda k, c: ((hT[:, 0, k, rows], hT[:, 1, k, rows]), w_rows(c, k % 2)), out_full, order,
                            (lambda m: pe.wait_ge(cat_split, KD * l + m + 1)) if first else None)

                def logits(t):
                    pe.wait_ge(tr_act, n * TT + t + 1)
                    pe.wait_ge(tr_dve, n * TT + t + 1)
                    for k in range(KD):
                        last = mm(ps[:, 4, t * NR:(t + 1) * NR], hT_route[:, k, t * P:(t + 1) * P], w_route[:, l, k, :],
                                  start=(k == 0), stop=(k == KD - 1))
                    last.then_inc(logits_full, 1)

                for t in range(TT):
                    tile(0, t)
                tile(1, 0)
                tile(1, 1)
                turn_h(n, 0)
                tile(1, 2)
                turn_h(n, 1)
                logits(0)
                tile(1, 3)
                turn_h(n, 2)
                logits(1)
                turn_h(n, 3)
                logits(2)
                logits(3)

            def route(l):
                pe.wait_ge(picks_ready, l + 1)
                for t in range(TT):
                    for r in range(t + 1):
                        mm(ps[:, 5, t * E:(t + 1) * E], (later if r == t else ones16)[:, :], member[:, r, :],
                           start=(r == 0), stop=(r == t))
                for r in range(TT):
                    last = mm(ps[:, 5, TT * E:(TT + 1) * E], ones16[:, :], member[:, r, :], start=(r == 0), stop=(r == TT - 1))
                last.then_inc(rank_full, 1)
                for e in range(E):
                    if e % 4 == 0:
                        pe.wait_ge(sel_ready, 4 * l + e // 4 + 1)
                    for t in range(TT):
                        last = mm(ps[0:CAP, IDX_BANK[e // 4], e:e + 1], sel[:, t, e, 0:CAP], tok_id[:, t:t + 1],
                                  start=(t == 0), stop=(t == TT - 1))
                    if e % 4 == 3:
                        last.then_inc(idx_full, 1)

            def turn_xg(n, u, landed_value):
                pe.wait_ge(xg_landed[u], landed_value)
                for k in range(KD):
                    last = nc.tensor.transpose(ps[:, 5 + k // 4, (k % 4) * P:(k % 4) * P + CAP],
                                               xg[0:CAP, u, k * P:(k + 1) * P], ident[0:CAP, 0:CAP])
                last.then_inc(xg_turned, 1)

            def gate_or_up(bank, u, c, i):
                for k in range(KD):
                    if k % 2 == 0:
                        pe.wait_ge(lo_ready, plus(c + k // 2 + 1, i, 24))
                    last = mm3(ps[0:CAP, bank, :], (xgT[:, u, 0, k, 0:CAP], xgT[:, u, 1, k, 0:CAP]),
                               w_rows(c + k // 2, k % 2), k == 0, k == KD - 1)
                    if k % 2 == 1:
                        last.then_inc(chunk_done, 1)

            def gate(n, u, c, i):
                pe.wait_ge(xgT_dve, n + 1)
                gate_or_up(0, u, c, i)

            def turn_act(n):
                pe.wait_ge(act_ready, n + 1)
                for k in range(KF):
                    last = nc.tensor.transpose(ps[:, 4, k * P:k * P + CAP], act_h[0:CAP, k * P:(k + 1) * P],
                                               ident[0:CAP, 0:CAP])
                last.then_inc(act_turned, 1)

            def down(n, u, c, i, first=False):
                pe.wait_ge(actT_ready, n + 1)
                if not first:
                    pe.wait_ge(y_act, n)
                    pe.wait_ge(y_dve, n)
                for k in range(KF):
                    pe.wait_ge(lo_ready, plus(c + k + 1, i, 24))
                    for half in range(2):
                        last = mm3(ps[0:CAP, 2 + half, :], (actT[:, u, 0, k, 0:CAP], actT[:, u, 1, k, 0:CAP]),
                                   w_rows(c + k, half), k == 0, k == KF - 1)
                    last.then_inc(chunk_done, 1)

            def experts(l):
                n0, c0 = E * l, step_chunk(l, 0)
                turn_xg(n0, 0, 16 * (n0 // 2 + 1))
                gate(n0, 0, c0, None)
                turn_xg(n0 + 1, 1, 16 * (n0 // 2 + 1))
                gate_or_up(1, 0, c0 + 4, None)

                def step(n, u, c, i, landed_next, first=False, last=False):
                    gate(n, u, c, i)
                    turn_act(n - 1)
                    gate_or_up(1, u, c + 4, i)
                    if not last:
                        turn_xg(n + 1, 1 - u, landed_next)
                    down(n - 1, 1 - u, c + 8, i, first)

                for e in (1, 2):
                    n = n0 + e
                    step(n, e % 2, step_chunk(l, e), None, 16 * ((n + 1) // 2 + 1), first=(l == 0 and e == 1))
                with pe.Fori(0, E // 2 - 2) as i:
                    for u in range(2):
                        step(i * 2 + (3 + u + n0), 1 - u, step_chunk(l, 3) + 12 * u, i,
                             i * 16 + 16 * ((4 + u + n0) // 2 + 1))
                n = n0 + E - 1
                step(n, 1, step_chunk(l, E - 1), None, None, last=True)
                turn_act(n)
                down(n, 1, step_chunk(l, E), None)
                o = over[l]
                pe.wait_ge(flag_ready, l + 1)
                with pe.If(pe.value_load(overflow_flag[0:1, l:l + 1], min_val=0, max_val=1) > 0):
                    pe.wait_ge(y_act, n0 + E)
                    pe.wait_ge(y_dve, n0 + E)
                    with pe.Fori(0, E * OVER) as it:
                        w8 = w_over.rearrange("p (k n) -> p k n", k=KD)
                        w4 = w_over.rearrange("p (k n) -> p k n", k=KF)
                        pe.wait_ge(o["sel"], it + 1)
                        for t in range(TT):
                            last = mm(ps[0:CAP, 0, 0:1], sel_over[:, t, 0:CAP], tok_id[:, t:t + 1],
                                      start=(t == 0), stop=(t == TT - 1))
                        last.then_inc(o["idx_full"], 1)
                        pe.wait_ge(o["xg"], it * 16 + 16)
                        for k in range(KD):
                            last = nc.tensor.transpose(ps[:, 1 + k // 4, (k % 4) * P:(k % 4) * P + CAP],
                                                       xg[0:CAP, 0, k * P:(k + 1) * P], ident[0:CAP, 0:CAP])
                        last.then_inc(o["turned"], 1)
                        pe.wait_ge(o["xgT"], it + 1)
                        for m in range(2):
                            pe.wait_ge(o["w"], it * 48 + 16 * (m + 1))
                            for k in range(KD):
                                last = mm(ps[0:CAP, 3 + m, :], xgT_over[:, k, 0:CAP], w8[:, k, :],
                                          start=(k == 0), stop=(k == KD - 1))
                            last.then_inc(o["done"], 1)
                        pe.wait_ge(o["act"], it + 1)
                        for k in range(KF):
                            last = nc.tensor.transpose(ps[:, 5, k * P:k * P + CAP], act_h[0:CAP, k * P:(k + 1) * P],
                                                       ident[0:CAP, 0:CAP])
                        last.then_inc(o["act_turned"], 1)
                        pe.wait_ge(o["actT"], it + 1)
                        pe.wait_ge(o["w"], it * 48 + 48)
                        for half in range(2):
                            for k in range(KF):
                                last = mm(ps[0:CAP, 6 + half, :], actT_over[:, k, 0:CAP], w4[:, k, half * 512:half * 512 + 512],
                                          start=(k == 0), stop=(k == KF - 1))
                        last.then_inc(o["done"], 1)

            project_out(0, 7)
            route(0)
            experts(0)
            norm(2)
            h_complete(2)
            for j in range(24):
                if j >= 8:
                    kind, i = (j - 8) // 4 % 3, (j - 8) // 12 * 4 + (j - 8) % 4
                    pe.wait_ge((odd_cg, odd_z, odd_y)[kind], i + 1)
                cs = slice(j % 4 * P, (j % 4 + 1) * P)
                project(ODD_BASE + j // 4, j % 4, ps[:, j % 8, :],
                        lambda k, c: (w_rows(c, k % 2, cs), (hT[:, 0, k, :], hT[:, 1, k, :])), odd_full)
            pe.wait_ge(odd_y, 8)
            project_out(1, ODD_BASE + 6)
            route(1)
            experts(1)


_INS = ["x", "rel_bias", "norm_mix", "norm_ffn", "norm_final", "w_in_even", "w_out_even", "m_igate_b", "m_fgate_b",
        "m_head_norm", "lam_q1", "lam_k1", "lam_q2", "lam_k2", "da_subln", "w_in_odd", "conv_w", "w_out_odd",
        "router_group_w", "router_group_b", "router_expert_w", "router_expert_b",
        "exp_w_gate", "exp_w_up", "exp_w_down"]


def kernel(**inputs):
    import concourse.bacc as bacc
    from concourse.bass_utils import run_bass_kernel_spmd

    nc = bacc.Bacc("TRN2", target_bir_lowering=False, num_devices=1)
    arrays, args = {}, {}
    named = [(name, np.ascontiguousarray(inputs[name])) for name in _INS] + [("bucket_table", bucket_table())]
    for name, a in named:
        arrays[f"in_{name}"] = a
        args[name] = nc.dram_tensor(f"in_{name}", a.shape, mybir.dt.from_np(a.dtype), kind="ExternalInput").ap()
    out = nc.dram_tensor("out", (1, T, D), F32, kind="ExternalOutput").ap()
    hybrid_trunk(nc, args, out)
    return run_bass_kernel_spmd(nc, [arrays], core_ids=[0]).results[0]["out"]
```
